# Optimizing a Trainium2 kernel written in Bass

```python
import math
import jax
import jax.numpy as jnp
from jax import lax
import numpy as np

D_MODEL = 1024
BATCH = 1
SEQ = 512
DEPTH = 2
DEC_BATCH = 8
DEC_SEQ = 4
PAST_LEN = 512
PAGE_SIZE = 128

NSA_HEADS = 16
NSA_KV_HEADS = 4
NSA_GROUP = NSA_HEADS // NSA_KV_HEADS
HEAD_DIM = D_MODEL // NSA_HEADS
NSA_KV_WIDTH = NSA_KV_HEADS * HEAD_DIM
CMP_STRIDE = 16
CMP_BLOCK = 2 * CMP_STRIDE
SEL_BLOCK = 64
TOP_N = 16
WINDOW = 512
Q_BLOCK = 128
ROPE_THETA = 10000.0
NSA_PROJ = NSA_HEADS * HEAD_DIM + 6 * NSA_KV_WIDTH + 3 * NSA_HEADS
GLA_HEADS = 4
GLA_DK = D_MODEL // 2 // GLA_HEADS
GLA_DV = D_MODEL // GLA_HEADS
GLA_GATE_RANK = 16
GLA_GATE_TEMP = 16.0
GLA_CHUNK = 64
GLA_PROJ = 2 * GLA_HEADS * GLA_DK + 2 * GLA_HEADS * GLA_DV + GLA_GATE_RANK
FFN_DIM = 2816
CONV_WIDTH = 3
N_NSA_LAYERS = (DEPTH + 1) // 2
N_GLA_LAYERS = DEPTH // 2
NORM_EPS = 1e-6
NEG_BIG = -1e30
FORCE = 1e6

kernel_name = "nsa_gla_convffn_hybrid_step"

def _rmsnorm(x, g):
    xf = x.astype(jnp.float32)
    y = xf * lax.rsqrt(jnp.mean(xf * xf, -1, keepdims=True) + NORM_EPS)
    return (y * g.astype(jnp.float32)).astype(x.dtype)

def _rope(x, pos):
    half = x.shape[-1] // 2
    inv = ROPE_THETA ** (-jnp.arange(half, dtype=jnp.float32) / half)
    ang = pos.astype(jnp.float32)[:, None] * inv[None, :]
    cos = jnp.cos(ang)[None, :, None, :]
    sin = jnp.sin(ang)[None, :, None, :]
    xf = x.astype(jnp.float32)
    x1, x2 = xf[..., :half], xf[..., half:]
    return jnp.concatenate([x1 * cos - x2 * sin, x2 * cos + x1 * sin], -1).astype(x.dtype)

def _masked_softmax(s, mask):
    s = jnp.where(mask, s, NEG_BIG)
    m = jnp.max(s, -1, keepdims=True)
    e = jnp.where(mask, jnp.exp(s - m), 0.0)
    return e / jnp.maximum(jnp.sum(e, -1, keepdims=True), 1e-30)

def _attend(q, k, v, mask):
    s = jnp.einsum('...tgrd,...sgd->...tgrs', q, k).astype(jnp.float32) * HEAD_DIM ** -0.5
    p = _masked_softmax(s, mask[..., :, None, None, :])
    return jnp.einsum('...tgrs,...sgd->...tgrd', p.astype(v.dtype), v)

def _compress(x, pe, w, n_blk):
    b = x.shape[0]
    c = x[:, :(n_blk + 1) * CMP_STRIDE].reshape(b, n_blk + 1, CMP_STRIDE, x.shape[2], x.shape[3])
    first = jnp.einsum('bcjgd,jde->bcge', c + pe[:CMP_STRIDE, None, :], w[:CMP_STRIDE])
    second = jnp.einsum('bcjgd,jde->bcge', c + pe[CMP_STRIDE:, None, :], w[CMP_STRIDE:])
    return first[:, :n_blk] + second[:, 1:]

def _cmp_branch(q, k_full, v_full, q_pos, pe, w):
    n_blk = k_full.shape[1] // CMP_STRIDE - 1
    kc = _compress(k_full, pe[0], w[0], n_blk)
    vc = _compress(v_full, pe[1], w[1], n_blk)
    s = jnp.einsum('btgrd,bngd->btgrn', q, kc).astype(jnp.float32) * HEAD_DIM ** -0.5
    blk_end = jnp.arange(n_blk) * CMP_STRIDE + CMP_BLOCK - 1
    mask = blk_end[None, :] <= q_pos[:, None]
    p = _masked_softmax(s, mask[:, None, None, :])
    o = jnp.einsum('btgrn,bngd->btgrd', p.astype(vc.dtype), vc)
    return o, p

def _select_blocks(p_cmp, q_pos, n_sel):
    n_blk = p_cmp.shape[-1]
    ps = jnp.sum(p_cmp, axis=3)
    i = jnp.arange(n_blk)[:, None]
    j = jnp.arange(n_sel)[None, :]
    overlap = ((i * CMP_STRIDE + CMP_BLOCK > j * SEL_BLOCK)
               & (i * CMP_STRIDE < (j + 1) * SEL_BLOCK)).astype(jnp.float32)
    sc = jnp.einsum('btgn,nj->btgj', ps, overlap)
    jj = jnp.arange(n_sel)[None, :]
    forced = (jj == (q_pos // SEL_BLOCK)[:, None]) | (jj == 0)
    future = jj * SEL_BLOCK > q_pos[:, None]
    sc = jnp.where(forced[:, None, :], FORCE, jnp.where(future[:, None, :], -FORCE, sc))
    vals, idx = lax.top_k(sc, min(TOP_N, n_sel))
    return idx, vals > -0.5 * FORCE

def _slc_seq(q, k, v, idx, valid, q_pos):
    n_kv = k.shape[1]
    kb = k.reshape(-1, SEL_BLOCK, n_kv, HEAD_DIM).transpose(2, 0, 1, 3)
    vb = v.reshape(-1, SEL_BLOCK, n_kv, HEAD_DIM).transpose(2, 0, 1, 3)
    g_ix = jnp.arange(n_kv)[None, :, None]

    def one_block(args):
        qb, ib, okb, pb = args
        ks = kb[g_ix, ib]
        vs = vb[g_ix, ib]
        kpos = ib[..., None] * SEL_BLOCK + jnp.arange(SEL_BLOCK)
        mask = okb[..., None] & (kpos <= pb[:, None, None, None])
        s = jnp.einsum('tgrd,tgnsd->tgrns', qb, ks).astype(jnp.float32) * HEAD_DIM ** -0.5
        t_, g_, r_, n_, sb_ = s.shape
        p = _masked_softmax(s.reshape(t_, g_, r_, n_ * sb_), mask.reshape(t_, g_, 1, n_ * sb_))
        return jnp.einsum('tgrm,tgmd->tgrd', p.astype(vs.dtype), vs.reshape(t_, g_, n_ * sb_, HEAD_DIM))

    t = q.shape[0]
    if t > Q_BLOCK and t % Q_BLOCK == 0:
        nb = t // Q_BLOCK
        split = lambda a: a.reshape(nb, Q_BLOCK, *a.shape[1:])
        o = lax.map(one_block, (split(q), split(idx), split(valid), split(q_pos)))
        return o.reshape(t, *o.shape[2:])
    return one_block((q, idx, valid, q_pos))

def _slc_branch(q, k_full, v_full, idx, valid, q_pos, n_sel):
    pad = n_sel * SEL_BLOCK - k_full.shape[1]
    kp = jnp.pad(k_full, ((0, 0), (0, pad), (0, 0), (0, 0)))
    vp = jnp.pad(v_full, ((0, 0), (0, pad), (0, 0), (0, 0)))
    return lax.map(lambda a: _slc_seq(a[0], a[1], a[2], a[3], a[4], q_pos), (q, kp, vp, idx, valid))

def _win_prompt(q, k, v):
    b, t, g, r, dh = q.shape
    nq = t // Q_BLOCK
    nw = WINDOW // Q_BLOCK
    kp = jnp.pad(k, ((0, 0), (WINDOW, 0), (0, 0), (0, 0))).reshape(b, nq + nw, Q_BLOCK, g, dh)
    vp = jnp.pad(v, ((0, 0), (WINDOW, 0), (0, 0), (0, 0))).reshape(b, nq + nw, Q_BLOCK, g, dh)
    bidx = jnp.arange(nq)[:, None] + jnp.arange(nw + 1)[None, :]
    span = (nw + 1) * Q_BLOCK
    kb = kp[:, bidx].reshape(b, nq, span, g, dh)
    vb = vp[:, bidx].reshape(b, nq, span, g, dh)
    qb = q.reshape(b, nq, Q_BLOCK, g, r, dh)
    a = jnp.arange(Q_BLOCK)[:, None]
    c = jnp.arange(span)[None, :]
    diff = a + WINDOW - c
    kpos = jnp.arange(nq)[:, None, None] * Q_BLOCK - WINDOW + c[None]
    mask = (diff >= 0)[None] & (diff <= WINDOW)[None] & (kpos >= 0)
    o = lax.map(lambda z: _attend(z[0], z[1], z[2], z[3]),
                (jnp.moveaxis(qb, 1, 0), jnp.moveaxis(kb, 1, 0), jnp.moveaxis(vb, 1, 0), mask))
    return jnp.moveaxis(o, 0, 1).reshape(b, t, g, r, dh)

def _win_sample(q, k_new, v_new, buf, pos):
    wb = buf.shape[1]
    k_all = jnp.concatenate([buf[:, :, 0], k_new], 1)
    v_all = jnp.concatenate([buf[:, :, 1], v_new], 1)
    k_pos = pos[0] - wb + jnp.arange(k_all.shape[1])
    diff = pos[:, None] - k_pos[None, :]
    mask = (diff >= 0) & (diff <= WINDOW)
    o = _attend(q, k_all, v_all, mask)
    return o, jnp.stack([k_all[:, -wb:], v_all[:, -wb:]], 2)

def _nsa_mixer(h, pos, w_in, cmp_pe, cmp_w, w_o, past, win_buf):
    b, t, _ = h.shape
    g, r, dh = NSA_KV_HEADS, NSA_GROUP, HEAD_DIM
    qd = NSA_HEADS * dh
    proj = h @ w_in
    q = _rope(proj[..., :qd].reshape(b, t, NSA_HEADS, dh), pos).reshape(b, t, g, r, dh)
    kvs = proj[..., qd:qd + 6 * NSA_KV_WIDTH].reshape(b, t, 6, g, dh)
    gates = jax.nn.sigmoid(proj[..., qd + 6 * NSA_KV_WIDTH:].astype(jnp.float32)).reshape(b, t, g, r, 3)
    k_c = _rope(kvs[:, :, 0], pos)
    v_c = kvs[:, :, 1]
    k_s = _rope(kvs[:, :, 2], pos)
    v_s = kvs[:, :, 3]
    k_w = _rope(kvs[:, :, 4], pos)
    v_w = kvs[:, :, 5]
    new_rows = jnp.stack([k_c, v_c, k_s, v_s], 2)
    full = new_rows if past is None else jnp.concatenate([past, new_rows], 1)
    o_c, p_c = _cmp_branch(q, full[:, :, 0], full[:, :, 1], pos, cmp_pe, cmp_w)
    n_sel = -(-full.shape[1] // SEL_BLOCK)
    idx, valid = _select_blocks(p_c, pos, n_sel)
    o_s = _slc_branch(q, full[:, :, 2], full[:, :, 3], idx, valid, pos, n_sel)
    if win_buf is None:
        o_w = _win_prompt(q, k_w, v_w)
        nb = min(WINDOW, t)
        new_win = jnp.stack([k_w[:, t - nb:], v_w[:, t - nb:]], 2)
    else:
        o_w, new_win = _win_sample(q, k_w, v_w, win_buf, pos)
    o = gates[..., 0:1] * o_c + gates[..., 1:2] * o_s + gates[..., 2:3] * o_w
    out = o.astype(h.dtype).reshape(b, t, qd) @ w_o
    return out, new_rows, new_win

def _gla_recurrence(q, k, v, log_a, s0):
    b, h, t, dk = q.shape
    dv = v.shape[-1]
    c = min(GLA_CHUNK, t)
    pad = (-t) % c
    if pad:
        padf = lambda a: jnp.pad(a, ((0, 0), (0, 0), (0, pad), (0, 0)))
        q, k, v, log_a = padf(q), padf(k), padf(v), padf(log_a)
    nc = (t + pad) // c
    to_chunks = lambda a: a.reshape(b, h, nc, c, a.shape[-1]).transpose(2, 0, 1, 3, 4)
    causal = jnp.tril(jnp.ones((c, c), bool))

    def step(s, xs):
        qc, kc, vc, ac = xs
        cum = jnp.cumsum(ac, axis=2)
        inter = jnp.einsum('bhtd,bhde->bhte', qc * jnp.exp(cum), s)
        diff = cum[:, :, :, None, :] - cum[:, :, None, :, :]
        dec = jnp.exp(jnp.where(causal[:, :, None], diff, -jnp.inf))
        att = jnp.einsum('bhtd,bhsd,bhtsd->bhts', qc, kc, dec)
        out = inter + jnp.einsum('bhts,bhse->bhte', att, vc)
        last = cum[:, :, -1]
        s = jnp.exp(last)[..., None] * s + jnp.einsum('bhsd,bhse->bhde', kc * jnp.exp(last[:, :, None, :] - cum), vc)
        return s, out

    s, o = lax.scan(step, s0, (to_chunks(q), to_chunks(k), to_chunks(v), to_chunks(log_a)))
    o = o.transpose(1, 2, 0, 3, 4).reshape(b, h, nc * c, dv)[:, :, :t]
    return o, s

def _gla_mixer(h, w_in, w_gate_up, b_gate, norm_g, w_o, s0):
    b, t, _ = h.shape
    nh, dk, dv = GLA_HEADS, GLA_DK, GLA_DV
    nk, nv = nh * dk, nh * dv
    proj = h @ w_in
    heads = lambda a, d: a.reshape(b, t, nh, d).transpose(0, 2, 1, 3).astype(jnp.float32)
    q = heads(proj[..., :nk], dk) * dk ** -0.5
    k = heads(proj[..., nk:2 * nk], dk)
    v = heads(proj[..., 2 * nk:2 * nk + nv], dv)
    r = proj[..., 2 * nk + nv:2 * nk + 2 * nv]
    gz = proj[..., 2 * nk + 2 * nv:] @ w_gate_up + b_gate
    log_a = heads(jax.nn.log_sigmoid(gz.astype(jnp.float32)) / GLA_GATE_TEMP, dk)
    if s0 is None:
        s0 = jnp.zeros((b, nh, dk, dv), jnp.float32)
    o, s = _gla_recurrence(q, k, v, log_a, s0.astype(jnp.float32))
    o = _rmsnorm(o.transpose(0, 2, 1, 3), norm_g) * jax.nn.silu(r.astype(jnp.float32)).reshape(b, t, nh, dv)
    out = o.reshape(b, t, nv).astype(h.dtype) @ w_o
    return out, s.astype(h.dtype)

def _conv_ffn(h, w_up, conv_w, conv_b, w_down, buf):
    b, t, _ = h.shape
    u = h @ w_up
    gate, val = u[..., :FFN_DIM], u[..., FFN_DIM:]
    if buf is None:
        buf = jnp.zeros((b, CONV_WIDTH - 1, FFN_DIM), gate.dtype)
    gc = jnp.concatenate([buf.astype(gate.dtype), gate], 1)
    conv = conv_b
    for j in range(CONV_WIDTH):
        conv = conv + conv_w[j] * gc[:, j:j + t]
    out = (jax.nn.gelu(conv) * val) @ w_down
    return out, gc[:, -(CONV_WIDTH - 1):]

def _trunk(x, pos, cache_nsa_kv, page_table, state_win_kv, state_gla, state_ffn_conv,
           norm_gain, nsa_w_in, nsa_cmp_pe, nsa_cmp_w, nsa_w_o,
           gla_w_in, gla_w_gate_up, gla_b_gate, gla_norm_gain, gla_w_o,
           ffn_w_up, ffn_conv_w, ffn_conv_b, ffn_w_down):
    sample = cache_nsa_kv is not None
    nsa_rows, win_bufs, gla_states, ffn_bufs = [], [], [], []
    for i in range(DEPTH):
        g = norm_gain[i]
        h = _rmsnorm(x, g[0])
        if i % 2 == 0:
            a = i // 2
            past, wbuf = None, None
            if sample:
                pages = cache_nsa_kv[a][page_table]
                past = pages.reshape(pages.shape[0], -1, *pages.shape[3:])
                wbuf = state_win_kv[a]
            out, rows, wb = _nsa_mixer(h, pos, nsa_w_in[a], nsa_cmp_pe[a], nsa_cmp_w[a], nsa_w_o[a], past, wbuf)
            nsa_rows.append(rows)
            win_bufs.append(wb)
        else:
            a = i // 2
            s0 = state_gla[a] if sample else None
            out, s = _gla_mixer(h, gla_w_in[a], gla_w_gate_up[a], gla_b_gate[a], gla_norm_gain[a], gla_w_o[a], s0)
            gla_states.append(s)
        x = x + _rmsnorm(out, g[1])
        h = _rmsnorm(x, g[2])
        out, fb = _conv_ffn(h, ffn_w_up[i], ffn_conv_w[i], ffn_conv_b[i], ffn_w_down[i],
                            state_ffn_conv[i] if sample else None)
        ffn_bufs.append(fb)
        x = x + _rmsnorm(out, g[3])
    return x, jnp.stack(nsa_rows), jnp.stack(win_bufs), jnp.stack(gla_states), jnp.stack(ffn_bufs)

def setup_inputs(seed: int = 0) -> dict:
    key = jax.random.key(seed)
    ks = jax.random.split(key, 24)
    f32 = jnp.float32
    nrm = lambda k, shape, scale: jax.random.normal(k, shape, f32) * scale
    n_pages = PAST_LEN // PAGE_SIZE
    n_phys = (5 * DEC_BATCH * n_pages + 3) // 4
    win_len = min(WINDOW, PAST_LEN)
    page_table = jax.random.permutation(ks[6], n_phys)[:DEC_BATCH * n_pages].reshape(DEC_BATCH, n_pages).astype(jnp.int32)
    return {
        'x_prompt': nrm(ks[0], (BATCH, SEQ, D_MODEL), 1.0),
        'x_sample': nrm(ks[1], (DEC_BATCH, DEC_SEQ, D_MODEL), 1.0),
        'cache_nsa_kv': nrm(ks[2], (N_NSA_LAYERS, n_phys, PAGE_SIZE, 4, NSA_KV_HEADS, HEAD_DIM), 1.0),
        'state_win_kv': nrm(ks[3], (N_NSA_LAYERS, DEC_BATCH, win_len, 2, NSA_KV_HEADS, HEAD_DIM), 1.0),
        'state_gla': nrm(ks[4], (N_GLA_LAYERS, DEC_BATCH, GLA_HEADS, GLA_DK, GLA_DV), 1.0),
        'state_ffn_conv': nrm(ks[5], (DEPTH, DEC_BATCH, CONV_WIDTH - 1, FFN_DIM), 1.0),
        'page_table': page_table,
        'norm_gain': 1.0 + nrm(ks[7], (DEPTH, 4, D_MODEL), 0.02),
        'nsa_w_in': nrm(ks[8], (N_NSA_LAYERS, D_MODEL, NSA_PROJ), D_MODEL ** -0.5),
        'nsa_cmp_pe': nrm(ks[9], (N_NSA_LAYERS, 2, CMP_BLOCK, HEAD_DIM), 0.5),
        'nsa_cmp_w': nrm(ks[10], (N_NSA_LAYERS, 2, CMP_BLOCK, HEAD_DIM, HEAD_DIM), (CMP_BLOCK * HEAD_DIM) ** -0.5),
        'nsa_w_o': nrm(ks[11], (N_NSA_LAYERS, NSA_HEADS * HEAD_DIM, D_MODEL), (NSA_HEADS * HEAD_DIM) ** -0.5),
        'gla_w_in': nrm(ks[12], (N_GLA_LAYERS, D_MODEL, GLA_PROJ), D_MODEL ** -0.5),
        'gla_w_gate_up': nrm(ks[13], (N_GLA_LAYERS, GLA_GATE_RANK, GLA_HEADS * GLA_DK), GLA_GATE_RANK ** -0.5),
        'gla_b_gate': nrm(ks[14], (N_GLA_LAYERS, GLA_HEADS * GLA_DK), 0.1),
        'gla_norm_gain': 1.0 + nrm(ks[15], (N_GLA_LAYERS, GLA_DV), 0.02),
        'gla_w_o': nrm(ks[16], (N_GLA_LAYERS, GLA_HEADS * GLA_DV, D_MODEL), (GLA_HEADS * GLA_DV) ** -0.5),
        'ffn_w_up': nrm(ks[17], (DEPTH, D_MODEL, 2 * FFN_DIM), D_MODEL ** -0.5),
        'ffn_conv_w': nrm(ks[18], (DEPTH, CONV_WIDTH, FFN_DIM), CONV_WIDTH ** -0.5),
        'ffn_conv_b': nrm(ks[19], (DEPTH, FFN_DIM), 0.02),
        'ffn_w_down': nrm(ks[20], (DEPTH, FFN_DIM, D_MODEL), FFN_DIM ** -0.5),
    }

def reference(x_prompt, x_sample, cache_nsa_kv, state_win_kv, state_gla, state_ffn_conv, page_table,
              norm_gain, nsa_w_in, nsa_cmp_pe, nsa_cmp_w, nsa_w_o,
              gla_w_in, gla_w_gate_up, gla_b_gate, gla_norm_gain, gla_w_o,
              ffn_w_up, ffn_conv_w, ffn_conv_b, ffn_w_down):
    pos_p = jnp.arange(x_prompt.shape[1], dtype=jnp.int32)
    past_len = page_table.shape[1] * cache_nsa_kv.shape[2]
    pos_s = past_len + jnp.arange(x_sample.shape[1], dtype=jnp.int32)
    y_prompt, nsa_p, win_p, gla_p, ffn_p = _trunk(
        x_prompt, pos_p, None, None, None, None, None,
        norm_gain, nsa_w_in, nsa_cmp_pe, nsa_cmp_w, nsa_w_o,
        gla_w_in, gla_w_gate_up, gla_b_gate, gla_norm_gain, gla_w_o,
        ffn_w_up, ffn_conv_w, ffn_conv_b, ffn_w_down)
    y_sample, nsa_s, win_s, gla_s, ffn_s = _trunk(
        x_sample, pos_s, cache_nsa_kv, page_table, state_win_kv, state_gla, state_ffn_conv,
        norm_gain, nsa_w_in, nsa_cmp_pe, nsa_cmp_w, nsa_w_o,
        gla_w_in, gla_w_gate_up, gla_b_gate, gla_norm_gain, gla_w_o,
        ffn_w_up, ffn_conv_w, ffn_conv_b, ffn_w_down)
    return (y_prompt, y_sample, nsa_p, nsa_s, win_p, win_s, gla_p, gla_s, ffn_p, ffn_s)


_drawn_inputs = setup_inputs


def setup_inputs(seed=0):
    import zlib

    import numpy as np

    out = dict(_drawn_inputs(seed))
    spreads = {}
    factors = {'gla_norm_gain': 5.799, 'ffn_conv_b': 2.804}
    for name, (base, spread) in spreads.items():
        noise = np.random.default_rng([zlib.crc32(name.encode()), seed]).standard_normal(out[name].shape)
        drawn = base * np.exp(spread * noise) if base else spread * noise
        out[name] = jnp.asarray(drawn.astype(out[name].dtype))
    for name, factor in factors.items():
        out[name] = (out[name] * factor).astype(out[name].dtype)
    return out
```

```python
from contextlib import ExitStack, contextmanager

import numpy as np

import concourse.bass as bass
from concourse import mybir

F32 = mybir.dt.float32
F16 = mybir.dt.float16
BF16 = mybir.dt.bfloat16
I32 = mybir.dt.int32
ALU = mybir.AluOpType
ACT = mybir.ActivationFunctionType
AX = mybir.AxisListType

P = 128
D = 1024
KD = D // P
SEQ = 512
DB, DS = 8, 4
SAMP = DB * DS
T = SEQ + SAMP
HALF = T // 2
NT = 5
PAST = 512
PAGE = 128
NPAGE = PAST // PAGE
HEADS, KVH, GRP, DH = 16, 4, 4, 64
KVW = KVH * DH
NBLK = PAST // 16 - 1
PROJ = HEADS * DH + 6 * KVW + 3 * HEADS
QKV = HEADS * DH + 6 * KVW
GH, DK, DV = 4, 128, 256
GPROJ = 2 * GH * DK + 2 * GH * DV + 16
F = 2816
KF = F // P
SCALE = DH ** -0.5
NEG = -1e30
EPS = 1e-6
STAGE_SEMS = 180
SLOTS = 4
SLOTW = 11 * P

C_ID = 0
C_TRIN = C_ID + P
C_TRI1 = C_TRIN + P
C_CMPP = C_TRI1 + P
C_NEW = C_CMPP + 4 * 32
C_WIN = C_NEW + DB * 32
C_CMPS = C_WIN + 4
C_COS = C_CMPS + P
C_SIN = C_COS + NT * 64
C_SEG = C_SIN + NT * 64
C_ATT = C_SEG + T
C_ROW = C_ATT + SAMP
C_SEL = C_ROW + DB
C_COLM = C_SEL + DS * 64
NCONST = C_COLM + DB * SAMP


def constants():
    c = np.zeros((P, NCONST), np.float32)
    r = np.arange(P)
    c[:, C_ID:C_ID + P] = np.eye(P)
    c[:, C_TRIN:C_TRIN + P] = np.where(r[None] <= r[:, None], 0, NEG)
    c[:, C_TRI1:C_TRI1 + P] = r[:, None] <= r[None]
    n = np.arange(32)
    for i in range(4):
        t = i * P + r
        c[:, C_CMPP + i * 32:C_CMPP + i * 32 + 32] = np.where(
            (16 * n[None] + 31 <= t[:, None]) & (n[None] < NBLK), 0, NEG)
    tok, branch, grp = r % DS, r // 64, (r // 16) % KVH
    for b in range(DB):
        c[:, C_NEW + b * 32:C_NEW + b * 32 + 32] = np.where(
            (n[None] // DS == b) & (n[None] % DS <= tok[:, None]), 0, NEG)
    c[:, C_WIN:C_WIN + 4] = np.where((branch[:, None] == 1) & (np.arange(4)[None] < tok[:, None]), NEG, 0)
    c[:, C_CMPS:C_CMPS + P] = np.where((r[None] // 32 == grp[:, None]) & (r[None] % 32 < NBLK), 0, NEG)
    inv = (10000.0 ** (-np.arange(32, dtype=np.float32) / 32).astype(np.float64)).astype(np.float32)
    for i in range(NT):
        pos = (i * P + r if i < 4 else PAST + r % DS).astype(np.float32)
        ang = (pos[:, None] * inv[None]).astype(np.float32)
        co, si = np.cos(ang.astype(np.float64)), np.sin(ang.astype(np.float64))
        c[:, C_COS + i * 64:C_COS + i * 64 + 64] = np.concatenate([co, co], 1)
        c[:, C_SIN + i * 64:C_SIN + i * 64 + 64] = np.concatenate([-si, si], 1)
    seg = np.ones(T)
    seg[0:SEQ:P] = 0
    seg[SEQ::DS] = 0
    c[:, C_SEG:C_SEG + T] = seg
    s = np.arange(SAMP)
    c[:SAMP, C_ATT:C_ATT + SAMP] = (s[:, None] // DS == s[None] // DS) & (s[:, None] <= s[None])
    c[:, C_ROW:C_ROW + DB] = (r[:, None] // DS) == np.arange(DB)[None]
    c[:, C_COLM:] = (s[None] // DS == np.arange(DB)[:, None]).reshape(1, -1)
    row = np.arange(64)
    for t in range(DS):
        c[:HEADS, C_SEL + t * 64:C_SEL + t * 64 + 64] = (r[:HEADS, None] == row[None] // DS) & (row[None] % DS == t)
    return c


def since(count):
    return max(count, 0) if type(count) is int else count


def run(eng, n, body):
    body(0)
    if n > 3:
        with eng.Fori(1, n - 1) as i:
            body(i)
    else:
        for i in range(1, n - 1):
            body(i)
    if n > 1:
        body(n - 1)


class Core:

    def __init__(self, nc, io, ctx):
        self.nc, self.io, self.ctx = nc, io, ctx
        self.signals, self.names = {}, {}
        self.stage_ctx = ExitStack()
        sb = self.sb
        self.const = sb("const", [P, NCONST], F32)
        self.identb = sb("identb", [P, P], BF16)
        self.maskb = sb("maskb", [P, C_COS - C_TRIN], BF16)
        self.ones = sb("ones", [P, P], F32)
        self.gains = sb("gains", [P, KD, 8], F32)
        self.taps = sb("taps", [P, 2, KF, 20], F32)
        self.xT = sb("xT", [P, KD, T], F32)
        self.hhi = sb("hhi", [P, KD, T], F16)
        self.hlo = sb("hlo", [P, KD, T], BF16)
        self.wst = sb("wst", [P, SLOTS, SLOTW], F32)
        self.whi = sb("whi", [P, SLOTS, SLOTW], F16)
        self.wlo = sb("wlo", [P, SLOTS, SLOTW], BF16)
        self.ps = ctx.enter_context(nc.psum_tensor("ps", [P, 8, 512], F32))
        self.ident = self.const[:, C_ID:C_ID + P]
        self.stream = []
        self.w_landed = [self.lasting(f"w_landed{k}") for k in range(SLOTS)]
        self.w_hi = self.lasting("w_hi_ready")
        self.w_lo = self.lasting("w_lo_ready")
        self.w_used = self.lasting("w_used")

    def sb(self, name, shape, dt, ctx=None):
        n = self.names[name] = self.names.get(name, 0) + 1
        return (ctx or self.ctx).enter_context(self.nc.sbuf_tensor(f"{name}_{n}" if n > 1 else name, shape, dt))

    def norm_buffers(self, ctx):
        self.yT = self.sb("yT", [P, KD, T], F32, ctx)
        self.ssq = self.sb("ssq", [P, T], F32, ctx)
        self.rstd = self.sb("rstd", [P, 2, T], F32, ctx)
        self.sq = self.sb("sq", [P, 2, T], F32, ctx)
        self.tmp = self.sb("tmp", [P, 2, T], F32, ctx)

    def lasting(self, name):
        return self.ctx.enter_context(self.nc.semaphore(name))

    def sig(self, name):
        if name not in self.signals:
            self.signals[name] = self.stage_ctx.enter_context(
                self.nc.semaphore(name, num=STAGE_SEMS + len(self.signals)))
        return self.signals[name]

    @contextmanager
    def stage(self):
        with self.nc.Block() as block:
            yield block
        self.nc.all_engine_barrier(sems_to_clear=range(STAGE_SEMS, STAGE_SEMS + len(self.signals)))
        self.stage_ctx.close()
        self.signals.clear()



def load_block(core, sp, seg, i, k, first):
    n_blocks, width, source = core.stream[seg]
    n = i * 4 + k
    sp.wait_ge(core.w_hi, since(first + n - SLOTS + 1))
    sp.wait_ge(core.w_lo, since(first + n - SLOTS + 1))
    src = source(i, k)
    dst = core.wst[:, k, 0:width].rearrange("p (a c) -> p a c", a=src.shape[1])
    sp.dma_start(dst, src).then_inc(core.w_landed[k], 16)


def load_stage(core, sp, seg, first):
    n_blocks = core.stream[seg][0]
    if n_blocks // 4 > 3:
        with sp.Fori(2, n_blocks // 4) as i:
            for k in range(4):
                load_block(core, sp, seg, i, k, first)
    else:
        for i in range(2, n_blocks // 4):
            for k in range(4):
                load_block(core, sp, seg, i, k, first)
    if seg + 1 < len(core.stream):
        for i in range(2):
            for k in range(4):
                load_block(core, sp, seg + 1, i, k, first + n_blocks)


def cast_width(core, seg, i):
    n_blocks, width, _ = core.stream[seg]
    if type(i) is int and i == n_blocks // 4 - 1:
        return core.stream[seg + 1][1] if seg + 1 < len(core.stream) else 0
    return width


def cast_hi(core, act, seg, i, k, first):
    w = cast_width(core, seg, i)
    if not w:
        return
    n = first + (i + 1) * 4 + k
    act.wait_ge(core.w_used, since(n - SLOTS + 1))
    act.wait_ge(core.w_landed[k], (n - k) * 4 + 16)
    act.copy(core.whi[:, k, 0:w], core.wst[:, k, 0:w]).then_inc(core.w_hi, 1)


def cast_lo(core, pool, seg, i, k, first):
    w = cast_width(core, seg, i)
    if not w:
        return
    n = first + (i + 1) * 4 + k
    pool.wait_ge(core.w_used, since(n - SLOTS + 1))
    pool.wait_ge(core.w_hi, n + 1)
    pool.tensor_tensor(core.wlo[:, k, 0:w], core.wst[:, k, 0:w], core.whi[:, k, 0:w], ALU.subtract).then_inc(core.w_lo, 1)


def weights_ready(core, pe, n):
    pe.wait_ge(core.w_hi, n + 1)
    pe.wait_ge(core.w_lo, n + 1)


def product(pe, out, parts, lhs, rhs, start, stop):
    n = len(parts)
    for j, (ka, kb) in enumerate(parts):
        a_hi, a_lo = lhs(ka)
        b_hi, b_lo = rhs(kb)
        pe.matmul(out, a_hi, b_hi, start=start and j == 0, stop=False)
        pe.matmul(out, a_hi, b_lo, start=False, stop=False)
        last = pe.matmul(out, a_lo, b_hi, start=False, stop=stop and j == n - 1)
    return last


def weight_streams(core):
    io = core.io

    def tokens_major(w, col0):
        def source(i, k):
            return w[(k % 2) * 512:(k % 2) * 512 + 512, bass.ds((i * 2 + k // 2) * 256 + col0, 256)].rearrange(
                "(a p) c -> p a c", p=P)
        return source

    def features(w, col0=0):
        def source(i, k):
            return w[:, bass.ds((i * 4 + k) * P + col0, P)].rearrange("(a p) c -> p a c", p=P)
        return source

    def up(w):
        def source(i, k):
            return w[:, bass.ds((i * 2 + k // 2) * P + (k % 2) * F, P)].rearrange("(a p) c -> p a c", p=P)
        return source

    def down(w):
        def source(i, k):
            r0 = (k % 2) * (F // 2)
            return w[r0:r0 + F // 2, bass.ds((i * 2 + k // 2) * P, P)].rearrange("(a p) c -> p a c", p=P)
        return source

    ffn = [[(2 * KF, 8 * P, up(io["ffn_w_up"][l])), (2 * KD, SLOTW, down(io["ffn_w_down"][l]))] for l in range(2)]
    core.stream = [
        (QKV // P, 8 * P, tokens_major(io["nsa_w_in"][0], 0)),
        (KD, 8 * P, features(io["nsa_w_o"][0])), *ffn[0],
        (2 * GH * DK // P, 8 * P, features(io["gla_w_in"][0])),
        (2 * GH * DV // P, 8 * P, tokens_major(io["gla_w_in"][0], 2 * GH * DK)),
        (KD, 8 * P, features(io["gla_w_o"][0])), *ffn[1]]
    core.starts = [sum(s[0] for s in core.stream[:n]) for n in range(len(core.stream))]



def setup(core):
    nc, io = core.nc, core.io
    ps = core.ps
    with ExitStack() as own:
        xtok = core.sb("xtok", [P, NT, D], F32, own)
        rows = core.sb("rows", [20, 2, F], F32, own)
        grow = core.sb("grow", [8, D], F32, own)
        const_in, x_in, gains_in, rows_in = (core.sig(n) for n in ("const_in", "x_in", "gains_in", "rows_in"))
        turned, turned_small, taken, taken_small, filled = (
            core.sig(n) for n in ("x_turned", "small_turned", "x_taken", "small_taken", "constants_filled"))

        with core.stage() as block:
            @block.sync
            def _(sp):
                sp.dma_start(core.const[:, :], io["consts"]).then_inc(const_in, 16)
                for i in range(4):
                    sp.dma_start(xtok[:, i, :], io["x_prompt"][0, i * P:(i + 1) * P, :]).then_inc(x_in, 16)
                sp.dma_start(xtok[0:SAMP, 4, :], io["x_sample"].rearrange("b t d -> (b t) d")).then_inc(x_in, 16)
                sp.dma_start(grow[:, :], io["norm_gain"].rearrange("l n d -> (l n) d")).then_inc(gains_in, 16)
                for k in range(4):
                    load_block(core, sp, 0, 0, k, 0)
                for l in range(2):
                    sp.dma_start(rows[0:3, l, :], io["ffn_conv_w"][l]).then_inc(rows_in, 16)
                    sp.dma_start(rows[3:4, l, :], io["ffn_conv_b"][l:l + 1]).then_inc(rows_in, 16)
                    sp.dma_start(rows[4:20, l, :], io["state_ffn_conv"][l].rearrange("b j f -> (b j) f")
                                 ).then_inc(rows_in, 16)
                for k in range(4):
                    load_block(core, sp, 0, 1, k, 0)

            @block.tensor
            def _(pe):
                pe.wait_ge(const_in, 16)
                pe.wait_ge(x_in, 80)
                for k in range(KD):
                    b = (k % 2) * 2
                    pe.wait_ge(taken, since(k - 1))
                    pe.wait_ge(taken_small, since(k - 1))
                    for i in range(4):
                        last = pe.transpose(ps[:, b, i * P:(i + 1) * P], xtok[:, i, k * P:(k + 1) * P], core.ident)
                    last.then_inc(turned, 1)
                    pe.transpose(ps[:, b + 1, 0:SAMP], xtok[0:SAMP, 4, k * P:(k + 1) * P],
                                 core.ident[0:SAMP, 0:SAMP]).then_inc(turned_small, 1)
                pe.wait_ge(gains_in, 16)
                for k in range(KD):
                    last = pe.transpose(ps[:, 4, k * 8:k * 8 + 8], grow[:, k * P:(k + 1) * P], core.ident[0:8, 0:8])
                last.then_inc(turned_small, 1)
                pe.wait_ge(rows_in, 96)
                for l in range(2):
                    for m in range(KF):
                        last = pe.transpose(ps[:, 5 + l, m * 20:m * 20 + 20], rows[:, l, m * P:(m + 1) * P],
                                            core.ident[0:20, 0:20])
                    last.then_inc(turned_small, 1)

            @block.scalar
            def _(act):
                for k in range(KD):
                    act.wait_ge(turned, k + 1)
                    act.copy(core.xT[:, k, 0:SEQ], ps[:, (k % 2) * 2, :]).then_inc(taken, 1)
                    if k % 2:
                        cast_hi(core, act, 0, -1, k // 2, 0)

            @block.vector
            def _(dve):
                dve.memset(core.ones[:, :], 1.0).then_inc(filled, 1)
                dve.wait_ge(const_in, 16)
                dve.tensor_copy(core.identb[:, :], core.ident).then_inc(filled, 1)
                dve.tensor_copy(core.maskb[:, :], core.const[:, C_TRIN:C_COS]).then_inc(filled, 1)
                for k in range(KD):
                    dve.wait_ge(turned_small, k + 1)
                    dve.tensor_copy(core.xT[:, k, SEQ:T], ps[:, (k % 2) * 2 + 1, 0:SAMP]).then_inc(taken_small, 1)
                dve.wait_ge(turned_small, KD + 1)
                dve.tensor_copy(core.gains[:, :, :], ps[:, 4, 0:KD * 8].rearrange("p (k g) -> p k g", g=8)).then_inc(taken_small, 1)
                for l in range(2):
                    dve.wait_ge(turned_small, KD + 2 + l)
                    dve.tensor_copy(core.taps[:, l, :, :], ps[:, 5 + l, 0:KF * 20].rearrange(
                    "p (m r) -> p m r", r=20)).then_inc(taken_small, 1)

            @block.gpsimd
            def _(pool):
                for k in range(4):
                    cast_lo(core, pool, 0, -1, k, 0)



def norms(core, post, pre):
    nc, ps = core.nc, core.ps
    xT, yT, sq, tmp, rstd = core.xT, core.yT, core.sq, core.tmp, core.rstd
    summed, var, root, inverse = (core.sig(n) for n in ("squares_summed", "variance", "deviation", "rstd_ready"))
    scaled, x_ready, sq_ready, sq_used, h32, h_hi, h_lo = (
        core.sig(n) for n in ("y_scaled", "x_ready", "square_ready", "square_used", "h_ready", "h_hi", "h_lo"))
    n_post, n_pre = post is not None, pre is not None
    with core.stage() as block:
        @block.tensor
        def _(pe):
            if n_post:
                for h in range(2):
                    last = pe.matmul(ps[:, h, 0:HALF], core.ones[:, :], core.ssq[:, h * HALF:(h + 1) * HALF],
                                     start=True, stop=True)
                last.then_inc(summed, 1)
            if n_pre:
                for k in range(KD):
                    pe.wait_ge(sq_ready, k + 1)
                    for h in range(2):
                        last = pe.matmul(ps[:, 2 + h, 0:HALF], core.ones[:, :],
                                         sq[:, k % 2, h * HALF:(h + 1) * HALF], start=(k == 0), stop=(k == KD - 1))
                    last.then_inc(sq_used, 1)

        @block.vector
        def _(dve):
            def variance(bank, slot, n):
                dve.tensor_scalar(rstd[:, slot, :].rearrange("p (h c) -> p h c", h=2),
                                  ps[:, bank:bank + 2, 0:HALF], 1.0 / D, EPS, ALU.mult, ALU.add).then_inc(var, 1)
                dve.wait_ge(root, n)
                dve.reciprocal(rstd[:, slot, :], rstd[:, slot, :]).then_inc(inverse, 1)
                dve.wait_ge(inverse, n)
            if n_post:
                dve.wait_ge(summed, 1)
                variance(0, 0, 1)
                for k in range(KD):
                    dve.wait_ge(x_ready, since(k - 1))
                    dve.tensor_tensor(tmp[:, k % 2, :], yT[:, k, :], rstd[:, 0, :], ALU.mult).then_inc(scaled, 1)
                    if k:
                        dve.wait_ge(scaled, k)
                        dve.scalar_tensor_tensor(xT[:, k - 1, :], tmp[:, (k - 1) % 2, :],
                                                 core.gains[:, k - 1, post:post + 1], xT[:, k - 1, :],
                                                 ALU.mult, ALU.add).then_inc(x_ready, 1)
                dve.wait_ge(scaled, KD)
                dve.scalar_tensor_tensor(xT[:, KD - 1, :], tmp[:, (KD - 1) % 2, :],
                                         core.gains[:, KD - 1, post:post + 1], xT[:, KD - 1, :],
                                         ALU.mult, ALU.add).then_inc(x_ready, 1)
                dve.wait_ge(x_ready, KD)
            if n_pre:
                dve.wait_ge(sq_used, KD)
                variance(2, 1, n_post + 1)
                for k in range(KD):
                    if k >= 2:
                        dve.wait_ge(h_hi, since(k - 1))
                        if k % 2 == 0:
                            dve.wait_ge(h_lo, k // 2)
                    dve.scalar_tensor_tensor(tmp[:, k % 2, :], xT[:, k, :], core.gains[:, k, pre:pre + 1],
                                             rstd[:, 1, :], ALU.mult, ALU.mult).then_inc(h32, 1)
                    if k % 2:
                        dve.wait_ge(h_hi, k + 1)
                        dve.tensor_tensor(core.hlo[:, k, :], tmp[:, 1, :], core.hhi[:, k, :], ALU.subtract).then_inc(core.sig("h_lo_odd"), 1)
                        dve.wait_ge(core.sig("h_lo_odd"), k // 2 + 1)

        @block.scalar
        def _(act):
            if n_post:
                act.wait_ge(var, 1)
                act.activation(rstd[:, 0, :], rstd[:, 0, :], ACT.Sqrt).then_inc(root, 1)
            if n_pre:
                for k in range(KD):
                    if n_post:
                        act.wait_ge(x_ready, k + 1)
                    act.wait_ge(sq_used, since(k - 1))
                    act.activation(sq[:, k % 2, :], xT[:, k, :], ACT.Square).then_inc(sq_ready, 1)
                act.wait_ge(var, n_post + 1)
                act.activation(rstd[:, 1, :], rstd[:, 1, :], ACT.Sqrt).then_inc(root, 1)
                for k in range(KD):
                    act.wait_ge(h32, k + 1)
                    act.copy(core.hhi[:, k, :], tmp[:, k % 2, :]).then_inc(h_hi, 1)

        @block.gpsimd
        def _(pool):
            if n_pre:
                for k in range(0, KD, 2):
                    pool.wait_ge(h_hi, k + 1)
                    pool.tensor_tensor(core.hlo[:, k, :], tmp[:, 0, :], core.hhi[:, k, :], ALU.subtract).then_inc(h_lo, 1)



def token_major(core, seg, dest, roped=None):
    nc, ps = core.nc, core.ps
    first = core.starts[seg]
    groups = core.stream[seg][0] // 2
    ready, taken, rot, t_ready = (core.sig(n) for n in ("rows_ready", "rows_taken", "rotated", "swapped"))
    cleared = core.sig("rows_cleared")
    h = lambda k, i: (core.hhi[:, k, i * P:min(i * P + P, T)], core.hlo[:, k, i * P:min(i * P + P, T)])

    with ExitStack() as own:
        swap = core.sb("swap", [P, NT, 256], F32, own) if roped else None
        with core.stage() as block:
            @block.sync
            def _(sp):
                load_stage(core, sp, seg, first)

            @block.tensor
            def _(pe):
                def body(i):
                    for g in range(2):
                        for k in (2 * g, 2 * g + 1):
                            weights_ready(core, pe, first + 4 * i + k)
                        pe.wait_ge(taken, since((2 * i + g) * 3 - 3))
                        for t in range(NT):
                            rows = P if t < 4 else SAMP
                            out = ps[0:rows, g * 3 + t // 2, (t % 2) * 256:(t % 2) * 256 + 256]
                            last = product(
                                pe, out, [(k, k) for k in range(KD)], lambda k: h(k, t),
                                lambda k: (block_hi(core, 2 * g + k // 4, 256)[:, k % 4, :],
                                           block_lo(core, 2 * g + k // 4, 256)[:, k % 4, :]), True, True)
                            if t in (1, 3):
                                last.then_inc(ready, 1)
                            if t == 4:
                                last.then_inc(core.w_used, 2)
                run(pe, groups // 2, body)

            @block.scalar
            def _(act):
                def body(i):
                    for g in range(2):
                        n = 2 * i + g
                        col = n * 256
                        for t in range(3):
                            tiles = 2 if t < 2 else 1
                            rows = P if t < 2 else SAMP
                            if t < 2:
                                act.wait_ge(ready, n * 2 + t + 1)
                            else:
                                act.wait_ge(core.w_used, first + 2 * n + 2)
                            act.copy(dest[0:rows, 2 * t:2 * t + tiles, bass.ds(col, 256)],
                                     ps[0:rows, g * 3 + t, 0:256 * tiles].rearrange("p (a c) -> p a c", c=256)).then_inc(taken, 1)
                        for k in (2 * g, 2 * g + 1):
                            cast_hi(core, act, seg, i, k, first)
                act.wait_ge(cleared, 1)
                run(act, groups // 2, body)

            @block.gpsimd
            def _(pool):
                def body(i):
                    for k in range(4):
                        cast_lo(core, pool, seg, i, k, first)
                run(pool, groups // 2, body)

            @block.vector
            def _(dve):
                if not roped:
                    dve.memset(dest[:, 4, :], 0.0).then_inc(cleared, 1)
                else:
                    cos = core.const[:, C_COS:C_SIN].rearrange("p (i d) -> p i d", i=NT)
                    sin = core.const[:, C_SIN:C_SEG].rearrange("p (i d) -> p i d", i=NT)
                    done = 0
                    dve.memset(dest[:, 4, :], 0.0).then_inc(cleared, 1)

                    def rotate(n, count):
                        dve.wait_ge(taken, n * 3 + 3)
                        x = dest[:, :, n * 256:n * 256 + 256]
                        x4 = x.rearrange("p i (h d) -> p i h d", d=DH)
                        s4 = swap[:, :, :].rearrange("p i (h d) -> p i h d", d=DH)
                        sn = sin.unsqueeze(2).broadcast_to([P, NT, 4, 64])
                        cs = cos.unsqueeze(2).broadcast_to([P, NT, 4, 64])
                        dve.wait_ge(rot, since(count))
                        dve.tensor_tensor(s4[:, :, :, 0:32], x4[:, :, :, 32:64], sn[:, :, :, 0:32], ALU.mult)
                        dve.tensor_tensor(s4[:, :, :, 32:64], x4[:, :, :, 0:32], sn[:, :, :, 32:64], ALU.mult).then_inc(t_ready, 1)
                        dve.wait_ge(t_ready, 2 * count + 1)
                        dve.tensor_tensor(x4, x4, cs, ALU.mult).then_inc(t_ready, 1)
                        dve.wait_ge(t_ready, 2 * count + 2)
                        dve.tensor_tensor(x, x, swap[:, :, :], ALU.add).then_inc(rot, 1)
                    for n in roped:
                        rotate(n, done)
                        done += 1


def block_hi(core, k, cols):
    return core.whi[:, k, 0:1024].rearrange("p (a c) -> p a c", c=cols)


def block_lo(core, k, cols):
    return core.wlo[:, k, 0:1024].rearrange("p (a c) -> p a c", c=cols)



class Compressed:

    def __init__(self, core, ctx):
        self.kcT = core.sb("kcT", [DH, DB + 1, P], F32, ctx)
        self.vcT = core.sb("vcT", [DH, DB + 1, P], F32, ctx)


def compress(core, cmp, units, loads):
    nc, ps = core.nc, core.ps
    turned, moved, summed, shifted, combined, biased = (core.sig(n) for n in (
        "taps_turned", "taps_moved", "chunks_summed", "second_shifted", "blocks_combined", "pe_projected"))
    moved_act = core.sig("taps_moved_act")
    w_in, cleared = core.sig("cmp_w_in"), core.sig("cmp_cleared")
    n_q = len(units) * 16
    with ExitStack() as own:
        pairs = core.sb("tap_pairs", [P, 2, 4 * units[0][0]], F32, own)
        second = core.sb("second_half", [DH, 2, 4 * units[0][0]], F32, own)
        bias2 = core.sb("bias_second", [DH, 2], F32, own)
        weight = core.sb("cmp_w", [P, 2, 8, 2, DH], F32, own)
        taps_pe = core.sb("cmp_pe", [P, 2, 2, 8], F32, own)
        bias = core.sb("cmp_bias", [DH, 2], F32, own)
        def move(eng, copy, q, j, signal):
            n = units[q // 16][0]
            eng.wait_ge(turned, q + 1)
            eng.wait_ge(summed, since(q - 1))
            for par in range(2):
                dst = pairs[j * DH:(j + 1) * DH, q % 2, 0:4 * n].rearrange("p (u a n) -> p u a n", u=2, a=2)[:, :, par]
                src = ps[par * DH:(par + 1) * DH, (q % 2) * 2 + j, 0:2 * n].rearrange("p (u n) -> p u n", u=2)
                copy(dst, src).then_inc(signal, 1)

        with core.stage() as block:
            @block.sync
            def _(sp):
                w = core.io["nsa_cmp_w"][0]
                for kv in range(2):
                    for h in range(2):
                        sp.dma_start(weight[:, kv, :, h, :], w[kv, h * 16:h * 16 + 16].rearrange(
                            "(a j) d e -> (j d) a e", j=2)).then_inc(w_in, 16)
                    sp.dma_start(taps_pe[:, kv, :, :], core.io["nsa_cmp_pe"][0, kv].rearrange(
                        "(c a j) d -> (j d) c a", c=2, j=2), allow_slow_non_contiguous=True).then_inc(w_in, 16)
                loads(sp)

            @block.tensor
            def _(pe):
                pe.wait_ge(w_in, 96)
                for kv in range(2):
                    for a in range(8):
                        last = pe.matmul(ps[:, 6, kv * 2:kv * 2 + 2],
                                         weight[:, kv, a, :, :].rearrange("p h e -> p (h e)"),
                                         taps_pe[:, kv, :, a], start=(a == 0), stop=(a == 7))
                last.then_inc(biased, 1)

                def turn(q):
                    n, x, landed, value, _, _ = units[q // 16]
                    kv, a = q // 8 % 2, q % 8
                    if q % 16 == 0:
                        pe.wait_ge(landed, value)
                    pe.wait_ge(moved, since(2 * (q - 1)))
                    pe.wait_ge(moved_act, since(2 * (q - 1)))
                    for j in range(2):
                        for u in range(2):
                            c = kv * KVW + u * P
                            last = pe.transpose(ps[:, (q % 2) * 2 + j, u * n:(u + 1) * n],
                                                x[0:n, 2 * a + j, c:c + P], core.ident[0:n, 0:n])
                    last.then_inc(turned, 1)
                turn(0)
                for q in range(n_q):
                    if q + 1 < n_q:
                        turn(q + 1)
                    n = units[q // 16][0]
                    kv, a, s = q // 8 % 2, q % 8, q // 8
                    if a == 0:
                        pe.wait_ge(combined, since(4 * (s - 1)))
                    pe.wait_ge(moved, 2 * q + 2)
                    pe.wait_ge(moved_act, 2 * q + 2)
                    pe.matmul(ps[:, 4 + s % 2, 0:4 * n], weight[:, kv, a, :, :].rearrange("p h e -> p (h e)"),
                              pairs[:, q % 2, 0:4 * n], start=(a == 0), stop=(a == 7)).then_inc(summed, 1)

            @block.scalar
            def _(act):
                act.wait_ge(biased, 1)
                act.copy(bias2[:, :], ps[DH:P, 6, 1:4:2]).then_inc(shifted, 1)

                def shift(s):
                    n = units[s // 2][0]
                    act.wait_ge(summed, 8 * s + 8)
                    act.wait_ge(combined, since(4 * (s - 1)))
                    act.copy(second[:, s % 2, 0:4 * n], ps[DH:P, 4 + s % 2, 0:4 * n]).then_inc(shifted, 1)
                for q in range(n_q):
                    move(act, act.copy, q, 0, moved_act)
                    if q % 8 == 7 and q > 8:
                        shift(q // 8 - 1)
                shift(n_q // 8 - 1)

            @block.vector
            def _(dve):
                b0 = units[0][4]
                for x in (cmp.kcT, cmp.vcT):
                    dve.memset(x[:, b0:b0 + sum(u[5] for u in units), :], 0.0).then_inc(cleared, 1)
                dve.wait_ge(shifted, 1)
                dve.tensor_tensor(bias[:, :], ps[0:DH, 6, 0:4:2], bias2[:, :], ALU.add).then_inc(cleared, 1)
                dve.wait_ge(cleared, 3)

                def combine(s):
                    n, _, _, _, b0, nb = units[s // 2]
                    kv = s % 2
                    dest = cmp.vcT if kv else cmp.kcT
                    dve.wait_ge(shifted, s + 2)
                    for g in range(KVH):
                        one = ps[0:DH, 4 + s % 2, g * n:(g + 1) * n].rearrange("p (b c) -> p b c", c=32)
                        two = second[:, s % 2, g * n:(g + 1) * n].rearrange("p (b c) -> p b c", c=32)
                        dve.scalar_tensor_tensor(
                        dest[:, b0:b0 + nb, g * 32:g * 32 + NBLK], one[:, :, 0:NBLK], bias[:, kv:kv + 1],
                        two[:, :, 1:NBLK + 1], ALU.add, ALU.add).then_inc(combined, 1)
                for q in range(n_q):
                    move(dve, dve.tensor_copy, q, 1, moved)
                    if q % 8 == 7 and q > 8:
                        combine(q // 8 - 1)
                combine(n_q // 8 - 1)



class Attention:
    def __init__(self, core, ctx):
        self.qkv = core.sb("qkv", [P, NT, QKV], F32, ctx)
        self.gates = core.sb("gates", [P, NT, 48], F32, ctx)
        self.qs = core.sb("q_sample", [DH, DB, 64], F32, ctx)
        self.qblk = core.sb("q_blocks", [P, DB, 2, 64], F32, ctx)
        self.gate_rows = core.sb("gate_rows", [P, DB, 2], F32, ctx)
        self.kTn = core.sb("new_keys", [P, 2, 2, SAMP], F32, ctx)

KS, VS, KW, VW = 1536, 1792, 2048, 2304


def attention_inputs(core, at, kT):
    nc, ps, io = core.nc, core.ps, core.io
    gw_cast, gates_summed, gates_done = core.sig("gate_w_cast"), core.sig("gates_summed"), core.sig("gates_done")
    keys_turned, keys_even, keys_odd = core.sig("keys_turned"), core.sig("keys_even"), core.sig("keys_odd")
    q_turned, q_moved, zeroed, g_turned, g_moved = (
        core.sig(n) for n in ("qs_turned", "qs_moved", "qblk_zeroed", "gates_turned", "gates_moved"))
    with ExitStack() as own:
        gT = core.sb("gates_turned", [HEADS, 3, SAMP], F32, own)
        gs = core.sb("gates_contig", [SAMP, 3, HEADS], F32, own)
        gw = core.sb("gate_w", [P, KD, 48], F32, own)
        gwhi, gwlo = core.sb("gate_w_hi", [P, KD, 48], F16, own), core.sb("gate_w_lo", [P, KD, 48], BF16, own)
        with core.stage() as block:
            @block.sync
            def _(sp):
                sp.dma_start(gw[:, :, :], io["nsa_w_in"][0][:, QKV:PROJ].rearrange("(k p) c -> p k c", p=P)
                             ).then_inc(core.sig("gate_w_in"), 16)

            @block.tensor
            def _(pe):
                for n in range(8):
                    y, g = n // 4, n % 4
                    col = (KS, KW)[y] + g * DH
                    if n % 2:
                        pe.wait_ge(keys_odd, since(n // 2 - 1))
                    else:
                        pe.wait_ge(keys_even, since(n // 2 - 1))
                    for i in range(4):
                        last = pe.transpose(ps[0:DH, n % 4, i * P:(i + 1) * P], at.qkv[:, i, col:col + DH], core.ident)
                    last.then_inc(keys_turned, 1)
                pe.wait_ge(gw_cast, 2)
                for t in range(NT):
                    rows = P if t < 4 else SAMP
                    last = product(pe, ps[0:rows, 4, t * 48:t * 48 + 48], [(k, k) for k in range(KD)],
                                   lambda k: (core.hhi[:, k, t * P:t * P + rows], core.hlo[:, k, t * P:t * P + rows]),
                                   lambda k: (gwhi[:, k, :], gwlo[:, k, :]), True, True)
                last.then_inc(gates_summed, 1)
                for h in range(HEADS):
                    last = pe.transpose(ps[0:DH, 5, h * SAMP:(h + 1) * SAMP],
                                        at.qkv[0:SAMP, 4, h * DH:(h + 1) * DH], core.ident[0:SAMP, 0:SAMP])
                last.then_inc(q_turned, 1)
                for y in range(2):
                    for u in range(2):
                        col = (KS, KW)[y] + u * P
                        last = pe.transpose(ps[:, 6, (y * 2 + u) * SAMP:(y * 2 + u + 1) * SAMP],
                                            at.qkv[0:SAMP, 4, col:col + P], core.ident[0:SAMP, 0:SAMP])
                last.then_inc(q_turned, 1)
                pe.wait_ge(gates_done, 4)
                for c in range(3):
                    last = pe.transpose(ps[0:HEADS, 7, c * SAMP:(c + 1) * SAMP], gs[:, c, :],
                                        core.ident[0:SAMP, 0:SAMP])
                last.then_inc(g_turned, 1)
                pe.wait_ge(g_moved, 1)
                for c in range(3):
                    for t in range(DS):
                        rows = slice(64, P) if c == 2 else slice(0, 64)
                        col = 128 + (8 if c == 0 else 0)
                        last = pe.matmul(ps[rows, 7, col:col + DB],
                                         core.const[0:HEADS, C_SEL + t * 64:C_SEL + t * 64 + 64],
                                         gT[:, c, :].rearrange("p (b t) -> p b t", t=DS)[:, :, t],
                                         start=(t == 0), stop=(t == DS - 1))
                last.then_inc(g_turned, 1)

            @block.scalar
            def _(act):
                act.wait_ge(core.sig("gate_w_in"), 16)
                act.wait_ge(zeroed, 1)
                act.copy(gwhi[:, :, :], gw[:, :, :]).then_inc(gw_cast, 1)
                for n in range(1, 8, 2):
                    act.wait_ge(keys_turned, n + 1)
                    act.copy(kT[:, n // 4, n % 4, :], ps[0:DH, n % 4, :]).then_inc(keys_odd, 1)
                act.wait_ge(gates_summed, 1)
                act.activation(at.gates[:, 0:4, :], ps[:, 4, 0:192].rearrange("p (t c) -> p t c", c=48),
                               ACT.Exp, scale=-1.0).then_inc(gates_done, 1)
                act.activation(at.gates[0:SAMP, 4, :], ps[0:SAMP, 4, 192:240], ACT.Exp, scale=-1.0).then_inc(gates_done, 1)

            @block.vector
            def _(dve):
                dve.memset(at.gates[:, 4, :], 0.0).then_inc(zeroed, 1)
                dve.memset(at.gate_rows[:, :, :], 0.0).then_inc(zeroed, 1)
                dve.memset(at.qblk[:, :, :, :], 0.0).then_inc(zeroed, 1)
                dve.wait_ge(gw_cast, 1)
                dve.tensor_tensor(gwlo[:, :, :], gw[:, :, :], gwhi[:, :, :], ALU.subtract).then_inc(gw_cast, 1)
                for n in range(0, 8, 2):
                    dve.wait_ge(keys_turned, n + 1)
                    dve.tensor_copy(kT[:, n // 4, n % 4, :], ps[0:DH, n % 4, :]).then_inc(keys_even, 1)
                dve.wait_ge(q_turned, 1)
                dve.tensor_copy(at.qs[:, :, :].rearrange("p b (h t) -> p h b t", t=DS),
                                ps[0:DH, 5, :].rearrange("p (h b t) -> p h b t", h=HEADS, b=DB)).then_inc(q_moved, 1)
                dve.wait_ge(q_turned, 2)
                dve.tensor_copy(at.kTn[:, :, :, :], ps[:, 6, 0:4 * SAMP].rearrange(
                "p (y u c) -> p y u c", y=2, u=2)).then_inc(q_moved, 1)
                dve.wait_ge(q_moved, 1)
                dve.wait_ge(zeroed, 3)
                for g in range(KVH):
                    p0 = (g % 2) * DH
                    dve.tensor_copy(at.qblk[p0:p0 + DH, :, g // 2, g * 16:g * 16 + 16],
                                    at.qs[:, :, g * 16:g * 16 + 16]).then_inc(q_moved, 1)
                dve.wait_ge(gates_done, 2)
                dve.tensor_scalar(at.gates[:, :, :], at.gates[:, :, :], 1.0, None, ALU.add).then_inc(gates_done, 1)
                dve.wait_ge(gates_done, 3)
                dve.reciprocal(at.gates[:, :, :], at.gates[:, :, :]).then_inc(q_moved, 1)
                dve.wait_ge(q_moved, 7)
                dve.tensor_copy(gs[:, :, :], at.gates[0:SAMP, 4, :].rearrange("p (h c) -> p c h", c=3)).then_inc(gates_done, 1)
                dve.wait_ge(g_turned, 1)
                dve.tensor_copy(gT[:, :, :], ps[0:HEADS, 7, 0:3 * SAMP].rearrange("p (c n) -> p c n", c=3)).then_inc(g_moved, 1)
                dve.wait_ge(g_turned, 2)
                dve.tensor_copy(at.gate_rows[:, :, 0], ps[:, 7, 128:128 + DB]).then_inc(g_moved, 1)
                dve.tensor_copy(at.gate_rows[0:64, :, 1], ps[0:64, 7, 136:136 + DB]).then_inc(g_moved, 1)



def prompt_attention(core, at, cmp, kT):
    nc, ps = core.nc, core.ps
    names = ("q_staged", "vc_staged", "qT_turned", "qT_moved", "cmp_scored", "cmp_step", "cmp_turned", "cmp_moved",
             "scored", "row_max", "exp_done", "p_scaled", "p_turned", "pT_slc", "pT_win", "attended", "out_taken",
             "out_hi", "out_lo", "exp_cmp", "sum_step", "staged_v")
    (q_staged, vc_staged, qT_turned, qT_moved, cmp_scored, cmp_step, cmp_turned, cmp_moved, scored, row_max, exp_done,
     p_scaled, p_turned, pT_slc, pT_win, attended, out_taken, out_hi, out_lo, exp_cmp, sum_step, staged_v) = (
        core.sig(n) for n in names)
    trin = core.maskb[:, 0:P]
    cmpp = core.maskb[:, C_CMPP - C_TRIN:C_NEW - C_TRIN]
    U = 16
    with ExitStack() as own:
        sb = lambda n, s: core.sb(n, s, F32, own)
        qg, vg, qT = sb("q_group", [P, 4, 256]), sb("v_group", [P, 4, 2, DH]), sb("qT", [DH, 4, SEQ])
        kcg, vcx, vcz = sb("kc_group", [DH, 32]), sb("vc_repeated", [DH, 4, 32]), sb("vc_by_tile", [P, 4, DH])
        pc, pcT = sb("p_cmp", [P, U, 32]), sb("p_cmp_T", [P, 4, P])
        mc, sc = sb("max_cmp", [P, U]), sb("sum_cmp", [P, U])
        prob = sb("prob", [P, 2, 2, SEQ])
        pT = at.qkv[:, 0:4, 1024:1024 + SEQ].rearrange("p (a y) c -> p a y c", a=2)
        mx, sums, coef, rcp = sb("row_max", [P, 2, 2]), sb("row_sum", [P, 2, 2]), sb("coef", [P, 2, 2]), sb("rcp", [P, 2, 2])
        oF = sb("o_head", [P, SEQ])

        with core.stage() as block:
            @block.tensor
            def _(pe):
                def body(g):
                    pe.wait_ge(vc_staged, g + 1)
                    pe.wait_ge(exp_done, since(32 * g))
                    pe.wait_ge(pT_slc, since(16 * g))
                    pe.wait_ge(cmp_moved, since(g))
                    pe.matmul(ps[:, 4, :].rearrange("p (h c) -> p h c", h=4), core.identb[:, :],
                              cmpp.unsqueeze(1).broadcast_to([P, 4, P]), start=True, stop=False)
                    for hh in range(4):
                        for i in range(4):
                            last = pe.transpose(ps[0:DH, hh, i * P:(i + 1) * P], qg[:, i, hh * DH:(hh + 1) * DH],
                                                core.ident)
                        last.then_inc(qT_turned, 1)
                    pe.transpose(ps[:, 5, 0:DH], vcx[:, :, :].rearrange("p i n -> p (i n)"),
                                 core.ident[0:DH, 0:DH]).then_inc(cmp_turned, 1)
                    pe.wait_ge(qT_moved, 4 * g + 4)
                    pe.wait_ge(staged_v, 5 * g + 5)
                    for u in range(U):
                        last = pe.matmul(ps[:, 4, u * 32:u * 32 + 32], qT[:, u // 4, (u % 4) * P:(u % 4 + 1) * P],
                                         kcg[:, :], start=False, stop=(u == U - 1))
                    last.then_inc(cmp_scored, 1)

                    def score(u):
                        hh, i = u // 4, u % 4
                        w = (i + 1) * P
                        pe.wait_ge(exp_done, since(32 * g + 2 * (u - 1)))
                        for y in range(2):
                            out = ps[:, (u % 2) * 2 + y, :]
                            pe.matmul(out[:, i * P:w], core.identb[:, :], trin, start=True, stop=False)
                            last = pe.matmul(out[:, i * P:w], qT[:, hh, i * P:w], kT[:, y, g, i * P:w],
                                             start=False, stop=True)
                            if i:
                                last = pe.matmul(out[:, 0:i * P], qT[:, hh, i * P:w], kT[:, y, g, 0:i * P],
                                                 start=True, stop=True)
                        last.then_inc(scored, 1)

                    def turn(u):
                        i = u % 4
                        pe.wait_ge(p_scaled, 32 * g + 2 * u + 2)
                        pe.wait_ge(pT_slc, since(16 * g + u))
                        pe.wait_ge(pT_win, since(16 * g + u))
                        for y in range(2):
                            for j in range(i + 1):
                                last = pe.transpose(ps[:, 5 + y, j * P:(j + 1) * P],
                                                    prob[:, u % 2, y, j * P:(j + 1) * P], core.ident)
                        last.then_inc(p_turned, 1)

                    def attend(u):
                        hh, i = u // 4, u % 4
                        pe.wait_ge(pT_slc, 16 * g + u + 1)
                        pe.wait_ge(pT_win, 16 * g + u + 1)
                        if i == 0:
                            pe.wait_ge(out_taken, since(4 * g + hh))
                        out = ps[0:DH, 7, i * P:(i + 1) * P]
                        for y in range(2):
                            for j in range(i + 1):
                                pe.matmul(out, vg[:, j, y, :], pT[:, u % 2, y, j * P:(j + 1) * P],
                                          start=(y == 0 and j == 0), stop=False)
                        pe.matmul(out, vcz[:, i, :], pcT[:, hh, :], start=False, stop=True).then_inc(attended, 1)

                    score(0)
                    score(1)
                    pe.wait_ge(cmp_step, 5 * g + 5)
                    for hh in range(4):
                        last = pe.transpose(ps[:, 4, hh * P:(hh + 1) * P],
                                            pc[:, hh * 4:hh * 4 + 4, :].rearrange("p u n -> p (u n)"), core.ident)
                    last.then_inc(cmp_turned, 1)
                    turn(0)
                    pe.wait_ge(cmp_moved, g + 1)
                    for u in range(U):
                        if u + 2 < U:
                            score(u + 2)
                        if u + 1 < U:
                            turn(u + 1)
                        attend(u)
                run(pe, KVH, body)

            @block.scalar
            def _(act):
                def body(g):
                    for hh in (1, 3):
                        act.wait_ge(qT_turned, 4 * g + hh + 1)
                        act.copy(qT[:, hh, :], ps[0:DH, hh, :]).then_inc(qT_moved, 1)
                    act.wait_ge(cmp_step, 5 * g + 3)
                    act.activation(pc[:, :, :], pc[:, :, :], ACT.Exp, scale=SCALE).then_inc(exp_cmp, 1)

                    def expo(u):
                        w = (u % 4 + 1) * P
                        act.wait_ge(row_max, 32 * g + 2 * u + 2)
                        act.wait_ge(p_turned, since(16 * g + u - 1))
                        for y in range(2):
                            act.activation(prob[:, u % 2, y, 0:w], ps[:, (u % 2) * 2 + y, 0:w], ACT.Exp,
                                           bias=mx[:, u % 2, y:y + 1], scale=SCALE,
                                           accum_out=sums[:, u % 2, y:y + 1]).then_inc(exp_done, 1)

                    def move(u):
                        w = (u % 4 + 1) * P
                        act.wait_ge(p_turned, 16 * g + u + 1)
                        act.wait_ge(attended, since(16 * g + u - 1))
                        act.copy(pT[:, u % 2, 1, 0:w], ps[:, 6, 0:w]).then_inc(pT_win, 1)

                    def out(hh):
                        rows = slice((hh % 2) * DH, (hh % 2) * DH + DH)
                        act.wait_ge(attended, 16 * g + 4 * hh + 4)
                        act.wait_ge(out_lo, since(4 * g + hh - 1))
                        act.copy(oF[rows, :], ps[0:DH, 7, :]).then_inc(out_taken, 1)
                        act.wait_ge(out_taken, 4 * g + hh + 1)
                        act.copy(core.hhi[rows, 2 * g + hh // 2, 0:SEQ], oF[rows, :]).then_inc(out_hi, 1)
                    expo(0)
                    expo(1)
                    for u in range(U):
                        move(u)
                        if u + 2 < U:
                            expo(u + 2)
                        if u % 4 == 0 and u:
                            out(u // 4 - 1)
                    out(3)
                run(act, KVH, body)

            @block.vector
            def _(dve):
                dve.memset(vcz[:, :, :], 0.0).then_inc(core.sig("vcz_zeroed"), 1)
                dve.wait_ge(core.sig("vcz_zeroed"), 1)

                def body(g):
                    dve.wait_ge(qT_turned, since(4 * g))
                    dve.tensor_copy(qg[:, :, :], at.qkv[:, 0:4, bass.ds(g * 256, 256)]).then_inc(q_staged, 1)
                    dve.tensor_copy(kcg[:, :], cmp.kcT[:, DB, bass.ds(g * 32, 32)]).then_inc(q_staged, 1)
                    dve.tensor_copy(vcx[:, :, :], cmp.vcT[:, DB, bass.ds(g * 32, 32)].unsqueeze(1)
                                    .broadcast_to([DH, 4, 32])).then_inc(vc_staged, 1)
                    dve.wait_ge(attended, since(16 * g))
                    for hh in (0, 2):
                        dve.wait_ge(qT_turned, 4 * g + hh + 1)
                        dve.tensor_copy(qT[:, hh, :], ps[0:DH, hh, :]).then_inc(qT_moved, 1)
                    dve.wait_ge(cmp_turned, 2 * g + 1)
                    for i in range(4):
                        rows = slice(i * 32, i * 32 + 32)
                        dve.tensor_copy(vcz[rows, i, :], ps[rows, 5, 0:DH]).then_inc(staged_v, 1)
                    dve.tensor_copy(
                    vg[:, :, :, :],
                    at.qkv[:, 0:4, VS:QKV].rearrange("p i (y c) -> p i y c", c=256)
                    [:, :, 0::2, bass.ds(g * DH, DH)]).then_inc(staged_v, 1)
                    dve.wait_ge(cmp_scored, g + 1)
                    s3 = ps[:, 4, :].rearrange("p (u n) -> p u n", n=32)
                    dve.tensor_reduce(mc[:, :], s3, AX.X, ALU.max).then_inc(cmp_step, 1)
                    dve.wait_ge(cmp_step, 5 * g + 1)
                    dve.tensor_scalar(mc[:, :], mc[:, :], NEG / 10, None, ALU.max).then_inc(cmp_step, 1)
                    dve.wait_ge(cmp_step, 5 * g + 2)
                    dve.tensor_tensor(pc[:, :, :], s3, mc[:, :].unsqueeze(2).broadcast_to([P, U, 32]),
                                      ALU.subtract).then_inc(cmp_step, 1)

                    def row(u):
                        w = (u % 4 + 1) * P
                        dve.wait_ge(scored, 16 * g + u + 1)
                        dve.tensor_reduce(mx[:, u % 2, :], ps[:, (u % 2) * 2:(u % 2) * 2 + 2, 0:w], AX.X,
                                          ALU.max).then_inc(row_max, 1)
                        dve.wait_ge(row_max, 32 * g + 2 * u + 1)
                        dve.tensor_scalar(mx[:, u % 2, :], mx[:, u % 2, :], -SCALE, None, ALU.mult).then_inc(row_max, 1)

                    def scale(u):
                        hh, i = u // 4, u % 4
                        w = (i + 1) * P
                        dve.wait_ge(exp_done, 32 * g + 2 * u + 2)
                        k = 48 * g + 3 * u
                        dve.tensor_scalar(rcp[:, u % 2, :], sums[:, u % 2, :], 1e-30, None, ALU.max).then_inc(sum_step, 1)
                        dve.wait_ge(sum_step, k + 1)
                        dve.reciprocal(rcp[:, u % 2, :], rcp[:, u % 2, :]).then_inc(sum_step, 1)
                        dve.wait_ge(sum_step, k + 2)
                        dve.tensor_tensor(coef[:, u % 2, :], rcp[:, u % 2, :],
                                          at.gates[:, i, bass.ds(g * 12 + hh * 3 + 1, 2)], ALU.mult).then_inc(sum_step, 1)
                        dve.wait_ge(sum_step, k + 3)
                        for y in range(2):
                            dve.tensor_scalar(prob[:, u % 2, y, 0:w], prob[:, u % 2, y, 0:w],
                                              coef[:, u % 2, y:y + 1], None, ALU.mult).then_inc(p_scaled, 1)

                    def move(u):
                        w = (u % 4 + 1) * P
                        dve.wait_ge(p_turned, 16 * g + u + 1)
                        dve.wait_ge(attended, since(16 * g + u - 1))
                        dve.tensor_copy(pT[:, u % 2, 0, 0:w], ps[:, 5, 0:w]).then_inc(pT_slc, 1)

                    def out(hh):
                        rows = slice((hh % 2) * DH, (hh % 2) * DH + DH)
                        dve.wait_ge(out_hi, 4 * g + hh + 1)
                        dve.tensor_tensor(core.hlo[rows, 2 * g + hh // 2, 0:SEQ], oF[rows, :],
                                          core.hhi[rows, 2 * g + hh // 2, 0:SEQ], ALU.subtract).then_inc(out_lo, 1)
                    row(0)
                    row(1)
                    dve.wait_ge(exp_cmp, g + 1)
                    dve.tensor_reduce(sc[:, :], pc[:, :, :], AX.X, ALU.add).then_inc(cmp_step, 1)
                    dve.wait_ge(cmp_step, 5 * g + 4)
                    dve.tensor_scalar(sc[:, :], sc[:, :], 1e-30, None, ALU.max).then_inc(core.sig("cmp_recip"), 1)
                    dve.wait_ge(core.sig("cmp_recip"), 3 * g + 1)
                    dve.reciprocal(sc[:, :], sc[:, :]).then_inc(core.sig("cmp_recip"), 1)
                    dve.wait_ge(core.sig("cmp_recip"), 3 * g + 2)
                    dve.tensor_tensor(
                    sc[:, :].rearrange("p (h i) -> p h i", i=4), sc[:, :].rearrange("p (h i) -> p h i", i=4),
                    at.gates[:, 0:4, bass.ds(g * 12, 12)].rearrange("p i (h c) -> p h i c", c=3)[:, :, :, 0],
                    ALU.mult).then_inc(core.sig("cmp_recip"), 1)
                    dve.wait_ge(core.sig("cmp_recip"), 3 * g + 3)
                    dve.tensor_tensor(pc[:, :, :], pc[:, :, :], sc[:, :].unsqueeze(2).broadcast_to([P, U, 32]),
                                      ALU.mult).then_inc(cmp_step, 1)
                    scale(0)
                    dve.wait_ge(cmp_turned, 2 * g + 2)
                    dve.tensor_copy(pcT[:, :, :], ps[:, 4, :].rearrange("p (h t) -> p h t", h=4)).then_inc(cmp_moved, 1)
                    scale(1)
                    for u in range(U):
                        move(u)
                        if u + 2 < U:
                            row(u + 2)
                            scale(u + 2)
                        if u % 4 == 1 and u > 1:
                            out(u // 4 - 1)
                    out(3)
                run(dve, KVH, body)



def sample_attention(core, at, cmp):
    nc, ps, io = core.nc, core.ps, core.io
    names = ("page_in", "vc_turned", "vc_moved", "keys_filled", "k_landed", "v_landed0", "v_landed1", "k_turned",
             "kT_moved_dve", "kT_moved_act", "rows_staged", "v_staged", "s_scored", "s_max", "s_exp", "s_sum",
             "s_scaled", "s_turned", "s_moved", "s_attended", "s_out", "s_spread", "s_hi", "s_lo")
    (page_in, vc_turned, vc_moved, keys_filled, k_landed, v_landed0, v_landed1, k_turned, kT_dve, kT_act, staged,
     v_staged, scored, maxed, exped, summed, scaled, turned, moved, attended, out_taken, spread, s_hi, s_lo) = (
        core.sig(n) for n in names)
    v_landed = (v_landed0, v_landed1)
    trin0 = C_TRIN
    with ExitStack() as own:
        sb = lambda n, s: core.sb(n, s, F32, own)
        pages = core.sb("pages", [1, DB * NPAGE], I32, own)
        kn, vn = sb("k_rows", [P, 2, NPAGE, 256]), sb("v_rows", [P, 2, 2, NPAGE, 256])
        kTb = sb("kT_batch", [P, 2, 2, T])
        qst, qcs, vcs = sb("q_stage", [P, 2, 64]), sb("qc_stage", [DH, P]), sb("vc_stage", [P, 2, DH])
        prob, pcs = sb("s_prob", [P, T]), sb("s_pcmp", [64, P])
        pT, pcT = sb("s_probT", [P, 5, P]), sb("s_pcmpT", [P, 64])
        mx2, mx = sb("s_max2", [P, 2]), sb("s_mx", [P, 2])
        sums, coef = sb("s_sums", [P, 2]), sb("s_coef", [P, 2])
        vc = sb("vc", [P, DB, DH])
        outs, oT = sb("s_outs", [P, DB, 64]), sb("s_oT", [P, KD, SAMP])

        with core.stage() as block:
            @block.sync
            def _(sp):
                sp.dma_start(pages[:, :], io["page_table"].rearrange("(o b) n -> o (b n)", o=1)).then_inc(
                    page_in, 16)
                sp.wait_ge(page_in, 16)

                def body(i):
                    for par in range(2):
                        b = 2 * i + par
                        ids = [sp.value_load(pages[0:1, bass.ds(b * NPAGE + n, 1)], min_val=0,
                                             max_val=io["cache_nsa_kv"].shape[1] - 1) for n in range(NPAGE)]
                        sp.wait_ge(k_turned, since(4 * b))
                        pool_kv = io["cache_nsa_kv"][0]
                        win = io["state_win_kv"][0, b] if type(b) is int else \
                            io["state_win_kv"][0, bass.ds(b, 1)].rearrange("o t s g d -> (o t) s g d")
                        for n in range(NPAGE):
                            page = pool_kv[bass.ds(ids[n], 1)].rearrange("o t s g d -> (o t) s (g d)")
                            sp.dma_start(kn[:, 0, n, :], page[:, 2, :]).then_inc(k_landed, 16)
                            if n == 0:
                                sp.wait_ge(attended, since(b - 1))
                            sp.dma_start(vn[:, par, 0, n, :], page[:, 3, :]).then_inc(v_landed[par], 16)
                        for y, dst, s in ((0, kn[:, 1, :, :], k_landed), (1, vn[:, par, 1, :, :], v_landed[par])):
                            sp.dma_start(dst, win[:, y].rearrange("(n p) g d -> p n (g d)", p=P)).then_inc(s, 16)
                run(sp, DB // 2, body)

            @block.tensor
            def _(pe):
                for b in range(DB):
                    last = pe.transpose(ps[:, 7, b * DH:(b + 1) * DH], cmp.vcT[:, b, :], core.ident[0:DH, 0:DH])
                last.then_inc(vc_turned, 1)

                def turn_keys(b):
                    pe.wait_ge(k_landed, 16 * 5 * (b + 1))
                    pe.wait_ge(kT_dve, since(2 * b))
                    pe.wait_ge(kT_act, since(2 * b))
                    for y in range(2):
                        for u in range(2):
                            for n in range(NPAGE):
                                last = pe.transpose(ps[:, y * 2 + u, n * P:(n + 1) * P],
                                                    kn[:, y, n, u * P:(u + 1) * P], core.ident)
                            last.then_inc(k_turned, 1)

                def body(i):
                    for par in range(2):
                        b = 2 * i + par
                        pe.wait_ge(staged, 2 * b + 2)
                        pe.wait_ge(kT_dve, 2 * b + 2)
                        pe.wait_ge(kT_act, 2 * b + 2)
                        for y in range(2):
                            rows = slice(y * 64, y * 64 + 64)
                            for h in range(2):
                                for u in range(2):
                                    pe.matmul(ps[rows, 4 + h, 0:HALF], qst[:, u, :],
                                              kTb[:, y, u, h * HALF:(h + 1) * HALF], start=(u == 0), stop=False)
                        pe.matmul(ps[:, 4, 0:DS], core.identb[:, :],
                                  core.maskb[:, C_WIN - trin0:C_WIN - trin0 + DS], start=False, stop=True)
                        pe.matmul(ps[:, 5, HALF - 32:HALF], core.identb[:, :],
                                  core.maskb[:, bass.ds(b * 32 + C_NEW - trin0, 32)], start=False, stop=True)
                        pe.matmul(ps[:, 6, 0:P], core.identb[:, :],
                                  core.maskb[:, C_CMPS - trin0:C_CMPS - trin0 + P], start=True, stop=False)
                        pe.matmul(ps[:, 6, 0:P], qcs[:, :], cmp.kcT[:, b, :], start=False, stop=True).then_inc(scored, 1)
                        if not (type(b) is int and b == DB - 1):
                            turn_keys(b + 1)
                        pe.wait_ge(scaled, 2 * b + 2)
                        for n in range(4):
                            last = pe.transpose(ps[:, 7, n * P:(n + 1) * P], prob[:, n * P:(n + 1) * P], core.ident)
                        last.then_inc(turned, 1)
                        pe.transpose(ps[0:32, 6, P:2 * P], prob[:, SEQ:T], core.ident)
                        pe.transpose(ps[:, 6, 2 * P:2 * P + 64], pcs[:, :], core.ident[0:64, 0:64]).then_inc(turned, 1)
                        pe.wait_ge(moved, 2 * b + 2)
                        pe.wait_ge(core.sig("s_moved_act"), b + 1)
                        pe.wait_ge(v_staged, b + 1)
                        pe.wait_ge(v_landed[par], 16 * 5 * (i + 1))
                        for u in range(2):
                            out = ps[:, 6, 384 + u * 32:416 + u * 32]
                            for y in range(2):
                                c = y * 64 + u * 32
                                for n in range(4):
                                    pe.matmul(out, vn[:, par, y, n, u * P:(u + 1) * P], pT[:, n, c:c + 32],
                                              start=(y == 0 and n == 0), stop=False)
                                v = (VS, VW)[y] + u * P
                                pe.matmul(out, at.qkv[0:SAMP, 4, v:v + P], pT[0:SAMP, 4, c:c + 32],
                                          start=False, stop=False)
                            last = pe.matmul(out, vcs[:, :, :].rearrange("p a d -> p (a d)"),
                                             pcT[:, u * 32:u * 32 + 32], start=False, stop=True)
                        last.then_inc(attended, 1)
                        pe.wait_ge(out_taken, b + 1)
                pe.wait_ge(vc_moved, 1)
                turn_keys(0)
                run(pe, DB // 2, body)

            @block.scalar
            def _(act):
                def move_keys(b):
                    for u in range(2):
                        act.wait_ge(k_turned, 4 * b + 3 + u)
                        act.wait_ge(scored, since(b))
                        act.copy(kTb[:, 1, u, 0:PAST], ps[:, 2 + u, :]).then_inc(kT_act, 1)

                def body(i):
                    for par in range(2):
                        b = 2 * i + par
                        act.wait_ge(maxed, 5 * b + 5)
                        act.wait_ge(turned, since(2 * b))
                        act.activation(prob[:, :].rearrange("p (h c) -> p h c", h=2), ps[:, 4:6, 0:HALF], ACT.Exp,
                                       bias=mx[:, 0:1], scale=SCALE, accum_out=sums[:, 0:1]).then_inc(exped, 1)
                        act.activation(pcs[:, :], ps[0:64, 6, 0:P], ACT.Exp, bias=mx[0:64, 1:2], scale=SCALE,
                                       accum_out=sums[0:64, 1:2]).then_inc(exped, 1)
                        if not (type(b) is int and b == DB - 1):
                            move_keys(b + 1)
                        act.wait_ge(turned, 2 * b + 2)
                        act.wait_ge(attended, since(b))
                        act.copy(pT[:, 0:4, :], ps[:, 7, :].rearrange("p (n r) -> p n r", n=4)).then_inc(core.sig("s_moved_act"), 1)
                move_keys(0)
                run(act, DB // 2, body)
                act.wait_ge(spread, 8)
                act.copy(core.hhi[:, :, SEQ:T], oT[:, :, :]).then_inc(s_hi, 1)

            @block.vector
            def _(dve):
                dve.memset(sums[:, :], 1.0).then_inc(keys_filled, 1)
                dve.memset(mx[:, :], 0.0).then_inc(keys_filled, 1)
                dve.memset(qcs[:, :], 0.0).then_inc(keys_filled, 1)
                dve.tensor_copy(kTb[:, :, :, PAST:T], at.kTn[:, :, :, :]).then_inc(keys_filled, 1)
                dve.wait_ge(vc_turned, 1)
                dve.tensor_copy(vc[:, :, :], ps[:, 7, :].rearrange("p (b d) -> p b d", d=DH)).then_inc(vc_moved, 1)
                dve.wait_ge(vc_moved, 1)
                dve.wait_ge(keys_filled, 4)

                def move_keys(b):
                    for u in range(2):
                        dve.wait_ge(k_turned, 4 * b + 1 + u)
                        dve.wait_ge(scored, since(b))
                        dve.tensor_copy(kTb[:, 0, u, 0:PAST], ps[:, u, :]).then_inc(kT_dve, 1)

                def body(i):
                    for par in range(2):
                        b = 2 * i + par
                        dve.wait_ge(scored, since(b))
                        dve.tensor_copy(qst[:, :, :], at.qblk[:, b, :, :]).then_inc(staged, 1)
                        dve.tensor_copy(qcs[:, 0:64], at.qs[:, b, :]).then_inc(staged, 1)
                        dve.wait_ge(scored, b + 1)
                        dve.tensor_reduce(mx2[:, :], ps[:, 4:6, 0:HALF], AX.X, ALU.max).then_inc(maxed, 1)
                        dve.tensor_reduce(mx[0:64, 1:2], ps[0:64, 6, 0:P], AX.X, ALU.max).then_inc(maxed, 1)
                        dve.wait_ge(maxed, 5 * b + 2)
                        dve.tensor_reduce(mx[:, 0:1], mx2[:, :], AX.X, ALU.max).then_inc(maxed, 1)
                        dve.tensor_scalar(mx[0:64, 1:2], mx[0:64, 1:2], NEG / 10, -SCALE, ALU.max, ALU.mult).then_inc(maxed, 1)
                        dve.wait_ge(maxed, 5 * b + 3)
                        dve.tensor_scalar(mx[:, 0:1], mx[:, 0:1], -SCALE, None, ALU.mult).then_inc(maxed, 1)
                        dve.wait_ge(exped, 2 * b + 2)
                        dve.tensor_scalar(coef[:, :], sums[:, :], 1e-30, None, ALU.max).then_inc(summed, 1)
                        dve.wait_ge(summed, 3 * b + 1)
                        dve.reciprocal(coef[:, :], coef[:, :]).then_inc(summed, 1)
                        dve.wait_ge(summed, 3 * b + 2)
                        dve.tensor_tensor(coef[:, :], coef[:, :], at.gate_rows[:, b, :], ALU.mult).then_inc(summed, 1)
                        dve.wait_ge(summed, 3 * b + 3)
                        dve.tensor_scalar(prob[:, :], prob[:, :], coef[:, 0:1], None, ALU.mult).then_inc(scaled, 1)
                        dve.tensor_scalar(pcs[:, :], pcs[:, :], coef[0:64, 1:2], None, ALU.mult).then_inc(scaled, 1)
                        if not (type(b) is int and b == DB - 1):
                            move_keys(b + 1)
                        dve.wait_ge(attended, since(b))
                        dve.tensor_copy(vcs[:, :, :], vc[:, b, :].unsqueeze(1).broadcast_to([P, 2, DH])).then_inc(v_staged, 1)
                        dve.wait_ge(turned, 2 * b + 2)
                        dve.tensor_copy(pT[0:32, 4, :], ps[0:32, 6, P:2 * P]).then_inc(moved, 1)
                        dve.tensor_copy(pcT[:, :], ps[:, 6, 2 * P:2 * P + 64]).then_inc(moved, 1)
                        dve.wait_ge(attended, b + 1)
                        dve.tensor_copy(outs[:, b, :], ps[:, 6, 384:448]).then_inc(out_taken, 1)
                move_keys(0)
                run(dve, DB // 2, body)
                dve.wait_ge(out_taken, DB)
                for g in range(KVH):
                    for c in range(2):
                        src = outs[(g % 2) * DH:(g % 2) * DH + DH, :, g * 16:g * 16 + 16].rearrange(
                            "p b (a c t) -> p c a b t", a=2, c=2)[:, c]
                        dst = oT[c * DH:c * DH + DH, 2 * g:2 * g + 2, :].rearrange("p a (b t) -> p a b t", t=DS)
                        dve.tensor_copy(dst, src).then_inc(spread, 1)
                dve.wait_ge(s_hi, 1)
                dve.tensor_tensor(core.hlo[:, :, SEQ:T], oT[:, :, :], core.hhi[:, :, SEQ:T], ALU.subtract).then_inc(s_lo, 1)



def features_to_y(core, seg, moving, parts, epilogue=None):
    nc, ps = core.nc, core.ps
    first = core.starts[seg]
    n_tiles = core.stream[seg][0] // parts
    kt = core.stream[seg][1] // P
    per = 4 // parts
    y_taken, y_sq, y_added, cleared = core.sig("y_taken"), core.sig("y_squared"), core.sig("ssq_added"), core.sig("ssq_cleared")
    hi, lo = moving
    extra = epilogue or {}
    with core.stage() as block:
        @block.sync
        def _(sp):
            load_stage(core, sp, seg, first)
            if "sync" in extra:
                extra["sync"](sp)

        @block.tensor
        def _(pe):
            if "tensor" in extra:
                extra["tensor"](pe)

            def body(i):
                for k in range(4):
                    m, part = i * per + k // parts, k % parts
                    bank = (k // parts) % 2 * 2
                    weights_ready(core, pe, first + 4 * i + k)
                    if part == 0:
                        pe.wait_ge(y_taken, since(m - 1))
                    w_hi, w_lo = (w[:, k, 0:kt * P].rearrange("p (a c) -> p a c", c=P) for w in (core.whi, core.wlo))
                    for h in range(2):
                        cols = slice(h * HALF, (h + 1) * HALF)
                        last = product(pe, ps[:, bank + h, 0:HALF], [(a, part * kt + a) for a in range(kt)],
                                       lambda a: (w_hi[:, a, :], w_lo[:, a, :]),
                                       lambda a: (hi[:, a, cols], lo[:, a, cols]), part == 0, part == parts - 1)
                    last.then_inc(core.w_used, 1)
            run(pe, n_tiles // per, body)

        @block.scalar
        def _(act):
            if "scalar" in extra:
                extra["scalar"](act)

            def body(i):
                for k in range(4):
                    m = i * per + k // parts
                    cast_hi(core, act, seg, i, k, first)
                    if k % parts == parts - 1:
                        act.wait_ge(y_taken, m + 1)
                        act.wait_ge(y_added, since(m - 1))
                        act.activation(core.sq[:, (k // parts) % 2, :], core.yT[:, m, :], ACT.Square).then_inc(y_sq, 1)
            run(act, n_tiles // per, body)

        @block.vector
        def _(dve):
            dve.memset(core.ssq[:, :], 0.0).then_inc(cleared, 1)
            dve.wait_ge(cleared, 1)
            if "vector" in extra:
                extra["vector"](dve)

            def body(i):
                for j in range(per):
                    m = i * per + j
                    dve.wait_ge(core.w_used, first + (m + 1) * parts)
                    dve.tensor_copy(core.yT[:, m, :].rearrange("p (h c) -> p h c", h=2),
                                    ps[:, (j % 2) * 2:(j % 2) * 2 + 2, 0:HALF]).then_inc(y_taken, 1)
                    dve.wait_ge(y_sq, m + 1)
                    dve.wait_ge(y_added, since(m))
                    dve.tensor_tensor(core.ssq[:, :], core.ssq[:, :], core.sq[:, j % 2, :], ALU.add).then_inc(y_added, 1)
            run(dve, n_tiles // per, body)

        @block.gpsimd
        def _(pool):
            def body(i):
                for k in range(4):
                    cast_lo(core, pool, seg, i, k, first)
            run(pool, n_tiles // per, body)



GW = 2 + SEQ + DB * (DS + 2)


def ffn_up(core, l, seg, ghi, glo, kept):
    nc, ps = core.nc, core.ps
    first = core.starts[seg]
    gate_in, conv, gelu, prod, g_hi, g_lo, keep, cleared = (core.sig(n) for n in (
        "gate_in", "conv_step", "gelu_done", "product_done", "g_hi", "g_lo", "rows_kept", "gate_cleared"))
    with ExitStack() as own:
        gate = core.sb("gate", [P, 2, GW], F32, own)
        cv = core.sb("conv", [P, 2, GW - 2], F32, own)
        ge = core.sb("gelu", [P, 2, GW - 2], F32, own)
        gp = core.sb("gated", [P, 2, T], F32, own)
        later = lambda x: x.rearrange("p (b j) -> p b j", j=DS + 2)
        with core.stage() as block:
            @block.sync
            def _(sp):
                load_stage(core, sp, seg, first)

            @block.tensor
            def _(pe):
                def body(i):
                    for k in range(4):
                        m, q, val = 2 * i + k // 2, k // 2, k % 2
                        weights_ready(core, pe, first + 4 * i + k)
                        if val:
                            pe.wait_ge(prod, since(3 * (m - 1)))
                        else:
                            pe.wait_ge(gate_in, since(4 * (m - 1)))
                        w_hi, w_lo = block_hi(core, k, P), block_lo(core, k, P)
                        for h in range(2):
                            cols = slice(h * HALF, (h + 1) * HALF)
                            last = product(pe, ps[:, 4 * q + 2 * val + h, 0:HALF], [(a, a) for a in range(KD)],
                                           lambda a: (w_hi[:, a, :], w_lo[:, a, :]),
                                           lambda a: (core.hhi[:, a, cols], core.hlo[:, a, cols]), True, True)
                        last.then_inc(core.w_used, 1)
                run(pe, KF // 2, body)

            @block.scalar
            def _(act):
                act.wait_ge(cleared, 1)

                def body(i):
                    for q in range(2):
                        m = 2 * i + q
                        act.wait_ge(core.w_used, first + 2 * m + 1)
                        act.wait_ge(conv, since(3 * (m - 1)))
                        act.wait_ge(keep, since(2 * (m - 1)))
                        act.copy(gate[:, q, 2:2 + HALF], ps[:, 4 * q, 0:HALF]).then_inc(gate_in, 1)
                        act.copy(gate[:, q, 2 + HALF:2 + SEQ], ps[:, 4 * q + 1, 0:SEQ - HALF]).then_inc(gate_in, 1)
                        act.copy(later(gate[:, q, 2 + SEQ:GW])[:, :, 2:],
                                 ps[:, 4 * q + 1, SEQ - HALF:HALF].rearrange("p (b t) -> p b t", t=DS)).then_inc(gate_in, 1)
                        act.copy(later(gate[:, q, 2 + SEQ:GW])[:, :, 0:2],
                                 core.taps[:, l, m, 4:20].rearrange("p (b j) -> p b j", j=2)).then_inc(gate_in, 1)
                        cast_hi(core, act, seg, i, 2 * q, first)
                        act.wait_ge(conv, 3 * m + 3)
                        act.wait_ge(prod, since(3 * (m - 1)))
                        act.activation(ge[:, q, :], cv[:, q, :], ACT.Gelu_apprx_tanh).then_inc(gelu, 1)
                        cast_hi(core, act, seg, i, 2 * q + 1, first)
                        act.wait_ge(prod, 3 * m + 3)
                        act.copy(ghi[:, m, :], gp[:, q, :]).then_inc(g_hi, 1)
                run(act, KF // 2, body)

            @block.vector
            def _(dve):
                dve.memset(gate[:, :, 0:2], 0.0).then_inc(cleared, 1)

                def body(i):
                    for q in range(2):
                        m = 2 * i + q
                        tap = lambda j: core.taps[:, l, m, j:j + 1]
                        dve.wait_ge(gate_in, 4 * m + 4)
                        dve.wait_ge(gelu, since(m - 1))
                        dve.tensor_scalar(cv[:, q, :], gate[:, q, 0:GW - 2], tap(0), tap(3), ALU.mult, ALU.add).then_inc(conv, 1)
                        for j in (1, 2):
                            dve.wait_ge(conv, 3 * m + j)
                            dve.scalar_tensor_tensor(cv[:, q, :], gate[:, q, j:GW - 2 + j], tap(j), cv[:, q, :],
                                                     ALU.mult, ALU.add).then_inc(conv, 1)
                        dve.wait_ge(gelu, m + 1)
                        dve.wait_ge(core.w_used, first + 2 * m + 2)
                        dve.wait_ge(g_lo, since(m - 1))
                        for out, a, v in (
                                (gp[:, q, 0:HALF], ge[:, q, 0:HALF], ps[:, 4 * q + 2, 0:HALF]),
                                (gp[:, q, HALF:SEQ], ge[:, q, HALF:SEQ], ps[:, 4 * q + 3, 0:SEQ - HALF]),
                                (gp[:, q, SEQ:T].rearrange("p (b t) -> p b t", t=DS), later(ge[:, q, SEQ:])[:, :, 2:],
                                 ps[:, 4 * q + 3, SEQ - HALF:HALF].rearrange("p (b t) -> p b t", t=DS))):
                            dve.tensor_tensor(out, a, v, ALU.mult).then_inc(prod, 1)
                run(dve, KF // 2, body)

            @block.gpsimd
            def _(pool):
                def body(i):
                    for q in range(2):
                        m = 2 * i + q
                        pool.wait_ge(gate_in, 4 * m + 4)
                        pool.tensor_copy(kept[:, m, 0:2], gate[:, q, SEQ:SEQ + 2]).then_inc(keep, 1)
                        pool.tensor_copy(kept[:, m, 2:18].rearrange("p (b j) -> p b j", j=2),
                                         later(gate[:, q, 2 + SEQ:GW])[:, :, DS:]).then_inc(keep, 1)
                        cast_lo(core, pool, seg, i, 2 * q, first)
                        pool.wait_ge(g_hi, m + 1)
                        pool.tensor_tensor(glo[:, m, :], gp[:, q, :], ghi[:, m, :], ALU.subtract).then_inc(g_lo, 1)
                        cast_lo(core, pool, seg, i, 2 * q + 1, first)
                run(pool, KF // 2, body)


def ffn(core, l, seg):
    io, ps = core.io, core.ps
    with ExitStack() as own:
        ghi = core.sb("g_hi", [P, KF, T], F16, own)
        glo = core.sb("g_lo", [P, KF, T], BF16, own)
        kept = core.sb("kept", [P, KF, 18], F32, own)
        rows = core.sb("kept_rows", [18, F], F32, own)
        ffn_up(core, l, seg, ghi, glo, kept)
        k_turned, k_moved = core.sig("kept_turned"), core.sig("kept_moved")
        core.conv_out = core.sig("conv_rows_out")
        n = -(-KF // 4)

        def turn(pe):
            for j in range(n):
                pe.wait_ge(k_moved, since(j - 3))
                for m in range(4 * j, min(4 * j + 4, KF)):
                    last = pe.transpose(ps[0:18, 4 + j % 4, (m % 4) * P:(m % 4 + 1) * P], kept[:, m, :], core.ident)
                last.then_inc(k_turned, 1)

        def move(dve):
            for j in range(n):
                dve.wait_ge(k_turned, j + 1)
                w = min(512, F - 512 * j)
                dve.tensor_copy(rows[:, 512 * j:512 * j + w], ps[0:18, 4 + j % 4, 0:w]).then_inc(k_moved, 1)

        def out(sp):
            sp.wait_ge(k_moved, n)
            sp.dma_start(io["out_ffn_p"][l, 0], rows[0:2, :]).then_inc(core.conv_out, 16)
            sp.dma_start(io["out_ffn_s"][l].rearrange("b j f -> (b j) f"), rows[2:18, :]).then_inc(core.conv_out, 16)
            sp.wait_ge(core.conv_out, 32)
        features_to_y(core, seg + 1, (ghi, glo), 2, dict(sync=out, tensor=turn, vector=move))



class Gla:
    def __init__(self, core, ctx):
        self.qk = core.sb("gla_qk", [P, 2 * GH, T], F32, ctx)
        self.cum = core.sb("gla_cum", [P, GH, T], F32, ctx)
        self.vr = core.sb("gla_vr", [P, NT, 2 * GH * DV], F32, ctx)
        self.sumsq = core.sb("gla_sumsq", [P, NT, GH], F32, ctx)
        self.ng = core.sb("gla_norm", [P, DV], F32, ctx)


def gla_heads(core, gla, seg):
    nc, ps, io = core.nc, core.ps, core.io
    first = core.starts[seg]
    n_tiles = core.stream[seg][0]
    taken, small_in, low, low_taken, z_ready, z_taken, steps, cast = (core.sig(n) for n in (
        "qk_taken", "gla_small_in", "low_rank_ready", "low_rank_taken", "gates_raw", "gates_biased", "decay_step",
        "low_w_cast"))
    with ExitStack() as own:
        gw = core.sb("low_w", [P, KD, 16], F32, own)
        gwhi, gwlo = core.sb("low_w_hi", [P, KD, 16], F16, own), core.sb("low_w_lo", [P, KD, 16], BF16, own)
        up = core.sb("gate_up", [16, GH * DK], F32, own)
        bias = core.sb("gate_bias", [P, GH], F32, own)
        ngrow = core.sb("norm_row", [1, DV], F32, own)
        lowT = core.sb("low_T", [16, T], F32, own)
        z = core.sb("z", [P, GH, T], F32, own)
        with core.stage() as block:
            @block.sync
            def _(sp):
                sp.dma_start(gw[:, :, :], io["gla_w_in"][0][:, GPROJ - 16:GPROJ].rearrange("(k p) c -> p k c", p=P)
                             ).then_inc(small_in, 16)
                sp.dma_start(up[:, :], io["gla_w_gate_up"][0]).then_inc(small_in, 16)
                sp.dma_start(bias[:, :], io["gla_b_gate"].rearrange("o (h p) -> p (o h)", p=P),
                             allow_slow_non_contiguous=True).then_inc(
                    small_in, 16)
                sp.dma_start(ngrow[:, :], io["gla_norm_gain"]).then_inc(small_in, 16)
                load_stage(core, sp, seg, first)

            @block.tensor
            def _(pe):
                pe.wait_ge(small_in, 64)
                pe.matmul(ps[:, 6, 0:DV], core.ones[0:1, :], ngrow[:, :], start=True, stop=True).then_inc(low, 1)
                pe.wait_ge(cast, 2)
                for h in range(2):
                    cols = slice(h * HALF, (h + 1) * HALF)
                    last = product(pe, ps[0:16, 4 + h, 0:HALF], [(a, a) for a in range(KD)],
                                   lambda a: (gwhi[:, a, :], gwlo[:, a, :]),
                                   lambda a: (core.hhi[:, a, cols], core.hlo[:, a, cols]), True, True)
                last.then_inc(low, 1)
                pe.wait_ge(low_taken, 2)
                for t in range(GH):
                    pe.wait_ge(z_taken, since(t))
                    for h in range(2):
                        last = pe.matmul(ps[:, 4 + h, 0:HALF], up[:, t * DK:(t + 1) * DK],
                                         lowT[:, h * HALF:(h + 1) * HALF], start=True, stop=True)
                    last.then_inc(z_ready, 1)

                def body(i):
                    for k in range(4):
                        n = 4 * i + k
                        weights_ready(core, pe, first + n)
                        pe.wait_ge(taken, since(n - 1))
                        w_hi, w_lo = block_hi(core, k, P), block_lo(core, k, P)
                        for h in range(2):
                            cols = slice(h * HALF, (h + 1) * HALF)
                            last = product(pe, ps[:, (k % 2) * 2 + h, 0:HALF], [(a, a) for a in range(KD)],
                                           lambda a: (w_hi[:, a, :], w_lo[:, a, :]),
                                           lambda a: (core.hhi[:, a, cols], core.hlo[:, a, cols]), True, True)
                        last.then_inc(core.w_used, 1)
                run(pe, n_tiles // 4, body)

            @block.scalar
            def _(act):
                act.wait_ge(small_in, 64)
                act.copy(gwhi[:, :, :], gw[:, :, :]).then_inc(cast, 1)
                act.wait_ge(low, 1)
                act.copy(gla.ng[:, :], ps[:, 6, 0:DV]).then_inc(low_taken, 1)
                act.wait_ge(low, 2)
                act.copy(lowT[:, :].rearrange("p (h c) -> p h c", h=2), ps[0:16, 4:6, 0:HALF]).then_inc(low_taken, 1)
                for t in range(GH):
                    act.wait_ge(z_ready, t + 1)
                    act.activation(z[:, t, :].rearrange("p (h c) -> p h c", h=2), ps[:, 4:6, 0:HALF],
                                   ACT.Identity, bias=bias[:, t:t + 1]).then_inc(z_taken, 1)

                def body(i):
                    for k in range(4):
                        act.wait_ge(core.w_used, first + 4 * i + k + 1)
                        act.copy(gla.qk[:, 4 * i + k, :].rearrange("p (h c) -> p h c", h=2),
                                 ps[:, (k % 2) * 2:(k % 2) * 2 + 2, 0:HALF]).then_inc(taken, 1)
                        cast_hi(core, act, seg, i, k, first)
                run(act, n_tiles // 4, body)
                act.wait_ge(steps, 1)
                act.activation(gla.cum[:, :, :], gla.cum[:, :, :], ACT.Exp).then_inc(steps, 1)
                act.wait_ge(steps, 2)
                act.activation(gla.cum[:, :, :], gla.cum[:, :, :], ACT.Ln, bias=1.0).then_inc(steps, 1)

            @block.vector
            def _(dve):
                dve.wait_ge(small_in, 64)
                dve.wait_ge(cast, 1)
                dve.tensor_tensor(gwlo[:, :, :], gw[:, :, :], gwhi[:, :, :], ALU.subtract).then_inc(cast, 1)
                dve.wait_ge(z_taken, GH)
                dve.scalar_tensor_tensor(gla.cum[:, :, :], z[:, :, :], -1.0, z[:, :, :], ALU.mult, ALU.min).then_inc(steps, 1)
                dve.wait_ge(steps, 3)
                dve.scalar_tensor_tensor(z[:, :, :], z[:, :, :], 0.0, gla.cum[:, :, :], ALU.min, ALU.subtract).then_inc(steps, 1)
                dve.wait_ge(steps, 4)
                for h in range(GH):
                    dve.tensor_tensor_scan(gla.cum[:, h, :], core.const[:, C_SEG:C_SEG + T], z[:, h, :], 0.0,
                                           ALU.mult, ALU.add).then_inc(steps, 1)

            @block.gpsimd
            def _(pool):
                def body(i):
                    for k in range(4):
                        cast_lo(core, pool, seg, i, k, first)
                run(pool, n_tiles // 4, body)



LIMIT = 40 * 16.0


def gla_core(core, gla, o):
    nc, ps, io = core.nc, core.ps, core.io
    C = SEQ // P
    names = ("g_diff", "g_exp", "g_prod", "g_turned", "g_kend", "g_att", "g_att_masked", "g_kv", "g_state", "g_out",
             "g_out_taken", "s0_in0", "s_rows", "s_kv", "s_new", "states_out", "g_qb")
    (diff, exped, prod, turned, kend_ready, att, att_masked, kv, state, out, out_taken, s0_in, s_rows, s_kv, s_new,
     states_out, _) = (core.sig(n) for n in names)
    core.states_out = states_out
    with ExitStack() as own:
        sb = lambda n, s: core.sb(n, s, F32, own)
        d = sb("g_d", [P, 2, T])
        e = sb("g_e", [P, 4, T])
        qd, kd, qi, ke = sb("g_qd", [P, T]), sb("g_kd", [P, T]), sb("g_qi", [P, T]), sb("g_ke", [P, T])
        kend = sb("g_kend", [P, NT, P])
        am = sb("g_am", [P, SEQ + 32])
        S = sb("g_S", [P, C, DV])
        el = sb("g_el", [P, C + DB])
        qb, kb = sb("g_qb", [P, DB, SAMP]), sb("g_kb", [SAMP, DB, P])
        s0, s1 = (x[:, :, :].rearrange("p k t -> p (k t)").bitcast(F32)[:, 0:DB * DV].rearrange(
            "p (b v) -> p b v", b=DB) for x in (core.hhi, core.hlo))
        sqs = sb("g_sqs", [P, DV])
        chunks = lambda x: x[:, 0:SEQ].rearrange("p (c t) -> p c t", t=P)
        seqs = lambda x: x[:, SEQ:T].rearrange("p (b t) -> p b t", t=DS)

        with core.stage() as block:
            @block.sync
            def _(sp):
                def body(h):
                    sp.wait_ge(s_new, since(8 * h))
                    g_read = core.sig("s0_read")
                    sp.wait_ge(g_read, since(h))
                    src = io["state_gla"][0].rearrange("b h k v -> h k b v")
                    sp.dma_start(s0[:, :, :], src[h] if type(h) is int else
                                 src[bass.ds(h, 1)].rearrange("o k b v -> (o k) b v")).then_inc(s0_in, 16)
                    sp.wait_ge(s_new, 8 * h + 8)
                    dst = io["out_gla_s"][0].rearrange("b h k v -> h k b v")
                    sp.dma_start(dst[h] if type(h) is int else dst[bass.ds(h, 1)].rearrange("o k b v -> (o k) b v"),
                                 s1[:, :, :]).then_inc(states_out, 16)
                    sp.wait_ge(state, C * h + C)
                    dst = io["out_gla_p"][0, 0]
                    sp.dma_start(dst[h] if type(h) is int else dst[bass.ds(h, 1)].rearrange("o k v -> (o k) v"),
                                 S[:, C - 1, :]).then_inc(core.sig("state_p_out"), 16)
                run(sp, GH, body)
                sp.wait_ge(states_out, 16 * GH)
                sp.wait_ge(core.sig("state_p_out"), 16 * GH)

            @block.tensor
            def _(pe):
                def body(h):
                    v = lambda i, rows: gla.vr[0:rows, i, bass.ds(h * DV, DV)]
                    pe.wait_ge(prod, 5 * h + 1)
                    pe.wait_ge(kend_ready, since(h))
                    for c in range(C):
                        last = pe.transpose(ps[:, 0, c * P:(c + 1) * P], ke[:, c * P:(c + 1) * P], core.ident)
                    last.then_inc(turned, 1)
                    pe.transpose(ps[0:SAMP, 6, 0:P], ke[:, SEQ:T], core.ident).then_inc(turned, 1)
                    pe.wait_ge(prod, 5 * h + 5)
                    for c in range(C):
                        last = pe.matmul(ps[:, 1, c * P:(c + 1) * P], kd[:, c * P:(c + 1) * P],
                                         qd[:, c * P:(c + 1) * P], start=True, stop=True)
                    last.then_inc(att, 1)
                    pe.matmul(ps[0:SAMP, 7, 0:SAMP], kd[:, SEQ:T], qi[:, SEQ:T], start=True, stop=True).then_inc(att, 1)
                    pe.wait_ge(s_rows, 2 * h + 2)
                    pe.wait_ge(out_taken, since(3 * h))
                    for b in range(DB):
                        last = pe.matmul(ps[:, 2 + b // 2, (b % 2) * DV:(b % 2 + 1) * DV], kb[:, b, :],
                                         v(4, SAMP), start=True, stop=True)
                        if b % 2:
                            last.then_inc(s_kv, 1)
                    pe.wait_ge(core.sig("set"), 2)
                    pe.wait_ge(att_masked, 2 * h + 2)
                    pe.wait_ge(s0_in, 16 * h + 16)
                    o_s = ps[0:SAMP, 6, 256:512]
                    for b in range(DB):
                        pe.matmul(o_s, qb[:, b, :], s0[:, b, :], start=(b == 0), stop=False)
                    pe.matmul(o_s, am[:, SEQ:SEQ + SAMP], v(4, P), start=False, stop=True).then_inc(core.sig("s0_read"), 1)
                    pe.wait_ge(s_new, 8 * h + 8)
                    pe.wait_ge(kend_ready, h + 1)
                    for c in range(C):
                        last = pe.matmul(ps[:, 2 + c // 2, (c % 2) * DV:(c % 2 + 1) * DV], kend[:, c, :], v(c, P),
                                         start=True, stop=True)
                    last.then_inc(kv, 1)
                    for c in range(C):
                        o_c = ps[:, 4 + c // 2, (c % 2) * DV:(c % 2 + 1) * DV]
                        last = pe.matmul(o_c, am[:, c * P:(c + 1) * P], v(c, P), start=True, stop=(c == 0))
                        if c:
                            pe.wait_ge(state, C * h + c)
                            last = pe.matmul(o_c, qi[:, c * P:(c + 1) * P], S[:, c - 1, :], start=False, stop=True)
                        if c % 2:
                            last.then_inc(out, 1)
                run(pe, GH, body)

            @block.scalar
            def _(act):
                def body(h):
                    act.wait_ge(prod, since(5 * h))
                    act.activation(e[:, 2, :], gla.cum[:, h, :], ACT.Exp, scale=1 / 16).then_inc(exped, 1)
                    act.wait_ge(diff, 5 * h + 5)
                    act.activation(e[:, 3, :], d[:, 1, :], ACT.Exp, scale=1 / 16).then_inc(exped, 1)
                    act.activation(e[:, 0, :], d[:, 0, :], ACT.Exp, scale=1 / 16).then_inc(exped, 1)
                    act.activation(e[:, 1, :], d[:, 0, :], ACT.Exp, scale=-1 / 16).then_inc(exped, 1)
                    act.wait_ge(turned, 2 * h + 1)
                    act.wait_ge(kv, since(h))
                    act.copy(kend[:, 0:C, :], ps[:, 0, :].rearrange("p (c k) -> p c k", k=P)).then_inc(kend_ready, 1)
                    for n in range(3):
                        if n == 0:
                            act.wait_ge(core.sig("s0_read"), h + 1)
                            src, rows, t0, nt = ps[0:SAMP, 6, 256:512], SAMP, 4, 1
                        else:
                            act.wait_ge(out, 2 * h + n)
                            src, rows, t0, nt = ps[:, 3 + n, :], P, 2 * n - 2, 2
                        dst = o[0:rows, t0:t0 + nt, bass.ds(h * DV, DV)]
                        act.copy(dst, src.rearrange("p (a c) -> p a c", c=DV)).then_inc(out_taken, 1)
                        act.wait_ge(out_taken, 3 * h + n + 1)
                        for t in range(t0, t0 + nt):
                            act.activation(sqs[0:rows, :], o[0:rows, t, bass.ds(h * DV, DV)], ACT.Square,
                                           accum_out=gla.sumsq[0:rows, t, bass.ds(h, 1)]).then_inc(core.sig("squared"), 1)
                            act.wait_ge(core.sig("squared"), 5 * h + {4: 0, 0: 1, 1: 2, 2: 3, 3: 4}[t] + 1)
                run(act, GH, body)

            @block.vector
            def _(dve):
                dve.memset(gla.sumsq[:, 4, :], 1.0).then_inc(core.sig("set"), 1)
                dve.memset(am[:, SEQ:SEQ + SAMP], 0.0).then_inc(core.sig("set"), 1)

                def body(h):
                    cum = gla.cum[:, h, :]
                    q, k = gla.qk[:, h, :], gla.qk[:, h + GH, :]
                    c3, s3 = chunks(cum), seqs(cum)
                    dve.wait_ge(exped, since(4 * h))
                    k5 = 5 * h
                    dve.tensor_tensor(chunks(d[:, 1, :]), c3[:, :, P - 1:P].broadcast_to([P, C, P]), c3,
                                      ALU.subtract).then_inc(diff, 1)
                    dve.tensor_tensor(seqs(d[:, 1, :]), s3[:, :, DS - 1:DS].broadcast_to([P, DB, DS]), s3,
                                      ALU.subtract).then_inc(diff, 1)
                    dve.tensor_tensor(chunks(d[:, 0, :]), c3, c3[:, :, P // 2 - 1:P // 2].broadcast_to([P, C, P]),
                                      ALU.subtract).then_inc(diff, 1)
                    dve.tensor_copy(d[:, 0, SEQ:T], cum[:, SEQ:T]).then_inc(diff, 1)
                    dve.wait_ge(diff, k5 + 4)
                    dve.tensor_scalar(d[:, 0, :], d[:, 0, :], LIMIT, -LIMIT, ALU.min, ALU.max).then_inc(diff, 1)
                    dve.wait_ge(exped, 4 * h + 1)
                    dve.wait_ge(state, since(C * h))
                    dve.tensor_copy(el[:, 0:C].unsqueeze(2), chunks(e[:, 2, :])[:, :, P - 1:P]).then_inc(core.sig("decays"), 1)
                    dve.tensor_copy(el[:, C:C + DB].unsqueeze(2), seqs(e[:, 2, :])[:, :, DS - 1:DS]).then_inc(core.sig("decays"), 1)
                    dve.wait_ge(out, since(2 * h))
                    dve.wait_ge(exped, 4 * h + 2)
                    dve.tensor_tensor(ke[:, :], k, e[:, 3, :], ALU.mult).then_inc(prod, 1)
                    dve.scalar_tensor_tensor(qi[:, :], q, DK ** -0.5, e[:, 2, :], ALU.mult, ALU.mult).then_inc(prod, 1)
                    dve.wait_ge(prod, 5 * h + 2)
                    dve.tensor_tensor(qb[:, :, :], qi[:, SEQ:T].unsqueeze(1).broadcast_to([P, DB, SAMP]),
                                      core.const[:, C_COLM:C_COLM + DB * SAMP].rearrange(
                                          "p (b c) -> p b c", b=DB), ALU.mult).then_inc(prod, 1)
                    dve.wait_ge(exped, 4 * h + 4)
                    dve.scalar_tensor_tensor(qd[:, :], q, DK ** -0.5, e[:, 0, :], ALU.mult, ALU.mult).then_inc(prod, 1)
                    dve.tensor_tensor(kd[:, :], k, e[:, 1, :], ALU.mult).then_inc(prod, 1)
                    dve.wait_ge(turned, 2 * h + 2)
                    dve.wait_ge(s_kv, since(4 * h))
                    dve.tensor_copy(kend[0:SAMP, C, :], ps[0:SAMP, 6, 0:P]).then_inc(s_rows, 1)
                    dve.wait_ge(s_rows, 2 * h + 1)
                    dve.tensor_tensor(kb[:, :, :], kend[0:SAMP, C:C + 1, :].broadcast_to([SAMP, DB, P]),
                                      core.const[0:SAMP, C_ROW:C_ROW + DB].unsqueeze(2).broadcast_to(
                                          [SAMP, DB, P]), ALU.mult).then_inc(s_rows, 1)
                    dve.wait_ge(att, 2 * h + 1)
                    dve.scalar_tensor_tensor(
                    chunks(am), ps[:, 1, :].rearrange("p (c t) -> p c t", t=P), 3e38,
                    core.const[:, C_TRI1:C_TRI1 + P].unsqueeze(1).broadcast_to([P, C, P]), ALU.min, ALU.mult).then_inc(att_masked, 1)
                    dve.wait_ge(core.sig("set"), 2)
                    dve.wait_ge(att, 2 * h + 2)
                    dve.scalar_tensor_tensor(am[0:SAMP, SEQ:SEQ + SAMP], ps[0:SAMP, 7, 0:SAMP], 3e38,
                                             core.const[0:SAMP, C_ATT:C_ATT + SAMP], ALU.min, ALU.mult).then_inc(att_masked, 1)
                    dve.wait_ge(core.sig("decays"), 2 * h + 2)
                    dve.wait_ge(s0_in, 16 * h + 16)
                    dve.wait_ge(states_out, since(16 * h))
                    for b in range(DB):
                        dve.wait_ge(s_kv, 4 * h + b // 2 + 1)
                        dve.scalar_tensor_tensor(s1[:, b, :], s0[:, b, :], el[:, C + b:C + b + 1],
                                                 ps[:, 2 + b // 2, (b % 2) * DV:(b % 2 + 1) * DV],
                                                 ALU.mult, ALU.add).then_inc(s_new, 1)
                    dve.wait_ge(kv, h + 1)
                    dve.wait_ge(core.sig("state_p_out"), since(16 * h))
                    dve.tensor_copy(S[:, 0, :], ps[:, 2, 0:DV]).then_inc(state, 1)
                    for c in range(1, C):
                        dve.wait_ge(state, C * h + c)
                        dve.scalar_tensor_tensor(S[:, c, :], S[:, c - 1, :], el[:, c:c + 1],
                                                 ps[:, 2 + c // 2, (c % 2) * DV:(c % 2 + 1) * DV],
                                                 ALU.mult, ALU.add).then_inc(state, 1)
                run(dve, GH, body)


def gla_finish(core, gla, o):
    nc, ps = core.nc, core.ps
    names = ("f_var", "f_silu", "f_normed", "f_gated", "f_turned", "f_hi", "f_lo")
    var, silu, normed, gated, turned, f_hi, f_lo = (core.sig(n) for n in names)
    NV = GH * DV
    with core.stage() as block:
        @block.tensor
        def _(pe):
            pe.wait_ge(gated, NT)
            for k in range(KD):
                pe.wait_ge(f_lo, since(2 * (k - 1)))
                for i in range(4):
                    pe.transpose(ps[:, (k % 2) * 2, i * P:(i + 1) * P], o[:, i, k * P:(k + 1) * P], core.ident)
                pe.transpose(ps[:, (k % 2) * 2 + 1, 0:SAMP], o[0:SAMP, 4, k * P:(k + 1) * P],
                             core.ident[0:SAMP, 0:SAMP]).then_inc(turned, 1)

        @block.scalar
        def _(act):
            for i in range(NT):
                act.activation(gla.vr[:, i, NV:2 * NV], gla.vr[:, i, NV:2 * NV], ACT.Silu).then_inc(silu, 1)
            act.wait_ge(var, 1)
            act.activation(gla.sumsq[:, :, :], gla.sumsq[:, :, :], ACT.Sqrt).then_inc(var, 1)
            for k in range(KD):
                act.wait_ge(turned, k + 1)
                act.copy(core.hhi[:, k, 0:SEQ], ps[:, (k % 2) * 2, :]).then_inc(f_hi, 1)
                act.copy(core.hhi[:, k, SEQ:T], ps[:, (k % 2) * 2 + 1, 0:SAMP]).then_inc(f_hi, 1)

        @block.vector
        def _(dve):
            dve.tensor_scalar(gla.sumsq[:, :, :], gla.sumsq[:, :, :], 1.0 / DV, EPS, ALU.mult, ALU.add).then_inc(var, 1)
            dve.wait_ge(var, 2)
            dve.reciprocal(gla.sumsq[:, :, :], gla.sumsq[:, :, :]).then_inc(var, 1)
            dve.wait_ge(var, 3)
            for i in range(NT):
                rows = P if i < 4 else SAMP
                for h in range(GH):
                    x = o[0:rows, i, h * DV:(h + 1) * DV]
                    dve.scalar_tensor_tensor(x, x, gla.sumsq[0:rows, i, h:h + 1], gla.ng[0:rows, :], ALU.mult,
                                             ALU.mult).then_inc(normed, 1)
                dve.wait_ge(silu, i + 1)
                dve.wait_ge(normed, GH * (i + 1))
                dve.tensor_tensor(o[0:rows, i, :], o[0:rows, i, :], gla.vr[0:rows, i, NV:2 * NV], ALU.mult).then_inc(gated, 1)
            for k in range(KD):
                dve.wait_ge(f_hi, 2 * k + 2)
                dve.tensor_tensor(core.hlo[:, k, 0:SEQ], ps[:, (k % 2) * 2, :], core.hhi[:, k, 0:SEQ],
                                  ALU.subtract).then_inc(f_lo, 1)
                dve.tensor_tensor(core.hlo[:, k, SEQ:T], ps[:, (k % 2) * 2 + 1, 0:SAMP], core.hhi[:, k, SEQ:T],
                                  ALU.subtract).then_inc(f_lo, 1)



def write_y(core):
    nc, ps, io = core.nc, core.ps, core.io
    turned, moved_a, moved_d = core.sig("y_turned"), core.sig("y_moved_act"), core.sig("y_moved_dve")
    y_out = [core.sig("y_out0"), core.sig("y_out1")]
    with ExitStack() as own:
        yt = core.sb("y_rows", [P, 2, D], F32, own)
        with core.stage() as block:
            @block.tensor
            def _(pe):
                for i in range(NT):
                    rows = P if i < 4 else SAMP
                    pe.wait_ge(moved_a, since(i - 1))
                    pe.wait_ge(moved_d, since(i - 1))
                    for k in range(KD):
                        last = pe.transpose(ps[0:rows, (i % 2) * 2 + k // 4, (k % 4) * P:(k % 4 + 1) * P],
                                            core.xT[:, k, i * P:i * P + rows], core.ident)
                    last.then_inc(turned, 1)

            def mover(eng, copy, half, moved):
                for i in range(NT):
                    rows = P if i < 4 else SAMP
                    eng.wait_ge(turned, i + 1)
                    eng.wait_ge(y_out[i % 2], since(16 * (i // 2)))
                    copy(yt[0:rows, i % 2, half * 512:half * 512 + 512], ps[0:rows, (i % 2) * 2 + half, :]).then_inc(moved, 1)

            @block.scalar
            def _(act):
                mover(act, act.copy, 0, moved_a)

            @block.vector
            def _(dve):
                mover(dve, dve.tensor_copy, 1, moved_d)

            @block.sync
            def _(sp):
                for i in range(NT):
                    rows = P if i < 4 else SAMP
                    sp.wait_ge(moved_a, i + 1)
                    sp.wait_ge(moved_d, i + 1)
                    dst = io["out_y_p"][0, i * P:(i + 1) * P, :] if i < 4 else \
                        io["out_y_s"].rearrange("b t d -> (b t) d")
                    sp.dma_start(dst, yt[0:rows, i % 2, :]).then_inc(y_out[i % 2], 16)
                sp.wait_ge(y_out[0], 48)
                sp.wait_ge(y_out[1], 32)
                sp.wait_ge(core.rows_out, 16 * (2 + DB))
                sp.wait_ge(core.prompt_rows_out, 16)
                sp.wait_ge(core.window_out, 16 * DB)


def write_rows(core, at, sp):
    io = core.io
    core.rows_out = core.lasting("cache_rows_out")
    core.prompt_rows_out = core.lasting("prompt_rows_out")
    sp.dma_start(io["out_nsa_p"][0, 0].rearrange("(i p) s g d -> p i (s g d)", p=P),
                 at.qkv[:, 0:4, 1024:2048]).then_inc(core.prompt_rows_out, 16)
    sp.dma_start(io["out_nsa_s"][0].rearrange("b t s g d -> (b t) (s g d)"),
                 at.qkv[0:SAMP, 4, 1024:2048]).then_inc(core.rows_out, 16)
    sp.dma_start(io["out_win_p"][0, 0].rearrange("(i p) s g d -> p i (s g d)", p=P),
                 at.qkv[:, 0:4, KW:QKV]).then_inc(core.rows_out, 16)
    for b in range(DB):
        sp.dma_start(io["out_win_s"][0, b, PAST - DS:PAST].rearrange("t s g d -> t (s g d)"),
                     at.qkv[b * DS:b * DS + DS, 4, KW:QKV]).then_inc(core.rows_out, 16)


def program(nc, io):
    with ExitStack() as ctx:
        core = Core(nc, io, ctx)
        weight_streams(core)
        with ExitStack() as norm_ctx:
            core.norm_buffers(norm_ctx)
            setup(core)
            norms(core, None, 0)
        with ExitStack() as nsa:
            cmp = Compressed(core, nsa)
            with ExitStack() as own:
                chunks = core.sb("chunks", [P, 2, 16, 512], F32, own)
                pages = core.sb("chunk_pages", [1, DB * NPAGE], I32, own)
                landed = [core.sig("chunks_in0"), core.sig("chunks_in1")]
                core.window_out = core.lasting("window_out")

                def loads(sp):
                    sp.dma_start(pages[:, :], io["page_table"].rearrange("(o b) n -> o (b n)", o=1)).then_inc(
                        core.sig("chunk_pages_in"), 16)
                    sp.wait_ge(core.sig("chunk_pages_in"), 16)
                    for b in range(DB):
                        for n in range(NPAGE):
                            page = sp.value_load(pages[0:1, b * NPAGE + n:b * NPAGE + n + 1], min_val=0,
                                                 max_val=io["cache_nsa_kv"].shape[1] - 1)
                            p0 = (b % 4) * 32 + n * 8
                            sp.dma_start(chunks[p0:p0 + 8, b // 4, :, :],
                                         io["cache_nsa_kv"][0][bass.ds(page, 1)].rearrange(
                                             "o (c j) s g d -> (o c) j (s g d)", j=16)[:, :, 0:512]).then_inc(
                                landed[b // 4], 16)
                    for b in range(DB):
                        sp.dma_start(io["out_win_s"][0, b, 0:PAST - DS].rearrange("t s g d -> t (s g d)"),
                                     io["state_win_kv"][0, b, DS:PAST].rearrange("t s g d -> t (s g d)")).then_inc(
                            core.window_out, 16)
                compress(core, cmp, [(P, chunks[:, h, :, :], landed[h], 256, 4 * h, 4) for h in range(2)], loads)
            at = Attention(core, nsa)
            token_major(core, 0, at.qkv, roped=(0, 1, 2, 3, 4, 6, 8))
            with ExitStack() as own:
                chunks = core.sb("prompt_chunks", [32, 16, 512], F32, own)

                def loads(sp):
                    write_rows(core, at, sp)
                    sp.wait_ge(core.prompt_rows_out, 16)
                    sp.dma_start(chunks[:, :, :], io["out_nsa_p"][0, 0].rearrange(
                        "(c j) s g d -> c j (s g d)", j=16)[:, :, 0:512]).then_inc(core.sig("prompt_chunks"), 16)
                compress(core, cmp, [(32, chunks[:, :, :], core.sig("prompt_chunks"), 16, DB, 1)], loads)
            with ExitStack() as own:
                kT = core.sb("kT", [DH, 2, KVH, SEQ], F32, own)
                attention_inputs(core, at, kT)
                prompt_attention(core, at, cmp, kT)
            sample_attention(core, at, cmp)
        with ExitStack() as norm_ctx:
            core.norm_buffers(norm_ctx)
            features_to_y(core, 1, (core.hhi, core.hlo), 1)
            norms(core, 1, 2)
            ffn(core, 0, 2)
            norms(core, 3, 4)
        with ExitStack() as own:
            gla = Gla(core, own)
            gla_heads(core, gla, 4)
            token_major(core, 5, gla.vr)
            o = gla.vr[:, :, 0:GH * DV]
            gla_core(core, gla, o)
            gla_finish(core, gla, o)
        with ExitStack() as norm_ctx:
            core.norm_buffers(norm_ctx)
            features_to_y(core, 6, (core.hhi, core.hlo), 1)
            norms(core, 5, 6)
            ffn(core, 1, 7)
            norms(core, 7, None)
            write_y(core)


_INS = ["x_prompt", "x_sample", "cache_nsa_kv", "state_win_kv", "state_gla", "state_ffn_conv", "page_table",
        "norm_gain", "nsa_w_in", "nsa_cmp_pe", "nsa_cmp_w", "nsa_w_o", "gla_w_in", "gla_w_gate_up", "gla_b_gate",
        "gla_norm_gain", "gla_w_o", "ffn_w_up", "ffn_conv_w", "ffn_conv_b", "ffn_w_down"]
_OUTS = [("out_y_p", (1, SEQ, D)), ("out_y_s", (DB, DS, D)), ("out_nsa_p", (1, 1, SEQ, 4, KVH, DH)),
         ("out_nsa_s", (1, DB, DS, 4, KVH, DH)), ("out_win_p", (1, 1, SEQ, 2, KVH, DH)),
         ("out_win_s", (1, DB, PAST, 2, KVH, DH)), ("out_gla_p", (1, 1, GH, DK, DV)),
         ("out_gla_s", (1, DB, GH, DK, DV)), ("out_ffn_p", (2, 1, 2, F)), ("out_ffn_s", (2, DB, 2, F))]


def kernel(**inputs):
    import numpy as _np
    import concourse.bacc as _bacc
    from concourse import mybir as _mybir
    from concourse.bass_utils import run_bass_kernel_spmd as _run

    nc = _bacc.Bacc("TRN2", target_bir_lowering=False, num_devices=1)
    arrays, io = {}, {}
    for name in _INS + ["consts"]:
        a = constants() if name == "consts" else _np.ascontiguousarray(inputs[name])
        arrays[f"in_{name}"] = a
        io[name] = nc.dram_tensor(f"in_{name}", a.shape, _mybir.dt.from_np(a.dtype), kind="ExternalInput").ap()
    for name, shape in _OUTS:
        io[name] = nc.dram_tensor(name, shape, _mybir.dt.from_np(_np.dtype("float32")), kind="ExternalOutput").ap()
    program(nc, io)
    r = _run(nc, [arrays], core_ids=[0])
    return tuple(r.results[0][name] for name, _ in _OUTS)
```

```python
from contextlib import ExitStack, contextmanager

import numpy as np

import concourse.bass as bass
from concourse import mybir

F32 = mybir.dt.float32
F16 = mybir.dt.float16
BF16 = mybir.dt.bfloat16
I32 = mybir.dt.int32
ALU = mybir.AluOpType
ACT = mybir.ActivationFunctionType
AX = mybir.AxisListType

P = 128
D = 1024
KD = D // P
SEQ = 512
DB, DS = 8, 4
SAMP = DB * DS
T = SEQ + SAMP
HALF = T // 2
NT = 5
PAST = 512
PAGE = 128
NPAGE = PAST // PAGE
HEADS, KVH, GRP, DH = 16, 4, 4, 64
KVW = KVH * DH
NBLK = PAST // 16 - 1
PROJ = HEADS * DH + 6 * KVW + 3 * HEADS
QKV = HEADS * DH + 6 * KVW
GH, DK, DV = 4, 128, 256
GPROJ = 2 * GH * DK + 2 * GH * DV + 16
F = 2816
KF = F // P
SCALE = DH ** -0.5
NEG = -1e30
EPS = 1e-6
STAGE_SEMS = 180
SLOTS = 4
SLOTW = 11 * P

C_ID = 0
C_TRIN = C_ID + P
C_TRI1 = C_TRIN + P
C_CMPP = C_TRI1 + P
C_NEW = C_CMPP + 4 * 32
C_WIN = C_NEW + DB * 32
C_CMPS = C_WIN + 4
C_COS = C_CMPS + P
C_SIN = C_COS + NT * 64
C_SEG = C_SIN + NT * 64
C_ATT = C_SEG + T
C_ROW = C_ATT + SAMP
C_SEL = C_ROW + DB
C_COLM = C_SEL + DS * 64
NCONST = C_COLM + DB * SAMP


def constants():
    c = np.zeros((P, NCONST), np.float32)
    r = np.arange(P)
    c[:, C_ID:C_ID + P] = np.eye(P)
    c[:, C_TRIN:C_TRIN + P] = np.where(r[None] <= r[:, None], 0, NEG)
    c[:, C_TRI1:C_TRI1 + P] = r[:, None] <= r[None]
    n = np.arange(32)
    for i in range(4):
        t = i * P + r
        c[:, C_CMPP + i * 32:C_CMPP + i * 32 + 32] = np.where(
            (16 * n[None] + 31 <= t[:, None]) & (n[None] < NBLK), 0, NEG)
    tok, branch, grp = r % DS, r // 64, (r // 16) % KVH
    for b in range(DB):
        c[:, C_NEW + b * 32:C_NEW + b * 32 + 32] = np.where(
            (n[None] // DS == b) & (n[None] % DS <= tok[:, None]), 0, NEG)
    c[:, C_WIN:C_WIN + 4] = np.where((branch[:, None] == 1) & (np.arange(4)[None] < tok[:, None]), NEG, 0)
    c[:, C_CMPS:C_CMPS + P] = np.where((r[None] // 32 == grp[:, None]) & (r[None] % 32 < NBLK), 0, NEG)
    inv = (10000.0 ** (-np.arange(32, dtype=np.float32) / 32).astype(np.float64)).astype(np.float32)
    for i in range(NT):
        pos = (i * P + r if i < 4 else PAST + r % DS).astype(np.float32)
        ang = (pos[:, None] * inv[None]).astype(np.float32)
        co, si = np.cos(ang.astype(np.float64)), np.sin(ang.astype(np.float64))
        c[:, C_COS + i * 64:C_COS + i * 64 + 64] = np.concatenate([co, co], 1)
        c[:, C_SIN + i * 64:C_SIN + i * 64 + 64] = np.concatenate([-si, si], 1)
    seg = np.ones(T)
    seg[0:SEQ:P] = 0
    seg[SEQ::DS] = 0
    c[:, C_SEG:C_SEG + T] = seg
    s = np.arange(SAMP)
    c[:SAMP, C_ATT:C_ATT + SAMP] = (s[:, None] // DS == s[None] // DS) & (s[:, None] <= s[None])
    c[:, C_ROW:C_ROW + DB] = (r[:, None] // DS) == np.arange(DB)[None]
    c[:, C_COLM:] = (s[None] // DS == np.arange(DB)[:, None]).reshape(1, -1)
    row = np.arange(64)
    for t in range(DS):
        c[:HEADS, C_SEL + t * 64:C_SEL + t * 64 + 64] = (r[:HEADS, None] == row[None] // DS) & (row[None] % DS == t)
    return c


def since(count):
    return max(count, 0) if type(count) is int else count


def run(eng, n, body):
    body(0)
    if n > 3:
        with eng.Fori(1, n - 1) as i:
            body(i)
    else:
        for i in range(1, n - 1):
            body(i)
    if n > 1:
        body(n - 1)


class Core:

    def __init__(self, nc, io, ctx):
        self.nc, self.io, self.ctx = nc, io, ctx
        self.signals, self.names = {}, {}
        self.stage_ctx = ExitStack()
        sb = self.sb
        self.const = sb("const", [P, NCONST], F32)
        self.identb = sb("identb", [P, P], BF16)
        self.maskb = sb("maskb", [P, C_COS - C_TRIN], BF16)
        self.ones = sb("ones", [P, P], F32)
        self.gains = sb("gains", [P, KD, 8], F32)
        self.taps = sb("taps", [P, 2, KF, 20], F32)
        self.xT = sb("xT", [P, KD, T], F32)
        self.hhi = sb("hhi", [P, KD, T], F16)
        self.hlo = sb("hlo", [P, KD, T], BF16)
        self.wst = sb("wst", [P, SLOTS, SLOTW], F32)
        self.whi = sb("whi", [P, SLOTS, SLOTW], F16)
        self.wlo = sb("wlo", [P, SLOTS, SLOTW], BF16)
        self.ps = ctx.enter_context(nc.psum_tensor("ps", [P, 8, 512], F32))
        self.ident = self.const[:, C_ID:C_ID + P]
        self.stream = []
        self.w_landed = [self.lasting(f"w_landed{k}") for k in range(SLOTS)]
        self.w_hi = self.lasting("w_hi_ready")
        self.w_lo = self.lasting("w_lo_ready")
        self.w_used = self.lasting("w_used")

    def sb(self, name, shape, dt, ctx=None):
        n = self.names[name] = self.names.get(name, 0) + 1
        return (ctx or self.ctx).enter_context(self.nc.sbuf_tensor(f"{name}_{n}" if n > 1 else name, shape, dt))

    def norm_buffers(self, ctx):
        self.yT = self.sb("yT", [P, KD, T], F32, ctx)
        self.ssq = self.sb("ssq", [P, T], F32, ctx)
        self.rstd = self.sb("rstd", [P, 2, T], F32, ctx)
        self.sq = self.sb("sq", [P, 2, T], F32, ctx)
        self.tmp = self.sb("tmp", [P, 2, T], F32, ctx)

    def lasting(self, name):
        return self.ctx.enter_context(self.nc.semaphore(name))

    def sig(self, name):
        if name not in self.signals:
            self.signals[name] = self.stage_ctx.enter_context(
                self.nc.semaphore(name, num=STAGE_SEMS + len(self.signals)))
        return self.signals[name]

    @contextmanager
    def stage(self):
        with self.nc.Block() as block:
            yield block
        self.nc.all_engine_barrier(sems_to_clear=range(STAGE_SEMS, STAGE_SEMS + len(self.signals)))
        self.stage_ctx.close()
        self.signals.clear()



def load_block(core, sp, seg, i, k, first):
    n_blocks, width, source = core.stream[seg]
    n = i * 4 + k
    sp.wait_ge(core.w_hi, since(first + n - SLOTS + 1))
    sp.wait_ge(core.w_lo, since(first + n - SLOTS + 1))
    src = source(i, k)
    dst = core.wst[:, k, 0:width].rearrange("p (a c) -> p a c", a=src.shape[1])
    sp.dma_start(dst, src).then_inc(core.w_landed[k], 16)


def load_stage(core, sp, seg, first):
    n_blocks = core.stream[seg][0]
    if n_blocks // 4 > 3:
        with sp.Fori(2, n_blocks // 4) as i:
            for k in range(4):
                load_block(core, sp, seg, i, k, first)
    else:
        for i in range(2, n_blocks // 4):
            for k in range(4):
                load_block(core, sp, seg, i, k, first)
    if seg + 1 < len(core.stream):
        for i in range(2):
            for k in range(4):
                load_block(core, sp, seg + 1, i, k, first + n_blocks)


def cast_width(core, seg, i):
    n_blocks, width, _ = core.stream[seg]
    if type(i) is int and i == n_blocks // 4 - 1:
        return core.stream[seg + 1][1] if seg + 1 < len(core.stream) else 0
    return width


def cast_hi(core, act, seg, i, k, first):
    w = cast_width(core, seg, i)
    if not w:
        return
    n = first + (i + 1) * 4 + k
    act.wait_ge(core.w_used, since(n - SLOTS + 1))
    act.wait_ge(core.w_landed[k], (n - k) * 4 + 16)
    act.copy(core.whi[:, k, 0:w], core.wst[:, k, 0:w]).then_inc(core.w_hi, 1)


def cast_lo(core, pool, seg, i, k, first):
    w = cast_width(core, seg, i)
    if not w:
        return
    n = first + (i + 1) * 4 + k
    pool.wait_ge(core.w_used, since(n - SLOTS + 1))
    pool.wait_ge(core.w_hi, n + 1)
    pool.tensor_tensor(core.wlo[:, k, 0:w], core.wst[:, k, 0:w], core.whi[:, k, 0:w], ALU.subtract).then_inc(core.w_lo, 1)


def weights_ready(core, pe, n):
    pe.wait_ge(core.w_hi, n + 1)
    pe.wait_ge(core.w_lo, n + 1)


def product(pe, out, parts, lhs, rhs, start, stop):
    n = len(parts)
    for j, (ka, kb) in enumerate(parts):
        a_hi, a_lo = lhs(ka)
        b_hi, b_lo = rhs(kb)
        pe.matmul(out, a_hi, b_hi, start=start and j == 0, stop=False)
        pe.matmul(out, a_hi, b_lo, start=False, stop=False)
        last = pe.matmul(out, a_lo, b_hi, start=False, stop=stop and j == n - 1)
    return last


def weight_streams(core):
    io = core.io

    def tokens_major(w, col0):
        def source(i, k):
            return w[(k % 2) * 512:(k % 2) * 512 + 512, bass.ds((i * 2 + k // 2) * 256 + col0, 256)].rearrange(
                "(a p) c -> p a c", p=P)
        return source

    def features(w, col0=0):
        def source(i, k):
            return w[:, bass.ds((i * 4 + k) * P + col0, P)].rearrange("(a p) c -> p a c", p=P)
        return source

    def up(w):
        def source(i, k):
            return w[:, bass.ds((i * 2 + k // 2) * P + (k % 2) * F, P)].rearrange("(a p) c -> p a c", p=P)
        return source

    def down(w):
        def source(i, k):
            r0 = (k % 2) * (F // 2)
            return w[r0:r0 + F // 2, bass.ds((i * 2 + k // 2) * P, P)].rearrange("(a p) c -> p a c", p=P)
        return source

    ffn = [[(2 * KF, 8 * P, up(io["ffn_w_up"][l])), (2 * KD, SLOTW, down(io["ffn_w_down"][l]))] for l in range(2)]
    core.stream = [
        (QKV // P, 8 * P, tokens_major(io["nsa_w_in"][0], 0)),
        (KD, 8 * P, features(io["nsa_w_o"][0])), *ffn[0],
        (2 * GH * DK // P, 8 * P, features(io["gla_w_in"][0])),
        (2 * GH * DV // P, 8 * P, tokens_major(io["gla_w_in"][0], 2 * GH * DK)),
        (KD, 8 * P, features(io["gla_w_o"][0])), *ffn[1]]
    core.starts = [sum(s[0] for s in core.stream[:n]) for n in range(len(core.stream))]



def setup(core):
    nc, io = core.nc, core.io
    ps = core.ps
    with ExitStack() as own:
        xtok = core.sb("xtok", [P, NT, D], F32, own)
        rows = core.sb("rows", [20, 2, F], F32, own)
        grow = core.sb("grow", [8, D], F32, own)
        const_in, x_in, gains_in, rows_in = (core.sig(n) for n in ("const_in", "x_in", "gains_in", "rows_in"))
        turned, turned_small, taken, taken_small, filled = (
            core.sig(n) for n in ("x_turned", "small_turned", "x_taken", "small_taken", "constants_filled"))

        with core.stage() as block:
            @block.sync
            def _(sp):
                sp.dma_start(core.const[:, :], io["consts"]).then_inc(const_in, 16)
                for i in range(4):
                    sp.dma_start(xtok[:, i, :], io["x_prompt"][0, i * P:(i + 1) * P, :]).then_inc(x_in, 16)
                sp.dma_start(xtok[0:SAMP, 4, :], io["x_sample"].rearrange("b t d -> (b t) d")).then_inc(x_in, 16)
                sp.dma_start(grow[:, :], io["norm_gain"].rearrange("l n d -> (l n) d")).then_inc(gains_in, 16)
                for k in range(4):
                    load_block(core, sp, 0, 0, k, 0)
                for l in range(2):
                    sp.dma_start(rows[0:3, l, :], io["ffn_conv_w"][l]).then_inc(rows_in, 16)
                    sp.dma_start(rows[3:4, l, :], io["ffn_conv_b"][l:l + 1]).then_inc(rows_in, 16)
                    sp.dma_start(rows[4:20, l, :], io["state_ffn_conv"][l].rearrange("b j f -> (b j) f")
                                 ).then_inc(rows_in, 16)
                for k in range(4):
                    load_block(core, sp, 0, 1, k, 0)

            @block.tensor
            def _(pe):
                pe.wait_ge(const_in, 16)
                pe.wait_ge(x_in, 80)
                for k in range(KD):
                    b = (k % 2) * 2
                    pe.wait_ge(taken, since(k - 1))
                    pe.wait_ge(taken_small, since(k - 1))
                    for i in range(4):
                        last = pe.transpose(ps[:, b, i * P:(i + 1) * P], xtok[:, i, k * P:(k + 1) * P], core.ident)
                    last.then_inc(turned, 1)
                    pe.transpose(ps[:, b + 1, 0:SAMP], xtok[0:SAMP, 4, k * P:(k + 1) * P],
                                 core.ident[0:SAMP, 0:SAMP]).then_inc(turned_small, 1)
                pe.wait_ge(gains_in, 16)
                for k in range(KD):
                    last = pe.transpose(ps[:, 4, k * 8:k * 8 + 8], grow[:, k * P:(k + 1) * P], core.ident[0:8, 0:8])
                last.then_inc(turned_small, 1)
                pe.wait_ge(rows_in, 96)
                for l in range(2):
                    for m in range(KF):
                        last = pe.transpose(ps[:, 5 + l, m * 20:m * 20 + 20], rows[:, l, m * P:(m + 1) * P],
                                            core.ident[0:20, 0:20])
                    last.then_inc(turned_small, 1)

            @block.scalar
            def _(act):
                for k in range(KD):
                    act.wait_ge(turned, k + 1)
                    act.copy(core.xT[:, k, 0:SEQ], ps[:, (k % 2) * 2, :]).then_inc(taken, 1)
                    if k % 2:
                        cast_hi(core, act, 0, -1, k // 2, 0)

            @block.vector
            def _(dve):
                dve.memset(core.ones[:, :], 1.0).then_inc(filled, 1)
                dve.wait_ge(const_in, 16)
                dve.tensor_copy(core.identb[:, :], core.ident).then_inc(filled, 1)
                dve.tensor_copy(core.maskb[:, :], core.const[:, C_TRIN:C_COS]).then_inc(filled, 1)
                for k in range(KD):
                    dve.wait_ge(turned_small, k + 1)
                    dve.tensor_copy(core.xT[:, k, SEQ:T], ps[:, (k % 2) * 2 + 1, 0:SAMP]).then_inc(taken_small, 1)
                dve.wait_ge(turned_small, KD + 1)
                dve.tensor_copy(core.gains[:, :, :], ps[:, 4, 0:KD * 8].rearrange("p (k g) -> p k g", g=8)).then_inc(taken_small, 1)
                for l in range(2):
                    dve.wait_ge(turned_small, KD + 2 + l)
                    dve.tensor_copy(core.taps[:, l, :, :], ps[:, 5 + l, 0:KF * 20].rearrange(
                    "p (m r) -> p m r", r=20)).then_inc(taken_small, 1)

            @block.gpsimd
            def _(pool):
                for k in range(4):
                    cast_lo(core, pool, 0, -1, k, 0)



def norms(core, post, pre):
    nc, ps = core.nc, core.ps
    xT, yT, sq, tmp, rstd = core.xT, core.yT, core.sq, core.tmp, core.rstd
    summed, var, root, inverse = (core.sig(n) for n in ("squares_summed", "variance", "deviation", "rstd_ready"))
    scaled, x_ready, sq_ready, sq_used, h32, h_hi, h_lo = (
        core.sig(n) for n in ("y_scaled", "x_ready", "square_ready", "square_used", "h_ready", "h_hi", "h_lo"))
    n_post, n_pre = post is not None, pre is not None
    with core.stage() as block:
        @block.tensor
        def _(pe):
            if n_post:
                for h in range(2):
                    last = pe.matmul(ps[:, h, 0:HALF], core.ones[:, :], core.ssq[:, h * HALF:(h + 1) * HALF],
                                     start=True, stop=True)
                last.then_inc(summed, 1)
            if n_pre:
                for k in range(KD):
                    pe.wait_ge(sq_ready, k + 1)
                    for h in range(2):
                        last = pe.matmul(ps[:, 2 + h, 0:HALF], core.ones[:, :],
                                         sq[:, k % 2, h * HALF:(h + 1) * HALF], start=(k == 0), stop=(k == KD - 1))
                    last.then_inc(sq_used, 1)

        @block.vector
        def _(dve):
            def variance(bank, slot, n):
                dve.tensor_scalar(rstd[:, slot, :].rearrange("p (h c) -> p h c", h=2),
                                  ps[:, bank:bank + 2, 0:HALF], 1.0 / D, EPS, ALU.mult, ALU.add).then_inc(var, 1)
                dve.wait_ge(root, n)
                dve.reciprocal(rstd[:, slot, :], rstd[:, slot, :]).then_inc(inverse, 1)
                dve.wait_ge(inverse, n)
            if n_post:
                dve.wait_ge(summed, 1)
                variance(0, 0, 1)
                for k in range(KD):
                    dve.wait_ge(x_ready, since(k - 1))
                    dve.tensor_tensor(tmp[:, k % 2, :], yT[:, k, :], rstd[:, 0, :], ALU.mult).then_inc(scaled, 1)
                    if k:
                        dve.wait_ge(scaled, k)
                        dve.scalar_tensor_tensor(xT[:, k - 1, :], tmp[:, (k - 1) % 2, :],
                                                 core.gains[:, k - 1, post:post + 1], xT[:, k - 1, :],
                                                 ALU.mult, ALU.add).then_inc(x_ready, 1)
                dve.wait_ge(scaled, KD)
                dve.scalar_tensor_tensor(xT[:, KD - 1, :], tmp[:, (KD - 1) % 2, :],
                                         core.gains[:, KD - 1, post:post + 1], xT[:, KD - 1, :],
                                         ALU.mult, ALU.add).then_inc(x_ready, 1)
                dve.wait_ge(x_ready, KD)
            if n_pre:
                dve.wait_ge(sq_used, KD)
                variance(2, 1, n_post + 1)
                for k in range(KD):
                    if k >= 2:
                        dve.wait_ge(h_hi, since(k - 1))
                        if k % 2 == 0:
                            dve.wait_ge(h_lo, k // 2)
                    dve.scalar_tensor_tensor(tmp[:, k % 2, :], xT[:, k, :], core.gains[:, k, pre:pre + 1],
                                             rstd[:, 1, :], ALU.mult, ALU.mult).then_inc(h32, 1)
                    if k % 2:
                        dve.wait_ge(h_hi, k + 1)
                        dve.tensor_tensor(core.hlo[:, k, :], tmp[:, 1, :], core.hhi[:, k, :], ALU.subtract).then_inc(core.sig("h_lo_odd"), 1)
                        dve.wait_ge(core.sig("h_lo_odd"), k // 2 + 1)

        @block.scalar
        def _(act):
            if n_post:
                act.wait_ge(var, 1)
                act.activation(rstd[:, 0, :], rstd[:, 0, :], ACT.Sqrt).then_inc(root, 1)
            if n_pre:
                for k in range(KD):
                    if n_post:
                        act.wait_ge(x_ready, k + 1)
                    act.wait_ge(sq_used, since(k - 1))
                    act.activation(sq[:, k % 2, :], xT[:, k, :], ACT.Square).then_inc(sq_ready, 1)
                act.wait_ge(var, n_post + 1)
                act.activation(rstd[:, 1, :], rstd[:, 1, :], ACT.Sqrt).then_inc(root, 1)
                for k in range(KD):
                    act.wait_ge(h32, k + 1)
                    act.copy(core.hhi[:, k, :], tmp[:, k % 2, :]).then_inc(h_hi, 1)

        @block.gpsimd
        def _(pool):
            if n_pre:
                for k in range(0, KD, 2):
                    pool.wait_ge(h_hi, k + 1)
                    pool.tensor_tensor(core.hlo[:, k, :], tmp[:, 0, :], core.hhi[:, k, :], ALU.subtract).then_inc(h_lo, 1)



def token_major(core, seg, dest, roped=None):
    nc, ps = core.nc, core.ps
    first = core.starts[seg]
    groups = core.stream[seg][0] // 2
    ready, taken, rot, t_ready = (core.sig(n) for n in ("rows_ready", "rows_taken", "rotated", "swapped"))
    cleared = core.sig("rows_cleared")
    h = lambda k, i: (core.hhi[:, k, i * P:min(i * P + P, T)], core.hlo[:, k, i * P:min(i * P + P, T)])

    with ExitStack() as own:
        swap = core.sb("swap", [P, NT, 256], F32, own) if roped else None
        with core.stage() as block:
            @block.sync
            def _(sp):
                load_stage(core, sp, seg, first)

            @block.tensor
            def _(pe):
                def body(i):
                    for g in range(2):
                        for k in (2 * g, 2 * g + 1):
                            weights_ready(core, pe, first + 4 * i + k)
                        pe.wait_ge(taken, since((2 * i + g) * 3 - 3))
                        for t in range(NT):
                            rows = P if t < 4 else SAMP
                            out = ps[0:rows, g * 3 + t // 2, (t % 2) * 256:(t % 2) * 256 + 256]
                            last = product(
                                pe, out, [(k, k) for k in range(KD)], lambda k: h(k, t),
                                lambda k: (block_hi(core, 2 * g + k // 4, 256)[:, k % 4, :],
                                           block_lo(core, 2 * g + k // 4, 256)[:, k % 4, :]), True, True)
                            if t in (1, 3):
                                last.then_inc(ready, 1)
                            if t == 4:
                                last.then_inc(core.w_used, 2)
                run(pe, groups // 2, body)

            @block.scalar
            def _(act):
                def body(i):
                    for g in range(2):
                        n = 2 * i + g
                        col = n * 256
                        for t in range(3):
                            tiles = 2 if t < 2 else 1
                            rows = P if t < 2 else SAMP
                            if t < 2:
                                act.wait_ge(ready, n * 2 + t + 1)
                            else:
                                act.wait_ge(core.w_used, first + 2 * n + 2)
                            act.copy(dest[0:rows, 2 * t:2 * t + tiles, bass.ds(col, 256)],
                                     ps[0:rows, g * 3 + t, 0:256 * tiles].rearrange("p (a c) -> p a c", c=256)).then_inc(taken, 1)
                        for k in (2 * g, 2 * g + 1):
                            cast_hi(core, act, seg, i, k, first)
                act.wait_ge(cleared, 1)
                run(act, groups // 2, body)

            @block.gpsimd
            def _(pool):
                def body(i):
                    for k in range(4):
                        cast_lo(core, pool, seg, i, k, first)
                run(pool, groups // 2, body)

            @block.vector
            def _(dve):
                if not roped:
                    dve.memset(dest[:, 4, :], 0.0).then_inc(cleared, 1)
                else:
                    cos = core.const[:, C_COS:C_SIN].rearrange("p (i d) -> p i d", i=NT)
                    sin = core.const[:, C_SIN:C_SEG].rearrange("p (i d) -> p i d", i=NT)
                    done = 0
                    dve.memset(dest[:, 4, :], 0.0).then_inc(cleared, 1)

                    def rotate(n, count):
                        dve.wait_ge(taken, n * 3 + 3)
                        x = dest[:, :, n * 256:n * 256 + 256]
                        x4 = x.rearrange("p i (h d) -> p i h d", d=DH)
                        s4 = swap[:, :, :].rearrange("p i (h d) -> p i h d", d=DH)
                        sn = sin.unsqueeze(2).broadcast_to([P, NT, 4, 64])
                        cs = cos.unsqueeze(2).broadcast_to([P, NT, 4, 64])
                        dve.wait_ge(rot, since(count))
                        dve.tensor_tensor(s4[:, :, :, 0:32], x4[:, :, :, 32:64], sn[:, :, :, 0:32], ALU.mult)
                        dve.tensor_tensor(s4[:, :, :, 32:64], x4[:, :, :, 0:32], sn[:, :, :, 32:64], ALU.mult).then_inc(t_ready, 1)
                        dve.wait_ge(t_ready, 2 * count + 1)
                        dve.tensor_tensor(x4, x4, cs, ALU.mult).then_inc(t_ready, 1)
                        dve.wait_ge(t_ready, 2 * count + 2)
                        dve.tensor_tensor(x, x, swap[:, :, :], ALU.add).then_inc(rot, 1)
                    for n in roped:
                        rotate(n, done)
                        done += 1


def block_hi(core, k, cols):
    return core.whi[:, k, 0:1024].rearrange("p (a c) -> p a c", c=cols)


def block_lo(core, k, cols):
    return core.wlo[:, k, 0:1024].rearrange("p (a c) -> p a c", c=cols)



class Compressed:

    def __init__(self, core, ctx):
        self.kcT = core.sb("kcT", [DH, DB + 1, P], F32, ctx)
        self.vcT = core.sb("vcT", [DH, DB + 1, P], F32, ctx)


def compress(core, cmp, units, loads):
    nc, ps = core.nc, core.ps
    turned, moved, summed, shifted, combined, biased = (core.sig(n) for n in (
        "taps_turned", "taps_moved", "chunks_summed", "second_shifted", "blocks_combined", "pe_projected"))
    moved_act = core.sig("taps_moved_act")
    w_in, cleared = core.sig("cmp_w_in"), core.sig("cmp_cleared")
    n_q = len(units) * 16
    with ExitStack() as own:
        pairs = core.sb("tap_pairs", [P, 2, 4 * units[0][0]], F32, own)
        second = core.sb("second_half", [DH, 2, 4 * units[0][0]], F32, own)
        bias2 = core.sb("bias_second", [DH, 2], F32, own)
        weight = core.sb("cmp_w", [P, 2, 8, 2, DH], F32, own)
        taps_pe = core.sb("cmp_pe", [P, 2, 2, 8], F32, own)
        bias = core.sb("cmp_bias", [DH, 2], F32, own)
        def move(eng, copy, q, j, signal):
            n = units[q // 16][0]
            eng.wait_ge(turned, q + 1)
            eng.wait_ge(summed, since(q - 1))
            for par in range(2):
                dst = pairs[j * DH:(j + 1) * DH, q % 2, 0:4 * n].rearrange("p (u a n) -> p u a n", u=2, a=2)[:, :, par]
                src = ps[par * DH:(par + 1) * DH, (q % 2) * 2 + j, 0:2 * n].rearrange("p (u n) -> p u n", u=2)
                copy(dst, src).then_inc(signal, 1)

        with core.stage() as block:
            @block.sync
            def _(sp):
                w = core.io["nsa_cmp_w"][0]
                for kv in range(2):
                    for h in range(2):
                        sp.dma_start(weight[:, kv, :, h, :], w[kv, h * 16:h * 16 + 16].rearrange(
                            "(a j) d e -> (j d) a e", j=2)).then_inc(w_in, 16)
                    sp.dma_start(taps_pe[:, kv, :, :], core.io["nsa_cmp_pe"][0, kv].rearrange(
                        "(c a j) d -> (j d) c a", c=2, j=2), allow_slow_non_contiguous=True).then_inc(w_in, 16)
                loads(sp)

            @block.tensor
            def _(pe):
                pe.wait_ge(w_in, 96)
                for kv in range(2):
                    for a in range(8):
                        last = pe.matmul(ps[:, 6, kv * 2:kv * 2 + 2],
                                         weight[:, kv, a, :, :].rearrange("p h e -> p (h e)"),
                                         taps_pe[:, kv, :, a], start=(a == 0), stop=(a == 7))
                last.then_inc(biased, 1)

                def turn(q):
                    n, x, landed, value, _, _ = units[q // 16]
                    kv, a = q // 8 % 2, q % 8
                    if q % 16 == 0:
                        pe.wait_ge(landed, value)
                    pe.wait_ge(moved, since(2 * (q - 1)))
                    pe.wait_ge(moved_act, since(2 * (q - 1)))
                    for j in range(2):
                        for u in range(2):
                            c = kv * KVW + u * P
                            last = pe.transpose(ps[:, (q % 2) * 2 + j, u * n:(u + 1) * n],
                                                x[0:n, 2 * a + j, c:c + P], core.ident[0:n, 0:n])
                    last.then_inc(turned, 1)
                turn(0)
                for q in range(n_q):
                    if q + 1 < n_q:
                        turn(q + 1)
                    n = units[q // 16][0]
                    kv, a, s = q // 8 % 2, q % 8, q // 8
                    if a == 0:
                        pe.wait_ge(combined, since(4 * (s - 1)))
                    pe.wait_ge(moved, 2 * q + 2)
                    pe.wait_ge(moved_act, 2 * q + 2)
                    pe.matmul(ps[:, 4 + s % 2, 0:4 * n], weight[:, kv, a, :, :].rearrange("p h e -> p (h e)"),
                              pairs[:, q % 2, 0:4 * n], start=(a == 0), stop=(a == 7)).then_inc(summed, 1)

            @block.scalar
            def _(act):
                act.wait_ge(biased, 1)
                act.copy(bias2[:, :], ps[DH:P, 6, 1:4:2]).then_inc(shifted, 1)

                def shift(s):
                    n = units[s // 2][0]
                    act.wait_ge(summed, 8 * s + 8)
                    act.wait_ge(combined, since(4 * (s - 1)))
                    act.copy(second[:, s % 2, 0:4 * n], ps[DH:P, 4 + s % 2, 0:4 * n]).then_inc(shifted, 1)
                for q in range(n_q):
                    move(act, act.copy, q, 0, moved_act)
                    if q % 8 == 7 and q > 8:
                        shift(q // 8 - 1)
                shift(n_q // 8 - 1)

            @block.vector
            def _(dve):
                b0 = units[0][4]
                for x in (cmp.kcT, cmp.vcT):
                    dve.memset(x[:, b0:b0 + sum(u[5] for u in units), :], 0.0).then_inc(cleared, 1)
                dve.wait_ge(shifted, 1)
                dve.tensor_tensor(bias[:, :], ps[0:DH, 6, 0:4:2], bias2[:, :], ALU.add).then_inc(cleared, 1)
                dve.wait_ge(cleared, 3)

                def combine(s):
                    n, _, _, _, b0, nb = units[s // 2]
                    kv = s % 2
                    dest = cmp.vcT if kv else cmp.kcT
                    dve.wait_ge(shifted, s + 2)
                    for g in range(KVH):
                        one = ps[0:DH, 4 + s % 2, g * n:(g + 1) * n].rearrange("p (b c) -> p b c", c=32)
                        two = second[:, s % 2, g * n:(g + 1) * n].rearrange("p (b c) -> p b c", c=32)
                        dve.scalar_tensor_tensor(
                        dest[:, b0:b0 + nb, g * 32:g * 32 + NBLK], one[:, :, 0:NBLK], bias[:, kv:kv + 1],
                        two[:, :, 1:NBLK + 1], ALU.add, ALU.add).then_inc(combined, 1)
                for q in range(n_q):
                    move(dve, dve.tensor_copy, q, 1, moved)
                    if q % 8 == 7 and q > 8:
                        combine(q // 8 - 1)
                combine(n_q // 8 - 1)



class Attention:
    def __init__(self, core, ctx):
        self.qkv = core.sb("qkv", [P, NT, QKV], F32, ctx)
        self.gates = core.sb("gates", [P, NT, 48], F32, ctx)
        self.qs = core.sb("q_sample", [DH, DB, 64], F32, ctx)
        self.qblk = core.sb("q_blocks", [P, DB, 2, 64], F32, ctx)
        self.gate_rows = core.sb("gate_rows", [P, DB, 2], F32, ctx)
        self.kTn = core.sb("new_keys", [P, 2, 2, SAMP], F32, ctx)

KS, VS, KW, VW = 1536, 1792, 2048, 2304


def attention_inputs(core, at, kk):
    nc, ps, io = core.nc, core.ps, core.io
    gw_cast, gates_summed, gates_done = core.sig("gate_w_cast"), core.sig("gates_summed"), core.sig("gates_done")
    keys_turned, keys_hi, keys_lo = core.sig("keys_turned"), core.sig("keys_hi"), core.sig("keys_lo")
    q_turned, q_moved, zeroed, g_turned, g_moved = (
        core.sig(n) for n in ("qs_turned", "qs_moved", "qblk_zeroed", "gates_turned", "gates_moved"))
    with ExitStack() as own:
        gT = core.sb("gates_turned", [HEADS, 3, SAMP], F32, own)
        gs = core.sb("gates_contig", [SAMP, 3, HEADS], F32, own)
        gw = core.sb("gate_w", [P, KD, 48], F32, own)
        gwhi, gwlo = core.sb("gate_w_hi", [P, KD, 48], F16, own), core.sb("gate_w_lo", [P, KD, 48], BF16, own)
        with core.stage() as block:
            @block.sync
            def _(sp):
                sp.dma_start(gw[:, :, :], io["nsa_w_in"][0][:, QKV:PROJ].rearrange("(k p) c -> p k c", p=P)
                             ).then_inc(core.sig("gate_w_in"), 16)

            @block.tensor
            def _(pe):
                for n in range(8):
                    y, g = n // 4, n % 4
                    col = (KS, KW)[y] + g * DH
                    pe.wait_ge(keys_lo, since(n - 3))
                    for i in range(4):
                        last = pe.transpose(ps[0:DH, n % 4, i * P:(i + 1) * P], at.qkv[:, i, col:col + DH], core.ident)
                    last.then_inc(keys_turned, 1)
                pe.wait_ge(gw_cast, 2)
                for t in range(NT):
                    rows = P if t < 4 else SAMP
                    last = product(pe, ps[0:rows, 4, t * 48:t * 48 + 48], [(k, k) for k in range(KD)],
                                   lambda k: (core.hhi[:, k, t * P:t * P + rows], core.hlo[:, k, t * P:t * P + rows]),
                                   lambda k: (gwhi[:, k, :], gwlo[:, k, :]), True, True)
                last.then_inc(gates_summed, 1)
                for h in range(HEADS):
                    last = pe.transpose(ps[0:DH, 5, h * SAMP:(h + 1) * SAMP],
                                        at.qkv[0:SAMP, 4, h * DH:(h + 1) * DH], core.ident[0:SAMP, 0:SAMP])
                last.then_inc(q_turned, 1)
                for y in range(2):
                    for u in range(2):
                        col = (KS, KW)[y] + u * P
                        last = pe.transpose(ps[:, 6, (y * 2 + u) * SAMP:(y * 2 + u + 1) * SAMP],
                                            at.qkv[0:SAMP, 4, col:col + P], core.ident[0:SAMP, 0:SAMP])
                last.then_inc(q_turned, 1)
                pe.wait_ge(gates_done, 4)
                for c in range(3):
                    last = pe.transpose(ps[0:HEADS, 7, c * SAMP:(c + 1) * SAMP], gs[:, c, :],
                                        core.ident[0:SAMP, 0:SAMP])
                last.then_inc(g_turned, 1)
                pe.wait_ge(g_moved, 1)
                for c in range(3):
                    for t in range(DS):
                        rows = slice(64, P) if c == 2 else slice(0, 64)
                        col = 128 + (8 if c == 0 else 0)
                        last = pe.matmul(ps[rows, 7, col:col + DB],
                                         core.const[0:HEADS, C_SEL + t * 64:C_SEL + t * 64 + 64],
                                         gT[:, c, :].rearrange("p (b t) -> p b t", t=DS)[:, :, t],
                                         start=(t == 0), stop=(t == DS - 1))
                last.then_inc(g_turned, 1)

            @block.scalar
            def _(act):
                act.wait_ge(core.sig("gate_w_in"), 16)
                act.wait_ge(zeroed, 1)
                act.copy(gwhi[:, :, :], gw[:, :, :]).then_inc(gw_cast, 1)
                for n in range(8):
                    act.wait_ge(keys_turned, n + 1)
                    act.copy(kk[0:DH, n // 4, n % 4, :], ps[0:DH, n % 4, :]).then_inc(keys_hi, 1)
                act.wait_ge(gates_summed, 1)
                act.activation(at.gates[:, 0:4, :], ps[:, 4, 0:192].rearrange("p (t c) -> p t c", c=48),
                               ACT.Exp, scale=-1.0).then_inc(gates_done, 1)
                act.activation(at.gates[0:SAMP, 4, :], ps[0:SAMP, 4, 192:240], ACT.Exp, scale=-1.0).then_inc(gates_done, 1)

            @block.vector
            def _(dve):
                dve.memset(at.gates[:, 4, :], 0.0).then_inc(zeroed, 1)
                dve.memset(at.gate_rows[:, :, :], 0.0).then_inc(zeroed, 1)
                dve.memset(at.qblk[:, :, :, :], 0.0).then_inc(zeroed, 1)
                dve.wait_ge(gw_cast, 1)
                dve.tensor_tensor(gwlo[:, :, :], gw[:, :, :], gwhi[:, :, :], ALU.subtract).then_inc(gw_cast, 1)
                for n in range(8):
                    dve.wait_ge(keys_hi, n + 1)
                    dve.tensor_tensor(kk[DH:P, n // 4, n % 4, :], ps[0:DH, n % 4, :], kk[0:DH, n // 4, n % 4, :],
                                      ALU.subtract).then_inc(keys_lo, 1)
                dve.wait_ge(q_turned, 1)
                dve.tensor_copy(at.qs[:, :, :].rearrange("p b (h t) -> p h b t", t=DS),
                                ps[0:DH, 5, :].rearrange("p (h b t) -> p h b t", h=HEADS, b=DB)).then_inc(q_moved, 1)
                dve.wait_ge(q_turned, 2)
                dve.tensor_copy(at.kTn[:, :, :, :], ps[:, 6, 0:4 * SAMP].rearrange(
                "p (y u c) -> p y u c", y=2, u=2)).then_inc(q_moved, 1)
                dve.wait_ge(q_moved, 1)
                dve.wait_ge(zeroed, 3)
                for g in range(KVH):
                    p0 = (g % 2) * DH
                    dve.tensor_copy(at.qblk[p0:p0 + DH, :, g // 2, g * 16:g * 16 + 16],
                                    at.qs[:, :, g * 16:g * 16 + 16]).then_inc(q_moved, 1)
                dve.wait_ge(gates_done, 2)
                dve.tensor_scalar(at.gates[:, :, :], at.gates[:, :, :], 1.0, None, ALU.add).then_inc(gates_done, 1)
                dve.wait_ge(gates_done, 3)
                dve.reciprocal(at.gates[:, :, :], at.gates[:, :, :]).then_inc(q_moved, 1)
                dve.wait_ge(q_moved, 7)
                dve.tensor_copy(gs[:, :, :], at.gates[0:SAMP, 4, :].rearrange("p (h c) -> p c h", c=3)).then_inc(gates_done, 1)
                dve.wait_ge(g_turned, 1)
                dve.tensor_copy(gT[:, :, :], ps[0:HEADS, 7, 0:3 * SAMP].rearrange("p (c n) -> p c n", c=3)).then_inc(g_moved, 1)
                dve.wait_ge(g_turned, 2)
                dve.tensor_copy(at.gate_rows[:, :, 0], ps[:, 7, 128:128 + DB]).then_inc(g_moved, 1)
                dve.tensor_copy(at.gate_rows[0:64, :, 1], ps[0:64, 7, 136:136 + DB]).then_inc(g_moved, 1)



def prompt_attention(core, at, cmp, kk):
    nc, ps = core.nc, core.ps
    names = ("q_staged", "v_staged", "kc_hi", "kc_lo", "vc_staged", "qT_turned", "q_hi", "q_lo", "vc_turned",
             "vc_by_tile", "cmp_scored", "cmp_step", "cmp_recip", "exp_cmp", "cmp_turned", "cmp_moved", "cmp_out",
             "out_set", "scored", "maxed", "shifts_ready", "keys_scored", "exp_done", "attended", "coef_step",
             "parts_taken", "parts_added", "out_turned", "out_hi", "out_lo", "tables_set")
    (q_staged, v_staged, kc_hi, kc_lo, vc_staged, qT_turned, q_hi, q_lo, vc_turned, vc_by_tile, cmp_scored, cmp_step,
     cmp_recip, exp_cmp, cmp_turned, cmp_moved, cmp_out, out_set, scored, maxed, shifts_ready, keys_scored, exp_done,
     attended, coef_step, parts_taken, parts_added, out_turned, out_hi, out_lo, tables_set) = (
        core.sig(n) for n in names)
    trin = core.maskb[:, 0:P]
    cmpp = core.maskb[:, C_CMPP - C_TRIN:C_NEW - C_TRIN]
    U = 16
    VD = DH + 1
    MAXB = (4, 7)
    OUTB = 5
    first = lambda g: type(g) is int and g == 0
    with ExitStack() as own:
        sb = lambda n, s, t=F32: core.sb(n, s, t, own)
        qd = at.qkv[:, 0:4, 1024:1024 + SEQ]
        vg = sb("v_group", [P, 4, 2, VD])
        qh, ql = sb("q_heads", [P, 4, SEQ], F16), sb("q_rests", [P, 4, SEQ], BF16)
        kcc, vcx, vcz = sb("kc_split", [P, 32], F16), sb("vc_repeated", [DH, 4, 32]), sb("vc_by_tile", [P, 4, DH])
        mc, sc = sb("max_cmp", [P, U]), sb("sum_cmp", [P, U])
        onesb, nident = sb("ones_bf16", [P, P], BF16), sb("neg_ident", [P, P], BF16)
        mx, shift = sb("row_max", [P, 2, 2, 4]), sb("shifts", [P, 2, 2, SEQ], BF16)
        pT = sb("prob_T", [P, 2, 4, SEQ])
        coef = sb("coef", [P, 2, 4])
        part = at.qkv[:, 0:4, KS:VS].rearrange("p i (u y d) -> p u y i d", u=2, y=2)
        shared = sb("cmp_then_out", [P, 4, 256])
        pc = shared[:, 0:2, :].rearrange("p a (u n) -> p (a u) n", n=32)
        pcT = shared[:, 2:4, :].rearrange("p a (h t) -> p (a h) t", t=P)
        og = shared[:, :, :]

        with core.stage() as block:
            @block.tensor
            def _(pe):
                def turn_out(g):
                    pe.wait_ge(parts_added, 8 * g)
                    for a in range(2):
                        for i in range(4):
                            last = pe.transpose(ps[:, MAXB[a], i * P:(i + 1) * P], og[:, i, a * P:(a + 1) * P],
                                                core.ident)
                        last.then_inc(out_turned, 1)

                def row_scores(g, hh, i):
                    n = 4 * g + hh
                    w = (i + 1) * P
                    for y in range(2):
                        pe.wait_ge(maxed, since(8 * n + 2 * i + y - 1))
                        out = ps[:, MAXB[y], :]
                        pe.matmul(out[:, i * P:w], core.identb[:, :], trin, start=True, stop=False)
                        last = pe.matmul(out[:, i * P:w], qh[0:DH, hh, i * P:w], kk[0:DH, y, g, i * P:w],
                                         start=False, stop=True)
                        if i:
                            last = pe.matmul(out[:, 0:i * P], qh[0:DH, hh, i * P:w], kk[0:DH, y, g, 0:i * P],
                                             start=True, stop=True)
                        last.then_inc(scored, 1)

                def key_scores(g, hh, j):
                    n = 4 * g + hh
                    if j == 0:
                        pe.wait_ge(shifts_ready, 8 * n + 8)
                    pe.wait_ge(exp_done, since(4 * n + j - 1))
                    for y in range(2):
                        out = ps[:, (j % 2) * 2 + y, j * P:SEQ]
                        keys = kk[:, y, g, j * P:(j + 1) * P]
                        pe.matmul(out, onesb[:, :], shift[:, hh % 2, y, j * P:SEQ], start=True, stop=False)
                        pe.matmul(out, keys, qh[:, hh, j * P:SEQ], start=False, stop=False)
                        pe.matmul(out, keys, ql[:, hh, j * P:SEQ], start=False, stop=False)
                        last = pe.matmul(ps[:, (j % 2) * 2 + y, j * P:(j + 1) * P], trin, core.identb[:, :],
                                         start=False, stop=True)
                    last.then_inc(keys_scored, 1)

                def body(g):
                    pe.wait_ge(q_staged, g + 1)
                    pe.wait_ge(exp_done, since(16 * g))
                    for hh in range(4):
                        for i in range(4):
                            last = pe.transpose(ps[:, hh, i * P:(i + 1) * P], qd[:, i, hh * P:(hh + 1) * P],
                                                core.ident)
                        last.then_inc(qT_turned, 1)
                    if not first(g):
                        turn_out(g)
                    pe.wait_ge(parts_taken, since(4 * g))
                    pe.wait_ge(vc_staged, g + 1)
                    pe.matmul(ps[:, OUTB, :].rearrange("p (h c) -> p h c", h=4), core.identb[:, :],
                              cmpp.unsqueeze(1).broadcast_to([P, 4, P]), start=True, stop=False)
                    pe.transpose(ps[:, OUTB + 1, 0:DH], vcx[:, :, :].rearrange("p i n -> p (i n)"),
                                 core.ident[0:DH, 0:DH]).then_inc(vc_turned, 1)
                    pe.wait_ge(kc_lo, g + 1)
                    pe.wait_ge(q_hi, 4 * g + 4)
                    pe.wait_ge(q_lo, 4 * g + 4)
                    for u in range(U):
                        for q in (qh, ql):
                            last = pe.matmul(ps[:, OUTB, u * 32:u * 32 + 32], q[:, u // 4, (u % 4) * P:(u % 4 + 1) * P],
                                             kcc[:, :], start=False, stop=(u == U - 1 and q is ql))
                    last.then_inc(cmp_scored, 1)
                    pe.wait_ge(out_lo, since(2 * g))
                    for i in range(4):
                        row_scores(g, 0, i)
                    pe.wait_ge(vc_by_tile, 4 * g + 4)
                    pe.wait_ge(cmp_step, 5 * g + 5)
                    for hh in range(4):
                        last = pe.transpose(ps[:, OUTB + 1, hh * P:(hh + 1) * P],
                                            pc[:, hh * 4:hh * 4 + 4, :].rearrange("p u n -> p (u n)"), core.ident)
                    last.then_inc(cmp_turned, 1)
                    key_scores(g, 0, 0)
                    pe.wait_ge(cmp_moved, g + 1)
                    for hh in range(4):
                        last = pe.matmul(ps[:, OUTB + hh // 2, (hh % 2) * 256:(hh % 2) * 256 + 256], pcT[:, hh, :],
                                         vcz[:, :, :].rearrange("p i d -> p (i d)"), start=True, stop=True)
                    last.then_inc(cmp_out, 1)
                    pe.wait_ge(v_staged, 2 * g + 2)
                    for hh in range(4):
                        n = 4 * g + hh
                        for j in range(4):
                            if hh or j:
                                key_scores(g, hh, j)
                            if hh < 3:
                                row_scores(g, hh + 1, j)
                        if hh == 0:
                            pe.wait_ge(out_set, 2 * g + 2)
                        else:
                            pe.wait_ge(parts_taken, n)
                        for i in range(4):
                            pe.wait_ge(exp_done, 4 * n + i + 1)
                            for y in range(2):
                                for j in range(i + 1):
                                    last = pe.matmul(ps[:, OUTB + y, i * VD:(i + 1) * VD],
                                                     pT[:, y, j, i * P:(i + 1) * P], vg[:, j, y, :],
                                                     start=(j == 0), stop=(j == i))
                        last.then_inc(attended, 1)
                pe.wait_ge(tables_set, 3)
                run(pe, KVH, body)
                turn_out(KVH)

            @block.scalar
            def _(act):
                def heads_of_out(g):
                    for a in range(2):
                        act.wait_ge(out_turned, 2 * g + a - 1)
                        act.copy(core.hhi[:, 2 * g + a - 2, 0:SEQ], ps[:, MAXB[a], :]).then_inc(out_hi, 1)

                def body(g):
                    act.wait_ge(cmp_scored, since(g))
                    act.copy(kcc[0:DH, :], cmp.kcT[:, DB, bass.ds(g * 32, 32)]).then_inc(kc_hi, 1)
                    for hh in range(4):
                        act.wait_ge(qT_turned, 4 * g + hh + 1)
                        act.copy(qh[:, hh, :], ps[:, hh, :]).then_inc(q_hi, 1)
                    if not first(g):
                        heads_of_out(g)
                    act.wait_ge(cmp_step, 5 * g + 3)
                    act.activation(pc[:, :, :], pc[:, :, :], ACT.Exp, scale=SCALE).then_inc(exp_cmp, 1)

                    def expo(hh, j):
                        n = 4 * g + hh
                        act.wait_ge(keys_scored, 4 * n + j + 1)
                        act.wait_ge(attended, since(n))
                        b = (j % 2) * 2
                        act.activation(pT[:, :, j, j * P:SEQ], ps[:, b:b + 2, j * P:SEQ], ACT.Exp, scale=SCALE
                                       ).then_inc(exp_done, 1)
                    expo(0, 0)
                    act.wait_ge(cmp_out, g + 1)
                    act.wait_ge(out_turned, since(2 * g))
                    for a in range(2):
                        act.copy(og[:, :, a * P:(a + 1) * P].rearrange("p i (h d) -> p h i d", d=DH),
                                 ps[:, OUTB + a, :].rearrange("p (h i d) -> p h i d", h=2, d=DH)
                                 ).then_inc(out_set, 1)
                    for hh in range(4):
                        for j in range(4):
                            if hh or j:
                                expo(hh, j)
                run(act, KVH, body)
                heads_of_out(KVH)

            @block.vector
            def _(dve):
                dve.memset(onesb[:, :], 1.0).then_inc(tables_set, 1)
                dve.tensor_scalar(nident[:, :], core.identb[:, :], -1.0, None, ALU.mult).then_inc(tables_set, 1)
                dve.memset(vcz[:, :, :], 0.0).then_inc(tables_set, 1)
                dve.wait_ge(tables_set, 3)

                def rests_of_out(g):
                    for a in range(2):
                        dve.wait_ge(out_hi, 2 * g + a - 1)
                        dve.tensor_tensor(core.hlo[:, 2 * g + a - 2, 0:SEQ], ps[:, MAXB[a], :],
                                          core.hhi[:, 2 * g + a - 2, 0:SEQ], ALU.subtract).then_inc(out_lo, 1)

                def body(g):
                    dve.wait_ge(vc_turned, since(g))
                    dve.tensor_copy(vcx[:, :, :], cmp.vcT[:, DB, bass.ds(g * 32, 32)].unsqueeze(1)
                                    .broadcast_to([DH, 4, 32])).then_inc(vc_staged, 1)
                    dve.wait_ge(kc_hi, g + 1)
                    dve.tensor_tensor(kcc[DH:P, :], cmp.kcT[:, DB, bass.ds(g * 32, 32)], kcc[0:DH, :],
                                      ALU.subtract).then_inc(kc_lo, 1)
                    for hh in range(4):
                        dve.wait_ge(q_hi, 4 * g + hh + 1)
                        dve.tensor_tensor(ql[:, hh, :], ps[:, hh, :], qh[:, hh, :], ALU.subtract).then_inc(q_lo, 1)
                    dve.wait_ge(vc_turned, g + 1)
                    for i in range(4):
                        rows = slice(i * 32, i * 32 + 32)
                        dve.tensor_copy(vcz[rows, i, :], ps[rows, OUTB + 1, 0:DH]).then_inc(vc_by_tile, 1)
                    dve.wait_ge(cmp_scored, g + 1)
                    s3 = ps[:, OUTB, :].rearrange("p (u n) -> p u n", n=32)
                    dve.tensor_reduce(mc[:, :], s3, AX.X, ALU.max).then_inc(cmp_step, 1)
                    dve.wait_ge(cmp_step, 5 * g + 1)
                    dve.tensor_scalar(mc[:, :], mc[:, :], NEG / 10, None, ALU.max).then_inc(cmp_step, 1)
                    dve.wait_ge(cmp_step, 5 * g + 2)
                    dve.tensor_tensor(pc[:, :, :], s3, mc[:, :].unsqueeze(2).broadcast_to([P, U, 32]),
                                      ALU.subtract).then_inc(cmp_step, 1)
                    if not first(g):
                        rests_of_out(g)

                    def shifts(hh, i):
                        n, w = 4 * g + hh, (i + 1) * P
                        dve.wait_ge(attended, since(n - 1))
                        for y in range(2):
                            dve.wait_ge(scored, 8 * n + 2 * i + y + 1)
                            dve.tensor_reduce(mx[:, hh % 2, y, i:i + 1], ps[:, MAXB[y], 0:w], AX.X, ALU.max
                                              ).then_inc(maxed, 1)
                        for y in range(2):
                            dve.wait_ge(maxed, 8 * n + 2 * i + y + 1)
                            dve.tensor_scalar(shift[:, hh % 2, y, i * P:w], nident[:, :], mx[:, hh % 2, y, i:i + 1],
                                              None, ALU.mult).then_inc(shifts_ready, 1)

                    def combine(hh):
                        n = 4 * g + hh
                        dve.wait_ge(attended, n + 1)
                        dve.wait_ge(parts_taken, since(n))
                        dve.wait_ge(parts_added, since(2 * (n - 1)))
                        both = ps[:, OUTB:OUTB + 2, 0:4 * VD].rearrange("p y (i c) -> p y i c", c=VD)
                        dve.tensor_scalar(coef[:, :, :], both[:, :, :, DH], 1e-30, None, ALU.max).then_inc(coef_step, 1)
                        dve.wait_ge(coef_step, 3 * n + 1)
                        dve.reciprocal(coef[:, :, :], coef[:, :, :]).then_inc(coef_step, 1)
                        dve.wait_ge(coef_step, 3 * n + 2)
                        dve.tensor_tensor(coef[:, :, :], coef[:, :, :],
                                          at.gates[:, 0:4, bass.ds(g * 12 + hh * 3 + 1, 2)].rearrange("p i y -> p y i"),
                                          ALU.mult).then_inc(coef_step, 1)
                        dve.wait_ge(coef_step, 3 * n + 3)
                        dve.tensor_tensor(part[:, hh % 2, :, :, :], both[:, :, :, 0:DH],
                                          coef[:, :, :].unsqueeze(3).broadcast_to([P, 2, 4, DH]), ALU.mult
                                          ).then_inc(parts_taken, 1)
                    for i in range(4):
                        shifts(0, i)
                    dve.wait_ge(exp_cmp, g + 1)
                    dve.tensor_reduce(sc[:, :], pc[:, :, :], AX.X, ALU.add).then_inc(cmp_step, 1)
                    dve.wait_ge(cmp_step, 5 * g + 4)
                    dve.tensor_scalar(sc[:, :], sc[:, :], 1e-30, None, ALU.max).then_inc(cmp_recip, 1)
                    dve.wait_ge(cmp_recip, 3 * g + 1)
                    dve.reciprocal(sc[:, :], sc[:, :]).then_inc(cmp_recip, 1)
                    dve.wait_ge(cmp_recip, 3 * g + 2)
                    dve.tensor_tensor(
                        sc[:, :].rearrange("p (h i) -> p h i", i=4), sc[:, :].rearrange("p (h i) -> p h i", i=4),
                        at.gates[:, 0:4, bass.ds(g * 12, 12)].rearrange("p i (h c) -> p h i c", c=3)[:, :, :, 0],
                        ALU.mult).then_inc(cmp_recip, 1)
                    dve.wait_ge(cmp_recip, 3 * g + 3)
                    dve.tensor_tensor(pc[:, :, :], pc[:, :, :], sc[:, :].unsqueeze(2).broadcast_to([P, U, 32]),
                                      ALU.mult).then_inc(cmp_step, 1)
                    dve.wait_ge(cmp_turned, g + 1)
                    dve.tensor_copy(pcT[:, :, :], ps[:, OUTB + 1, :].rearrange("p (h t) -> p h t", h=4)
                                    ).then_inc(cmp_moved, 1)
                    for hh in range(4):
                        if hh < 3:
                            for i in range(4):
                                shifts(hh + 1, i)
                        combine(hh)
                run(dve, KVH, body)
                rests_of_out(KVH)

            @block.gpsimd
            def _(pool):
                q4 = lambda g: at.qkv[:, 0:4, bass.ds(g * 256, 256)].rearrange("p i (h d) -> p i h d", d=DH)
                qd4 = qd.rearrange("p i (h u d) -> p i h u d", u=2, d=DH)

                def stage_q(g):
                    pool.wait_ge(qT_turned, since(4 * g))
                    pool.tensor_copy(qd4[:, :, :, 0, :], q4(g)).then_inc(q_doubled, 1)
                    pool.tensor_copy(qd4[:, :, :, 1, :], q4(g)).then_inc(q_staged, 1)
                q_doubled = core.sig("q_doubled")
                pool.memset(vg[:, :, :, DH:VD], 1.0).then_inc(core.sig("ones_set"), 1)
                stage_q(0)

                def body(g):
                    pool.wait_ge(attended, since(4 * g))
                    for y in range(2):
                        v = at.qkv[:, 0:4, bass.ds(g * DH + (VS, VW)[y], DH)]
                        pool.tensor_copy(vg[:, :, y, 0:DH], v).then_inc(v_staged, 1)
                    for hh in range(4):
                        n = 4 * g + hh
                        pool.wait_ge(out_set, 2 * g + 2)
                        pool.wait_ge(parts_taken, n + 1)
                        for y in range(2):
                            o = og[:, :, hh * DH:(hh + 1) * DH]
                            pool.wait_ge(parts_added, since(2 * n + y))
                            pool.tensor_tensor(o, o, part[:, hh % 2, y, :, :], ALU.add).then_inc(parts_added, 1)
                        if hh == 0 and not (type(g) is int and g == KVH - 1):
                            stage_q(g + 1)
                run(pool, KVH, body)



def sample_attention(core, at, cmp):
    nc, ps, io = core.nc, core.ps, core.io
    names = ("page_in", "vc_turned", "vc_moved", "keys_filled", "k_landed", "v_landed0", "v_landed1", "k_turned",
             "kT_moved_dve", "kT_moved_act", "rows_staged", "v_staged", "s_scored", "s_max", "s_exp", "s_sum",
             "s_scaled", "s_turned", "s_moved", "s_attended", "s_out", "s_spread", "s_hi", "s_lo")
    (page_in, vc_turned, vc_moved, keys_filled, k_landed, v_landed0, v_landed1, k_turned, kT_dve, kT_act, staged,
     v_staged, scored, maxed, exped, summed, scaled, turned, moved, attended, out_taken, spread, s_hi, s_lo) = (
        core.sig(n) for n in names)
    v_landed = (v_landed0, v_landed1)
    trin0 = C_TRIN
    with ExitStack() as own:
        sb = lambda n, s: core.sb(n, s, F32, own)
        pages = core.sb("pages", [1, DB * NPAGE], I32, own)
        kn, vn = sb("k_rows", [P, 2, NPAGE, 256]), sb("v_rows", [P, 2, 2, NPAGE, 256])
        kTb = sb("kT_batch", [P, 2, 2, T])
        qst, qcs, vcs = sb("q_stage", [P, 2, 64]), sb("qc_stage", [DH, P]), sb("vc_stage", [P, 2, DH])
        prob, pcs = sb("s_prob", [P, T]), sb("s_pcmp", [64, P])
        pT, pcT = sb("s_probT", [P, 5, P]), sb("s_pcmpT", [P, 64])
        mx2, mx = sb("s_max2", [P, 2]), sb("s_mx", [P, 2])
        sums, coef = sb("s_sums", [P, 2]), sb("s_coef", [P, 2])
        vc = sb("vc", [P, DB, DH])
        outs, oT = sb("s_outs", [P, DB, 64]), sb("s_oT", [P, KD, SAMP])

        with core.stage() as block:
            @block.sync
            def _(sp):
                sp.dma_start(pages[:, :], io["page_table"].rearrange("(o b) n -> o (b n)", o=1)).then_inc(
                    page_in, 16)
                sp.wait_ge(page_in, 16)

                def body(i):
                    for par in range(2):
                        b = 2 * i + par
                        ids = [sp.value_load(pages[0:1, bass.ds(b * NPAGE + n, 1)], min_val=0,
                                             max_val=io["cache_nsa_kv"].shape[1] - 1) for n in range(NPAGE)]
                        sp.wait_ge(k_turned, since(4 * b))
                        pool_kv = io["cache_nsa_kv"][0]
                        win = io["state_win_kv"][0, b] if type(b) is int else \
                            io["state_win_kv"][0, bass.ds(b, 1)].rearrange("o t s g d -> (o t) s g d")
                        for n in range(NPAGE):
                            page = pool_kv[bass.ds(ids[n], 1)].rearrange("o t s g d -> (o t) s (g d)")
                            sp.dma_start(kn[:, 0, n, :], page[:, 2, :]).then_inc(k_landed, 16)
                            if n == 0:
                                sp.wait_ge(attended, since(b - 1))
                            sp.dma_start(vn[:, par, 0, n, :], page[:, 3, :]).then_inc(v_landed[par], 16)
                        for y, dst, s in ((0, kn[:, 1, :, :], k_landed), (1, vn[:, par, 1, :, :], v_landed[par])):
                            sp.dma_start(dst, win[:, y].rearrange("(n p) g d -> p n (g d)", p=P)).then_inc(s, 16)
                run(sp, DB // 2, body)

            @block.tensor
            def _(pe):
                for b in range(DB):
                    last = pe.transpose(ps[:, 7, b * DH:(b + 1) * DH], cmp.vcT[:, b, :], core.ident[0:DH, 0:DH])
                last.then_inc(vc_turned, 1)

                def turn_keys(b):
                    pe.wait_ge(k_landed, 16 * 5 * (b + 1))
                    pe.wait_ge(kT_dve, since(2 * b))
                    pe.wait_ge(kT_act, since(2 * b))
                    for y in range(2):
                        for u in range(2):
                            for n in range(NPAGE):
                                last = pe.transpose(ps[:, y * 2 + u, n * P:(n + 1) * P],
                                                    kn[:, y, n, u * P:(u + 1) * P], core.ident)
                            last.then_inc(k_turned, 1)

                def body(i):
                    for par in range(2):
                        b = 2 * i + par
                        pe.wait_ge(staged, 2 * b + 2)
                        pe.wait_ge(kT_dve, 2 * b + 2)
                        pe.wait_ge(kT_act, 2 * b + 2)
                        for y in range(2):
                            rows = slice(y * 64, y * 64 + 64)
                            for h in range(2):
                                for u in range(2):
                                    pe.matmul(ps[rows, 4 + h, 0:HALF], qst[:, u, :],
                                              kTb[:, y, u, h * HALF:(h + 1) * HALF], start=(u == 0), stop=False)
                        pe.matmul(ps[:, 4, 0:DS], core.identb[:, :],
                                  core.maskb[:, C_WIN - trin0:C_WIN - trin0 + DS], start=False, stop=True)
                        pe.matmul(ps[:, 5, HALF - 32:HALF], core.identb[:, :],
                                  core.maskb[:, bass.ds(b * 32 + C_NEW - trin0, 32)], start=False, stop=True)
                        pe.matmul(ps[:, 6, 0:P], core.identb[:, :],
                                  core.maskb[:, C_CMPS - trin0:C_CMPS - trin0 + P], start=True, stop=False)
                        pe.matmul(ps[:, 6, 0:P], qcs[:, :], cmp.kcT[:, b, :], start=False, stop=True).then_inc(scored, 1)
                        if not (type(b) is int and b == DB - 1):
                            turn_keys(b + 1)
                        pe.wait_ge(scaled, 2 * b + 2)
                        for n in range(4):
                            last = pe.transpose(ps[:, 7, n * P:(n + 1) * P], prob[:, n * P:(n + 1) * P], core.ident)
                        last.then_inc(turned, 1)
                        pe.transpose(ps[0:32, 6, P:2 * P], prob[:, SEQ:T], core.ident)
                        pe.transpose(ps[:, 6, 2 * P:2 * P + 64], pcs[:, :], core.ident[0:64, 0:64]).then_inc(turned, 1)
                        pe.wait_ge(moved, 2 * b + 2)
                        pe.wait_ge(core.sig("s_moved_act"), b + 1)
                        pe.wait_ge(v_staged, b + 1)
                        pe.wait_ge(v_landed[par], 16 * 5 * (i + 1))
                        for u in range(2):
                            out = ps[:, 6, 384 + u * 32:416 + u * 32]
                            for y in range(2):
                                c = y * 64 + u * 32
                                for n in range(4):
                                    pe.matmul(out, vn[:, par, y, n, u * P:(u + 1) * P], pT[:, n, c:c + 32],
                                              start=(y == 0 and n == 0), stop=False)
                                v = (VS, VW)[y] + u * P
                                pe.matmul(out, at.qkv[0:SAMP, 4, v:v + P], pT[0:SAMP, 4, c:c + 32],
                                          start=False, stop=False)
                            last = pe.matmul(out, vcs[:, :, :].rearrange("p a d -> p (a d)"),
                                             pcT[:, u * 32:u * 32 + 32], start=False, stop=True)
                        last.then_inc(attended, 1)
                        pe.wait_ge(out_taken, b + 1)
                pe.wait_ge(vc_moved, 1)
                turn_keys(0)
                run(pe, DB // 2, body)

            @block.scalar
            def _(act):
                def move_keys(b):
                    for u in range(2):
                        act.wait_ge(k_turned, 4 * b + 3 + u)
                        act.wait_ge(scored, since(b))
                        act.copy(kTb[:, 1, u, 0:PAST], ps[:, 2 + u, :]).then_inc(kT_act, 1)

                def body(i):
                    for par in range(2):
                        b = 2 * i + par
                        act.wait_ge(maxed, 5 * b + 5)
                        act.wait_ge(turned, since(2 * b))
                        act.activation(prob[:, :].rearrange("p (h c) -> p h c", h=2), ps[:, 4:6, 0:HALF], ACT.Exp,
                                       bias=mx[:, 0:1], scale=SCALE, accum_out=sums[:, 0:1]).then_inc(exped, 1)
                        act.activation(pcs[:, :], ps[0:64, 6, 0:P], ACT.Exp, bias=mx[0:64, 1:2], scale=SCALE,
                                       accum_out=sums[0:64, 1:2]).then_inc(exped, 1)
                        if not (type(b) is int and b == DB - 1):
                            move_keys(b + 1)
                        act.wait_ge(turned, 2 * b + 2)
                        act.wait_ge(attended, since(b))
                        act.copy(pT[:, 0:4, :], ps[:, 7, :].rearrange("p (n r) -> p n r", n=4)).then_inc(core.sig("s_moved_act"), 1)
                move_keys(0)
                run(act, DB // 2, body)
                act.wait_ge(spread, 8)
                act.copy(core.hhi[:, :, SEQ:T], oT[:, :, :]).then_inc(s_hi, 1)

            @block.vector
            def _(dve):
                dve.memset(sums[:, :], 1.0).then_inc(keys_filled, 1)
                dve.memset(mx[:, :], 0.0).then_inc(keys_filled, 1)
                dve.memset(qcs[:, :], 0.0).then_inc(keys_filled, 1)
                dve.tensor_copy(kTb[:, :, :, PAST:T], at.kTn[:, :, :, :]).then_inc(keys_filled, 1)
                dve.wait_ge(vc_turned, 1)
                dve.tensor_copy(vc[:, :, :], ps[:, 7, :].rearrange("p (b d) -> p b d", d=DH)).then_inc(vc_moved, 1)
                dve.wait_ge(vc_moved, 1)
                dve.wait_ge(keys_filled, 4)

                def move_keys(b):
                    for u in range(2):
                        dve.wait_ge(k_turned, 4 * b + 1 + u)
                        dve.wait_ge(scored, since(b))
                        dve.tensor_copy(kTb[:, 0, u, 0:PAST], ps[:, u, :]).then_inc(kT_dve, 1)

                def body(i):
                    for par in range(2):
                        b = 2 * i + par
                        dve.wait_ge(scored, since(b))
                        dve.tensor_copy(qst[:, :, :], at.qblk[:, b, :, :]).then_inc(staged, 1)
                        dve.tensor_copy(qcs[:, 0:64], at.qs[:, b, :]).then_inc(staged, 1)
                        dve.wait_ge(scored, b + 1)
                        dve.tensor_reduce(mx2[:, :], ps[:, 4:6, 0:HALF], AX.X, ALU.max).then_inc(maxed, 1)
                        dve.tensor_reduce(mx[0:64, 1:2], ps[0:64, 6, 0:P], AX.X, ALU.max).then_inc(maxed, 1)
                        dve.wait_ge(maxed, 5 * b + 2)
                        dve.tensor_reduce(mx[:, 0:1], mx2[:, :], AX.X, ALU.max).then_inc(maxed, 1)
                        dve.tensor_scalar(mx[0:64, 1:2], mx[0:64, 1:2], NEG / 10, -SCALE, ALU.max, ALU.mult).then_inc(maxed, 1)
                        dve.wait_ge(maxed, 5 * b + 3)
                        dve.tensor_scalar(mx[:, 0:1], mx[:, 0:1], -SCALE, None, ALU.mult).then_inc(maxed, 1)
                        dve.wait_ge(exped, 2 * b + 2)
                        dve.tensor_scalar(coef[:, :], sums[:, :], 1e-30, None, ALU.max).then_inc(summed, 1)
                        dve.wait_ge(summed, 3 * b + 1)
                        dve.reciprocal(coef[:, :], coef[:, :]).then_inc(summed, 1)
                        dve.wait_ge(summed, 3 * b + 2)
                        dve.tensor_tensor(coef[:, :], coef[:, :], at.gate_rows[:, b, :], ALU.mult).then_inc(summed, 1)
                        dve.wait_ge(summed, 3 * b + 3)
                        dve.tensor_scalar(prob[:, :], prob[:, :], coef[:, 0:1], None, ALU.mult).then_inc(scaled, 1)
                        dve.tensor_scalar(pcs[:, :], pcs[:, :], coef[0:64, 1:2], None, ALU.mult).then_inc(scaled, 1)
                        if not (type(b) is int and b == DB - 1):
                            move_keys(b + 1)
                        dve.wait_ge(attended, since(b))
                        dve.tensor_copy(vcs[:, :, :], vc[:, b, :].unsqueeze(1).broadcast_to([P, 2, DH])).then_inc(v_staged, 1)
                        dve.wait_ge(turned, 2 * b + 2)
                        dve.tensor_copy(pT[0:32, 4, :], ps[0:32, 6, P:2 * P]).then_inc(moved, 1)
                        dve.tensor_copy(pcT[:, :], ps[:, 6, 2 * P:2 * P + 64]).then_inc(moved, 1)
                        dve.wait_ge(attended, b + 1)
                        dve.tensor_copy(outs[:, b, :], ps[:, 6, 384:448]).then_inc(out_taken, 1)
                move_keys(0)
                run(dve, DB // 2, body)
                dve.wait_ge(out_taken, DB)
                for g in range(KVH):
                    for c in range(2):
                        src = outs[(g % 2) * DH:(g % 2) * DH + DH, :, g * 16:g * 16 + 16].rearrange(
                            "p b (a c t) -> p c a b t", a=2, c=2)[:, c]
                        dst = oT[c * DH:c * DH + DH, 2 * g:2 * g + 2, :].rearrange("p a (b t) -> p a b t", t=DS)
                        dve.tensor_copy(dst, src).then_inc(spread, 1)
                dve.wait_ge(s_hi, 1)
                dve.tensor_tensor(core.hlo[:, :, SEQ:T], oT[:, :, :], core.hhi[:, :, SEQ:T], ALU.subtract).then_inc(s_lo, 1)



def features_to_y(core, seg, moving, parts, epilogue=None):
    nc, ps = core.nc, core.ps
    first = core.starts[seg]
    n_tiles = core.stream[seg][0] // parts
    kt = core.stream[seg][1] // P
    per = 4 // parts
    y_taken, y_sq, y_added, cleared = core.sig("y_taken"), core.sig("y_squared"), core.sig("ssq_added"), core.sig("ssq_cleared")
    hi, lo = moving
    extra = epilogue or {}
    with core.stage() as block:
        @block.sync
        def _(sp):
            load_stage(core, sp, seg, first)
            if "sync" in extra:
                extra["sync"](sp)

        @block.tensor
        def _(pe):
            if "tensor" in extra:
                extra["tensor"](pe)

            def body(i):
                for k in range(4):
                    m, part = i * per + k // parts, k % parts
                    bank = (k // parts) % 2 * 2
                    weights_ready(core, pe, first + 4 * i + k)
                    if part == 0:
                        pe.wait_ge(y_taken, since(m - 1))
                    w_hi, w_lo = (w[:, k, 0:kt * P].rearrange("p (a c) -> p a c", c=P) for w in (core.whi, core.wlo))
                    for h in range(2):
                        cols = slice(h * HALF, (h + 1) * HALF)
                        last = product(pe, ps[:, bank + h, 0:HALF], [(a, part * kt + a) for a in range(kt)],
                                       lambda a: (w_hi[:, a, :], w_lo[:, a, :]),
                                       lambda a: (hi[:, a, cols], lo[:, a, cols]), part == 0, part == parts - 1)
                    last.then_inc(core.w_used, 1)
            run(pe, n_tiles // per, body)

        @block.scalar
        def _(act):
            if "scalar" in extra:
                extra["scalar"](act)

            def body(i):
                for k in range(4):
                    m = i * per + k // parts
                    cast_hi(core, act, seg, i, k, first)
                    if k % parts == parts - 1:
                        act.wait_ge(y_taken, m + 1)
                        act.wait_ge(y_added, since(m - 1))
                        act.activation(core.sq[:, (k // parts) % 2, :], core.yT[:, m, :], ACT.Square).then_inc(y_sq, 1)
            run(act, n_tiles // per, body)

        @block.vector
        def _(dve):
            dve.memset(core.ssq[:, :], 0.0).then_inc(cleared, 1)
            dve.wait_ge(cleared, 1)
            if "vector" in extra:
                extra["vector"](dve)

            def body(i):
                for j in range(per):
                    m = i * per + j
                    dve.wait_ge(core.w_used, first + (m + 1) * parts)
                    dve.tensor_copy(core.yT[:, m, :].rearrange("p (h c) -> p h c", h=2),
                                    ps[:, (j % 2) * 2:(j % 2) * 2 + 2, 0:HALF]).then_inc(y_taken, 1)
                    dve.wait_ge(y_sq, m + 1)
                    dve.wait_ge(y_added, since(m))
                    dve.tensor_tensor(core.ssq[:, :], core.ssq[:, :], core.sq[:, j % 2, :], ALU.add).then_inc(y_added, 1)
            run(dve, n_tiles // per, body)

        @block.gpsimd
        def _(pool):
            def body(i):
                for k in range(4):
                    cast_lo(core, pool, seg, i, k, first)
            run(pool, n_tiles // per, body)



GW = 2 + SEQ + DB * (DS + 2)


def ffn_up(core, l, seg, ghi, glo, kept):
    nc, ps = core.nc, core.ps
    first = core.starts[seg]
    gate_in, conv, gelu, prod, g_hi, g_lo, keep, cleared = (core.sig(n) for n in (
        "gate_in", "conv_step", "gelu_done", "product_done", "g_hi", "g_lo", "rows_kept", "gate_cleared"))
    with ExitStack() as own:
        gate = core.sb("gate", [P, 2, GW], F32, own)
        cv = core.sb("conv", [P, 2, GW - 2], F32, own)
        ge = core.sb("gelu", [P, 2, GW - 2], F32, own)
        gp = core.sb("gated", [P, 2, T], F32, own)
        later = lambda x: x.rearrange("p (b j) -> p b j", j=DS + 2)
        with core.stage() as block:
            @block.sync
            def _(sp):
                load_stage(core, sp, seg, first)

            @block.tensor
            def _(pe):
                def body(i):
                    for k in range(4):
                        m, q, val = 2 * i + k // 2, k // 2, k % 2
                        weights_ready(core, pe, first + 4 * i + k)
                        if val:
                            pe.wait_ge(prod, since(3 * (m - 1)))
                        else:
                            pe.wait_ge(gate_in, since(4 * (m - 1)))
                        w_hi, w_lo = block_hi(core, k, P), block_lo(core, k, P)
                        for h in range(2):
                            cols = slice(h * HALF, (h + 1) * HALF)
                            last = product(pe, ps[:, 4 * q + 2 * val + h, 0:HALF], [(a, a) for a in range(KD)],
                                           lambda a: (w_hi[:, a, :], w_lo[:, a, :]),
                                           lambda a: (core.hhi[:, a, cols], core.hlo[:, a, cols]), True, True)
                        last.then_inc(core.w_used, 1)
                run(pe, KF // 2, body)

            @block.scalar
            def _(act):
                act.wait_ge(cleared, 1)

                def body(i):
                    for q in range(2):
                        m = 2 * i + q
                        act.wait_ge(core.w_used, first + 2 * m + 1)
                        act.wait_ge(conv, since(3 * (m - 1)))
                        act.wait_ge(keep, since(2 * (m - 1)))
                        act.copy(gate[:, q, 2:2 + HALF], ps[:, 4 * q, 0:HALF]).then_inc(gate_in, 1)
                        act.copy(gate[:, q, 2 + HALF:2 + SEQ], ps[:, 4 * q + 1, 0:SEQ - HALF]).then_inc(gate_in, 1)
                        act.copy(later(gate[:, q, 2 + SEQ:GW])[:, :, 2:],
                                 ps[:, 4 * q + 1, SEQ - HALF:HALF].rearrange("p (b t) -> p b t", t=DS)).then_inc(gate_in, 1)
                        act.copy(later(gate[:, q, 2 + SEQ:GW])[:, :, 0:2],
                                 core.taps[:, l, m, 4:20].rearrange("p (b j) -> p b j", j=2)).then_inc(gate_in, 1)
                        cast_hi(core, act, seg, i, 2 * q, first)
                        act.wait_ge(conv, 3 * m + 3)
                        act.wait_ge(prod, since(3 * (m - 1)))
                        act.activation(ge[:, q, :], cv[:, q, :], ACT.Gelu_apprx_tanh).then_inc(gelu, 1)
                        cast_hi(core, act, seg, i, 2 * q + 1, first)
                        act.wait_ge(prod, 3 * m + 3)
                        act.copy(ghi[:, m, :], gp[:, q, :]).then_inc(g_hi, 1)
                run(act, KF // 2, body)

            @block.vector
            def _(dve):
                dve.memset(gate[:, :, 0:2], 0.0).then_inc(cleared, 1)

                def body(i):
                    for q in range(2):
                        m = 2 * i + q
                        tap = lambda j: core.taps[:, l, m, j:j + 1]
                        dve.wait_ge(gate_in, 4 * m + 4)
                        dve.wait_ge(gelu, since(m - 1))
                        dve.tensor_scalar(cv[:, q, :], gate[:, q, 0:GW - 2], tap(0), tap(3), ALU.mult, ALU.add).then_inc(conv, 1)
                        for j in (1, 2):
                            dve.wait_ge(conv, 3 * m + j)
                            dve.scalar_tensor_tensor(cv[:, q, :], gate[:, q, j:GW - 2 + j], tap(j), cv[:, q, :],
                                                     ALU.mult, ALU.add).then_inc(conv, 1)
                        dve.wait_ge(gelu, m + 1)
                        dve.wait_ge(core.w_used, first + 2 * m + 2)
                        dve.wait_ge(g_lo, since(m - 1))
                        for out, a, v in (
                                (gp[:, q, 0:HALF], ge[:, q, 0:HALF], ps[:, 4 * q + 2, 0:HALF]),
                                (gp[:, q, HALF:SEQ], ge[:, q, HALF:SEQ], ps[:, 4 * q + 3, 0:SEQ - HALF]),
                                (gp[:, q, SEQ:T].rearrange("p (b t) -> p b t", t=DS), later(ge[:, q, SEQ:])[:, :, 2:],
                                 ps[:, 4 * q + 3, SEQ - HALF:HALF].rearrange("p (b t) -> p b t", t=DS))):
                            dve.tensor_tensor(out, a, v, ALU.mult).then_inc(prod, 1)
                run(dve, KF // 2, body)

            @block.gpsimd
            def _(pool):
                def body(i):
                    for q in range(2):
                        m = 2 * i + q
                        pool.wait_ge(gate_in, 4 * m + 4)
                        pool.tensor_copy(kept[:, m, 0:2], gate[:, q, SEQ:SEQ + 2]).then_inc(keep, 1)
                        pool.tensor_copy(kept[:, m, 2:18].rearrange("p (b j) -> p b j", j=2),
                                         later(gate[:, q, 2 + SEQ:GW])[:, :, DS:]).then_inc(keep, 1)
                        cast_lo(core, pool, seg, i, 2 * q, first)
                        pool.wait_ge(g_hi, m + 1)
                        pool.tensor_tensor(glo[:, m, :], gp[:, q, :], ghi[:, m, :], ALU.subtract).then_inc(g_lo, 1)
                        cast_lo(core, pool, seg, i, 2 * q + 1, first)
                run(pool, KF // 2, body)


def ffn(core, l, seg):
    io, ps = core.io, core.ps
    with ExitStack() as own:
        ghi = core.sb("g_hi", [P, KF, T], F16, own)
        glo = core.sb("g_lo", [P, KF, T], BF16, own)
        kept = core.sb("kept", [P, KF, 18], F32, own)
        rows = core.sb("kept_rows", [18, F], F32, own)
        ffn_up(core, l, seg, ghi, glo, kept)
        k_turned, k_moved = core.sig("kept_turned"), core.sig("kept_moved")
        core.conv_out = core.sig("conv_rows_out")
        n = -(-KF // 4)

        def turn(pe):
            for j in range(n):
                pe.wait_ge(k_moved, since(j - 3))
                for m in range(4 * j, min(4 * j + 4, KF)):
                    last = pe.transpose(ps[0:18, 4 + j % 4, (m % 4) * P:(m % 4 + 1) * P], kept[:, m, :], core.ident)
                last.then_inc(k_turned, 1)

        def move(dve):
            for j in range(n):
                dve.wait_ge(k_turned, j + 1)
                w = min(512, F - 512 * j)
                dve.tensor_copy(rows[:, 512 * j:512 * j + w], ps[0:18, 4 + j % 4, 0:w]).then_inc(k_moved, 1)

        def out(sp):
            sp.wait_ge(k_moved, n)
            sp.dma_start(io["out_ffn_p"][l, 0], rows[0:2, :]).then_inc(core.conv_out, 16)
            sp.dma_start(io["out_ffn_s"][l].rearrange("b j f -> (b j) f"), rows[2:18, :]).then_inc(core.conv_out, 16)
            sp.wait_ge(core.conv_out, 32)
        features_to_y(core, seg + 1, (ghi, glo), 2, dict(sync=out, tensor=turn, vector=move))



class Gla:
    def __init__(self, core, ctx):
        self.qk = core.sb("gla_qk", [P, 2 * GH, T], F32, ctx)
        self.cum = core.sb("gla_cum", [P, GH, T], F32, ctx)
        self.vr = core.sb("gla_vr", [P, NT, 2 * GH * DV], F32, ctx)
        self.sumsq = core.sb("gla_sumsq", [P, NT, GH], F32, ctx)
        self.ng = core.sb("gla_norm", [P, DV], F32, ctx)


def gla_heads(core, gla, seg):
    nc, ps, io = core.nc, core.ps, core.io
    first = core.starts[seg]
    n_tiles = core.stream[seg][0]
    taken, small_in, low, low_taken, z_ready, z_taken, steps, cast = (core.sig(n) for n in (
        "qk_taken", "gla_small_in", "low_rank_ready", "low_rank_taken", "gates_raw", "gates_biased", "decay_step",
        "low_w_cast"))
    with ExitStack() as own:
        gw = core.sb("low_w", [P, KD, 16], F32, own)
        gwhi, gwlo = core.sb("low_w_hi", [P, KD, 16], F16, own), core.sb("low_w_lo", [P, KD, 16], BF16, own)
        up = core.sb("gate_up", [16, GH * DK], F32, own)
        bias = core.sb("gate_bias", [P, GH], F32, own)
        ngrow = core.sb("norm_row", [1, DV], F32, own)
        lowT = core.sb("low_T", [16, T], F32, own)
        z = core.sb("z", [P, GH, T], F32, own)
        with core.stage() as block:
            @block.sync
            def _(sp):
                sp.dma_start(gw[:, :, :], io["gla_w_in"][0][:, GPROJ - 16:GPROJ].rearrange("(k p) c -> p k c", p=P)
                             ).then_inc(small_in, 16)
                sp.dma_start(up[:, :], io["gla_w_gate_up"][0]).then_inc(small_in, 16)
                sp.dma_start(bias[:, :], io["gla_b_gate"].rearrange("o (h p) -> p (o h)", p=P),
                             allow_slow_non_contiguous=True).then_inc(
                    small_in, 16)
                sp.dma_start(ngrow[:, :], io["gla_norm_gain"]).then_inc(small_in, 16)
                load_stage(core, sp, seg, first)

            @block.tensor
            def _(pe):
                pe.wait_ge(small_in, 64)
                pe.matmul(ps[:, 6, 0:DV], core.ones[0:1, :], ngrow[:, :], start=True, stop=True).then_inc(low, 1)
                pe.wait_ge(cast, 2)
                for h in range(2):
                    cols = slice(h * HALF, (h + 1) * HALF)
                    last = product(pe, ps[0:16, 4 + h, 0:HALF], [(a, a) for a in range(KD)],
                                   lambda a: (gwhi[:, a, :], gwlo[:, a, :]),
                                   lambda a: (core.hhi[:, a, cols], core.hlo[:, a, cols]), True, True)
                last.then_inc(low, 1)
                pe.wait_ge(low_taken, 2)
                for t in range(GH):
                    pe.wait_ge(z_taken, since(t))
                    for h in range(2):
                        last = pe.matmul(ps[:, 4 + h, 0:HALF], up[:, t * DK:(t + 1) * DK],
                                         lowT[:, h * HALF:(h + 1) * HALF], start=True, stop=True)
                    last.then_inc(z_ready, 1)

                def body(i):
                    for k in range(4):
                        n = 4 * i + k
                        weights_ready(core, pe, first + n)
                        pe.wait_ge(taken, since(n - 1))
                        w_hi, w_lo = block_hi(core, k, P), block_lo(core, k, P)
                        for h in range(2):
                            cols = slice(h * HALF, (h + 1) * HALF)
                            last = product(pe, ps[:, (k % 2) * 2 + h, 0:HALF], [(a, a) for a in range(KD)],
                                           lambda a: (w_hi[:, a, :], w_lo[:, a, :]),
                                           lambda a: (core.hhi[:, a, cols], core.hlo[:, a, cols]), True, True)
                        last.then_inc(core.w_used, 1)
                run(pe, n_tiles // 4, body)

            @block.scalar
            def _(act):
                act.wait_ge(small_in, 64)
                act.copy(gwhi[:, :, :], gw[:, :, :]).then_inc(cast, 1)
                act.wait_ge(low, 1)
                act.copy(gla.ng[:, :], ps[:, 6, 0:DV]).then_inc(low_taken, 1)
                act.wait_ge(low, 2)
                act.copy(lowT[:, :].rearrange("p (h c) -> p h c", h=2), ps[0:16, 4:6, 0:HALF]).then_inc(low_taken, 1)
                for t in range(GH):
                    act.wait_ge(z_ready, t + 1)
                    act.activation(z[:, t, :].rearrange("p (h c) -> p h c", h=2), ps[:, 4:6, 0:HALF],
                                   ACT.Identity, bias=bias[:, t:t + 1]).then_inc(z_taken, 1)

                def body(i):
                    for k in range(4):
                        act.wait_ge(core.w_used, first + 4 * i + k + 1)
                        act.copy(gla.qk[:, 4 * i + k, :].rearrange("p (h c) -> p h c", h=2),
                                 ps[:, (k % 2) * 2:(k % 2) * 2 + 2, 0:HALF]).then_inc(taken, 1)
                        cast_hi(core, act, seg, i, k, first)
                run(act, n_tiles // 4, body)
                act.wait_ge(steps, 1)
                act.activation(gla.cum[:, :, :], gla.cum[:, :, :], ACT.Exp).then_inc(steps, 1)
                act.wait_ge(steps, 2)
                act.activation(gla.cum[:, :, :], gla.cum[:, :, :], ACT.Ln, bias=1.0).then_inc(steps, 1)

            @block.vector
            def _(dve):
                dve.wait_ge(small_in, 64)
                dve.wait_ge(cast, 1)
                dve.tensor_tensor(gwlo[:, :, :], gw[:, :, :], gwhi[:, :, :], ALU.subtract).then_inc(cast, 1)
                dve.wait_ge(z_taken, GH)
                dve.scalar_tensor_tensor(gla.cum[:, :, :], z[:, :, :], -1.0, z[:, :, :], ALU.mult, ALU.min).then_inc(steps, 1)
                dve.wait_ge(steps, 3)
                dve.scalar_tensor_tensor(z[:, :, :], z[:, :, :], 0.0, gla.cum[:, :, :], ALU.min, ALU.subtract).then_inc(steps, 1)
                dve.wait_ge(steps, 4)
                for h in range(GH):
                    dve.tensor_tensor_scan(gla.cum[:, h, :], core.const[:, C_SEG:C_SEG + T], z[:, h, :], 0.0,
                                           ALU.mult, ALU.add).then_inc(steps, 1)

            @block.gpsimd
            def _(pool):
                def body(i):
                    for k in range(4):
                        cast_lo(core, pool, seg, i, k, first)
                run(pool, n_tiles // 4, body)



LIMIT = 40 * 16.0


def gla_core(core, gla, o):
    nc, ps, io = core.nc, core.ps, core.io
    C = SEQ // P
    names = ("g_diff", "g_exp", "g_prod", "g_turned", "g_kend", "g_att", "g_att_masked", "g_kv", "g_state", "g_out",
             "g_out_taken", "s0_in0", "s_rows", "s_kv", "s_new", "states_out", "g_qb")
    (diff, exped, prod, turned, kend_ready, att, att_masked, kv, state, out, out_taken, s0_in, s_rows, s_kv, s_new,
     states_out, _) = (core.sig(n) for n in names)
    core.states_out = states_out
    with ExitStack() as own:
        sb = lambda n, s: core.sb(n, s, F32, own)
        d = sb("g_d", [P, 2, T])
        e = sb("g_e", [P, 4, T])
        qd, kd, qi, ke = sb("g_qd", [P, T]), sb("g_kd", [P, T]), sb("g_qi", [P, T]), sb("g_ke", [P, T])
        kend = sb("g_kend", [P, NT, P])
        am = sb("g_am", [P, SEQ + 32])
        S = sb("g_S", [P, C, DV])
        el = sb("g_el", [P, C + DB])
        qb, kb = sb("g_qb", [P, DB, SAMP]), sb("g_kb", [SAMP, DB, P])
        s0, s1 = (x[:, :, :].rearrange("p k t -> p (k t)").bitcast(F32)[:, 0:DB * DV].rearrange(
            "p (b v) -> p b v", b=DB) for x in (core.hhi, core.hlo))
        sqs = sb("g_sqs", [P, DV])
        chunks = lambda x: x[:, 0:SEQ].rearrange("p (c t) -> p c t", t=P)
        seqs = lambda x: x[:, SEQ:T].rearrange("p (b t) -> p b t", t=DS)

        with core.stage() as block:
            @block.sync
            def _(sp):
                def body(h):
                    sp.wait_ge(s_new, since(8 * h))
                    g_read = core.sig("s0_read")
                    sp.wait_ge(g_read, since(h))
                    src = io["state_gla"][0].rearrange("b h k v -> h k b v")
                    sp.dma_start(s0[:, :, :], src[h] if type(h) is int else
                                 src[bass.ds(h, 1)].rearrange("o k b v -> (o k) b v")).then_inc(s0_in, 16)
                    sp.wait_ge(s_new, 8 * h + 8)
                    dst = io["out_gla_s"][0].rearrange("b h k v -> h k b v")
                    sp.dma_start(dst[h] if type(h) is int else dst[bass.ds(h, 1)].rearrange("o k b v -> (o k) b v"),
                                 s1[:, :, :]).then_inc(states_out, 16)
                    sp.wait_ge(state, C * h + C)
                    dst = io["out_gla_p"][0, 0]
                    sp.dma_start(dst[h] if type(h) is int else dst[bass.ds(h, 1)].rearrange("o k v -> (o k) v"),
                                 S[:, C - 1, :]).then_inc(core.sig("state_p_out"), 16)
                run(sp, GH, body)
                sp.wait_ge(states_out, 16 * GH)
                sp.wait_ge(core.sig("state_p_out"), 16 * GH)

            @block.tensor
            def _(pe):
                def body(h):
                    v = lambda i, rows: gla.vr[0:rows, i, bass.ds(h * DV, DV)]
                    pe.wait_ge(prod, 5 * h + 1)
                    pe.wait_ge(kend_ready, since(h))
                    for c in range(C):
                        last = pe.transpose(ps[:, 0, c * P:(c + 1) * P], ke[:, c * P:(c + 1) * P], core.ident)
                    last.then_inc(turned, 1)
                    pe.transpose(ps[0:SAMP, 6, 0:P], ke[:, SEQ:T], core.ident).then_inc(turned, 1)
                    pe.wait_ge(prod, 5 * h + 5)
                    for c in range(C):
                        last = pe.matmul(ps[:, 1, c * P:(c + 1) * P], kd[:, c * P:(c + 1) * P],
                                         qd[:, c * P:(c + 1) * P], start=True, stop=True)
                    last.then_inc(att, 1)
                    pe.matmul(ps[0:SAMP, 7, 0:SAMP], kd[:, SEQ:T], qi[:, SEQ:T], start=True, stop=True).then_inc(att, 1)
                    pe.wait_ge(s_rows, 2 * h + 2)
                    pe.wait_ge(out_taken, since(3 * h))
                    for b in range(DB):
                        last = pe.matmul(ps[:, 2 + b // 2, (b % 2) * DV:(b % 2 + 1) * DV], kb[:, b, :],
                                         v(4, SAMP), start=True, stop=True)
                        if b % 2:
                            last.then_inc(s_kv, 1)
                    pe.wait_ge(core.sig("set"), 2)
                    pe.wait_ge(att_masked, 2 * h + 2)
                    pe.wait_ge(s0_in, 16 * h + 16)
                    o_s = ps[0:SAMP, 6, 256:512]
                    for b in range(DB):
                        pe.matmul(o_s, qb[:, b, :], s0[:, b, :], start=(b == 0), stop=False)
                    pe.matmul(o_s, am[:, SEQ:SEQ + SAMP], v(4, P), start=False, stop=True).then_inc(core.sig("s0_read"), 1)
                    pe.wait_ge(s_new, 8 * h + 8)
                    pe.wait_ge(kend_ready, h + 1)
                    for c in range(C):
                        last = pe.matmul(ps[:, 2 + c // 2, (c % 2) * DV:(c % 2 + 1) * DV], kend[:, c, :], v(c, P),
                                         start=True, stop=True)
                    last.then_inc(kv, 1)
                    for c in range(C):
                        o_c = ps[:, 4 + c // 2, (c % 2) * DV:(c % 2 + 1) * DV]
                        last = pe.matmul(o_c, am[:, c * P:(c + 1) * P], v(c, P), start=True, stop=(c == 0))
                        if c:
                            pe.wait_ge(state, C * h + c)
                            last = pe.matmul(o_c, qi[:, c * P:(c + 1) * P], S[:, c - 1, :], start=False, stop=True)
                        if c % 2:
                            last.then_inc(out, 1)
                run(pe, GH, body)

            @block.scalar
            def _(act):
                def body(h):
                    act.wait_ge(prod, since(5 * h))
                    act.activation(e[:, 2, :], gla.cum[:, h, :], ACT.Exp, scale=1 / 16).then_inc(exped, 1)
                    act.wait_ge(diff, 5 * h + 5)
                    act.activation(e[:, 3, :], d[:, 1, :], ACT.Exp, scale=1 / 16).then_inc(exped, 1)
                    act.activation(e[:, 0, :], d[:, 0, :], ACT.Exp, scale=1 / 16).then_inc(exped, 1)
                    act.activation(e[:, 1, :], d[:, 0, :], ACT.Exp, scale=-1 / 16).then_inc(exped, 1)
                    act.wait_ge(turned, 2 * h + 1)
                    act.wait_ge(kv, since(h))
                    act.copy(kend[:, 0:C, :], ps[:, 0, :].rearrange("p (c k) -> p c k", k=P)).then_inc(kend_ready, 1)
                    for n in range(3):
                        if n == 0:
                            act.wait_ge(core.sig("s0_read"), h + 1)
                            src, rows, t0, nt = ps[0:SAMP, 6, 256:512], SAMP, 4, 1
                        else:
                            act.wait_ge(out, 2 * h + n)
                            src, rows, t0, nt = ps[:, 3 + n, :], P, 2 * n - 2, 2
                        dst = o[0:rows, t0:t0 + nt, bass.ds(h * DV, DV)]
                        act.copy(dst, src.rearrange("p (a c) -> p a c", c=DV)).then_inc(out_taken, 1)
                        act.wait_ge(out_taken, 3 * h + n + 1)
                        for t in range(t0, t0 + nt):
                            act.activation(sqs[0:rows, :], o[0:rows, t, bass.ds(h * DV, DV)], ACT.Square,
                                           accum_out=gla.sumsq[0:rows, t, bass.ds(h, 1)]).then_inc(core.sig("squared"), 1)
                            act.wait_ge(core.sig("squared"), 5 * h + {4: 0, 0: 1, 1: 2, 2: 3, 3: 4}[t] + 1)
                run(act, GH, body)

            @block.vector
            def _(dve):
                dve.memset(gla.sumsq[:, 4, :], 1.0).then_inc(core.sig("set"), 1)
                dve.memset(am[:, SEQ:SEQ + SAMP], 0.0).then_inc(core.sig("set"), 1)

                def body(h):
                    cum = gla.cum[:, h, :]
                    q, k = gla.qk[:, h, :], gla.qk[:, h + GH, :]
                    c3, s3 = chunks(cum), seqs(cum)
                    dve.wait_ge(exped, since(4 * h))
                    k5 = 5 * h
                    dve.tensor_tensor(chunks(d[:, 1, :]), c3[:, :, P - 1:P].broadcast_to([P, C, P]), c3,
                                      ALU.subtract).then_inc(diff, 1)
                    dve.tensor_tensor(seqs(d[:, 1, :]), s3[:, :, DS - 1:DS].broadcast_to([P, DB, DS]), s3,
                                      ALU.subtract).then_inc(diff, 1)
                    dve.tensor_tensor(chunks(d[:, 0, :]), c3, c3[:, :, P // 2 - 1:P // 2].broadcast_to([P, C, P]),
                                      ALU.subtract).then_inc(diff, 1)
                    dve.tensor_copy(d[:, 0, SEQ:T], cum[:, SEQ:T]).then_inc(diff, 1)
                    dve.wait_ge(diff, k5 + 4)
                    dve.tensor_scalar(d[:, 0, :], d[:, 0, :], LIMIT, -LIMIT, ALU.min, ALU.max).then_inc(diff, 1)
                    dve.wait_ge(exped, 4 * h + 1)
                    dve.wait_ge(state, since(C * h))
                    dve.tensor_copy(el[:, 0:C].unsqueeze(2), chunks(e[:, 2, :])[:, :, P - 1:P]).then_inc(core.sig("decays"), 1)
                    dve.tensor_copy(el[:, C:C + DB].unsqueeze(2), seqs(e[:, 2, :])[:, :, DS - 1:DS]).then_inc(core.sig("decays"), 1)
                    dve.wait_ge(out, since(2 * h))
                    dve.wait_ge(exped, 4 * h + 2)
                    dve.tensor_tensor(ke[:, :], k, e[:, 3, :], ALU.mult).then_inc(prod, 1)
                    dve.scalar_tensor_tensor(qi[:, :], q, DK ** -0.5, e[:, 2, :], ALU.mult, ALU.mult).then_inc(prod, 1)
                    dve.wait_ge(prod, 5 * h + 2)
                    dve.tensor_tensor(qb[:, :, :], qi[:, SEQ:T].unsqueeze(1).broadcast_to([P, DB, SAMP]),
                                      core.const[:, C_COLM:C_COLM + DB * SAMP].rearrange(
                                          "p (b c) -> p b c", b=DB), ALU.mult).then_inc(prod, 1)
                    dve.wait_ge(exped, 4 * h + 4)
                    dve.scalar_tensor_tensor(qd[:, :], q, DK ** -0.5, e[:, 0, :], ALU.mult, ALU.mult).then_inc(prod, 1)
                    dve.tensor_tensor(kd[:, :], k, e[:, 1, :], ALU.mult).then_inc(prod, 1)
                    dve.wait_ge(turned, 2 * h + 2)
                    dve.wait_ge(s_kv, since(4 * h))
                    dve.tensor_copy(kend[0:SAMP, C, :], ps[0:SAMP, 6, 0:P]).then_inc(s_rows, 1)
                    dve.wait_ge(s_rows, 2 * h + 1)
                    dve.tensor_tensor(kb[:, :, :], kend[0:SAMP, C:C + 1, :].broadcast_to([SAMP, DB, P]),
                                      core.const[0:SAMP, C_ROW:C_ROW + DB].unsqueeze(2).broadcast_to(
                                          [SAMP, DB, P]), ALU.mult).then_inc(s_rows, 1)
                    dve.wait_ge(att, 2 * h + 1)
                    dve.scalar_tensor_tensor(
                    chunks(am), ps[:, 1, :].rearrange("p (c t) -> p c t", t=P), 3e38,
                    core.const[:, C_TRI1:C_TRI1 + P].unsqueeze(1).broadcast_to([P, C, P]), ALU.min, ALU.mult).then_inc(att_masked, 1)
                    dve.wait_ge(core.sig("set"), 2)
                    dve.wait_ge(att, 2 * h + 2)
                    dve.scalar_tensor_tensor(am[0:SAMP, SEQ:SEQ + SAMP], ps[0:SAMP, 7, 0:SAMP], 3e38,
                                             core.const[0:SAMP, C_ATT:C_ATT + SAMP], ALU.min, ALU.mult).then_inc(att_masked, 1)
                    dve.wait_ge(core.sig("decays"), 2 * h + 2)
                    dve.wait_ge(s0_in, 16 * h + 16)
                    dve.wait_ge(states_out, since(16 * h))
                    for b in range(DB):
                        dve.wait_ge(s_kv, 4 * h + b // 2 + 1)
                        dve.scalar_tensor_tensor(s1[:, b, :], s0[:, b, :], el[:, C + b:C + b + 1],
                                                 ps[:, 2 + b // 2, (b % 2) * DV:(b % 2 + 1) * DV],
                                                 ALU.mult, ALU.add).then_inc(s_new, 1)
                    dve.wait_ge(kv, h + 1)
                    dve.wait_ge(core.sig("state_p_out"), since(16 * h))
                    dve.tensor_copy(S[:, 0, :], ps[:, 2, 0:DV]).then_inc(state, 1)
                    for c in range(1, C):
                        dve.wait_ge(state, C * h + c)
                        dve.scalar_tensor_tensor(S[:, c, :], S[:, c - 1, :], el[:, c:c + 1],
                                                 ps[:, 2 + c // 2, (c % 2) * DV:(c % 2 + 1) * DV],
                                                 ALU.mult, ALU.add).then_inc(state, 1)
                run(dve, GH, body)


def gla_finish(core, gla, o):
    nc, ps = core.nc, core.ps
    names = ("f_var", "f_silu", "f_normed", "f_gated", "f_turned", "f_hi", "f_lo")
    var, silu, normed, gated, turned, f_hi, f_lo = (core.sig(n) for n in names)
    NV = GH * DV
    with core.stage() as block:
        @block.tensor
        def _(pe):
            pe.wait_ge(gated, NT)
            for k in range(KD):
                pe.wait_ge(f_lo, since(2 * (k - 1)))
                for i in range(4):
                    pe.transpose(ps[:, (k % 2) * 2, i * P:(i + 1) * P], o[:, i, k * P:(k + 1) * P], core.ident)
                pe.transpose(ps[:, (k % 2) * 2 + 1, 0:SAMP], o[0:SAMP, 4, k * P:(k + 1) * P],
                             core.ident[0:SAMP, 0:SAMP]).then_inc(turned, 1)

        @block.scalar
        def _(act):
            for i in range(NT):
                act.activation(gla.vr[:, i, NV:2 * NV], gla.vr[:, i, NV:2 * NV], ACT.Silu).then_inc(silu, 1)
            act.wait_ge(var, 1)
            act.activation(gla.sumsq[:, :, :], gla.sumsq[:, :, :], ACT.Sqrt).then_inc(var, 1)
            for k in range(KD):
                act.wait_ge(turned, k + 1)
                act.copy(core.hhi[:, k, 0:SEQ], ps[:, (k % 2) * 2, :]).then_inc(f_hi, 1)
                act.copy(core.hhi[:, k, SEQ:T], ps[:, (k % 2) * 2 + 1, 0:SAMP]).then_inc(f_hi, 1)

        @block.vector
        def _(dve):
            dve.tensor_scalar(gla.sumsq[:, :, :], gla.sumsq[:, :, :], 1.0 / DV, EPS, ALU.mult, ALU.add).then_inc(var, 1)
            dve.wait_ge(var, 2)
            dve.reciprocal(gla.sumsq[:, :, :], gla.sumsq[:, :, :]).then_inc(var, 1)
            dve.wait_ge(var, 3)
            for i in range(NT):
                rows = P if i < 4 else SAMP
                for h in range(GH):
                    x = o[0:rows, i, h * DV:(h + 1) * DV]
                    dve.scalar_tensor_tensor(x, x, gla.sumsq[0:rows, i, h:h + 1], gla.ng[0:rows, :], ALU.mult,
                                             ALU.mult).then_inc(normed, 1)
                dve.wait_ge(silu, i + 1)
                dve.wait_ge(normed, GH * (i + 1))
                dve.tensor_tensor(o[0:rows, i, :], o[0:rows, i, :], gla.vr[0:rows, i, NV:2 * NV], ALU.mult).then_inc(gated, 1)
            for k in range(KD):
                dve.wait_ge(f_hi, 2 * k + 2)
                dve.tensor_tensor(core.hlo[:, k, 0:SEQ], ps[:, (k % 2) * 2, :], core.hhi[:, k, 0:SEQ],
                                  ALU.subtract).then_inc(f_lo, 1)
                dve.tensor_tensor(core.hlo[:, k, SEQ:T], ps[:, (k % 2) * 2 + 1, 0:SAMP], core.hhi[:, k, SEQ:T],
                                  ALU.subtract).then_inc(f_lo, 1)



def write_y(core):
    nc, ps, io = core.nc, core.ps, core.io
    turned, moved_a, moved_d = core.sig("y_turned"), core.sig("y_moved_act"), core.sig("y_moved_dve")
    y_out = [core.sig("y_out0"), core.sig("y_out1")]
    with ExitStack() as own:
        yt = core.sb("y_rows", [P, 2, D], F32, own)
        with core.stage() as block:
            @block.tensor
            def _(pe):
                for i in range(NT):
                    rows = P if i < 4 else SAMP
                    pe.wait_ge(moved_a, since(i - 1))
                    pe.wait_ge(moved_d, since(i - 1))
                    for k in range(KD):
                        last = pe.transpose(ps[0:rows, (i % 2) * 2 + k // 4, (k % 4) * P:(k % 4 + 1) * P],
                                            core.xT[:, k, i * P:i * P + rows], core.ident)
                    last.then_inc(turned, 1)

            def mover(eng, copy, half, moved):
                for i in range(NT):
                    rows = P if i < 4 else SAMP
                    eng.wait_ge(turned, i + 1)
                    eng.wait_ge(y_out[i % 2], since(16 * (i // 2)))
                    copy(yt[0:rows, i % 2, half * 512:half * 512 + 512], ps[0:rows, (i % 2) * 2 + half, :]).then_inc(moved, 1)

            @block.scalar
            def _(act):
                mover(act, act.copy, 0, moved_a)

            @block.vector
            def _(dve):
                mover(dve, dve.tensor_copy, 1, moved_d)

            @block.sync
            def _(sp):
                for i in range(NT):
                    rows = P if i < 4 else SAMP
                    sp.wait_ge(moved_a, i + 1)
                    sp.wait_ge(moved_d, i + 1)
                    dst = io["out_y_p"][0, i * P:(i + 1) * P, :] if i < 4 else \
                        io["out_y_s"].rearrange("b t d -> (b t) d")
                    sp.dma_start(dst, yt[0:rows, i % 2, :]).then_inc(y_out[i % 2], 16)
                sp.wait_ge(y_out[0], 48)
                sp.wait_ge(y_out[1], 32)
                sp.wait_ge(core.rows_out, 16 * (2 + DB))
                sp.wait_ge(core.prompt_rows_out, 16)
                sp.wait_ge(core.window_out, 16 * DB)


def write_rows(core, at, sp):
    io = core.io
    core.rows_out = core.lasting("cache_rows_out")
    core.prompt_rows_out = core.lasting("prompt_rows_out")
    sp.dma_start(io["out_nsa_p"][0, 0].rearrange("(i p) s g d -> p i (s g d)", p=P),
                 at.qkv[:, 0:4, 1024:2048]).then_inc(core.prompt_rows_out, 16)
    sp.dma_start(io["out_nsa_s"][0].rearrange("b t s g d -> (b t) (s g d)"),
                 at.qkv[0:SAMP, 4, 1024:2048]).then_inc(core.rows_out, 16)
    sp.dma_start(io["out_win_p"][0, 0].rearrange("(i p) s g d -> p i (s g d)", p=P),
                 at.qkv[:, 0:4, KW:QKV]).then_inc(core.rows_out, 16)
    for b in range(DB):
        sp.dma_start(io["out_win_s"][0, b, PAST - DS:PAST].rearrange("t s g d -> t (s g d)"),
                     at.qkv[b * DS:b * DS + DS, 4, KW:QKV]).then_inc(core.rows_out, 16)


def program(nc, io):
    with ExitStack() as ctx:
        core = Core(nc, io, ctx)
        weight_streams(core)
        with ExitStack() as norm_ctx:
            core.norm_buffers(norm_ctx)
            setup(core)
            norms(core, None, 0)
        with ExitStack() as nsa:
            cmp = Compressed(core, nsa)
            with ExitStack() as own:
                chunks = core.sb("chunks", [P, 2, 16, 512], F32, own)
                pages = core.sb("chunk_pages", [1, DB * NPAGE], I32, own)
                landed = [core.sig("chunks_in0"), core.sig("chunks_in1")]
                core.window_out = core.lasting("window_out")

                def loads(sp):
                    sp.dma_start(pages[:, :], io["page_table"].rearrange("(o b) n -> o (b n)", o=1)).then_inc(
                        core.sig("chunk_pages_in"), 16)
                    sp.wait_ge(core.sig("chunk_pages_in"), 16)
                    for b in range(DB):
                        for n in range(NPAGE):
                            page = sp.value_load(pages[0:1, b * NPAGE + n:b * NPAGE + n + 1], min_val=0,
                                                 max_val=io["cache_nsa_kv"].shape[1] - 1)
                            p0 = (b % 4) * 32 + n * 8
                            sp.dma_start(chunks[p0:p0 + 8, b // 4, :, :],
                                         io["cache_nsa_kv"][0][bass.ds(page, 1)].rearrange(
                                             "o (c j) s g d -> (o c) j (s g d)", j=16)[:, :, 0:512]).then_inc(
                                landed[b // 4], 16)
                    for b in range(DB):
                        sp.dma_start(io["out_win_s"][0, b, 0:PAST - DS].rearrange("t s g d -> t (s g d)"),
                                     io["state_win_kv"][0, b, DS:PAST].rearrange("t s g d -> t (s g d)")).then_inc(
                            core.window_out, 16)
                compress(core, cmp, [(P, chunks[:, h, :, :], landed[h], 256, 4 * h, 4) for h in range(2)], loads)
            at = Attention(core, nsa)
            token_major(core, 0, at.qkv, roped=(0, 1, 2, 3, 4, 6, 8))
            with ExitStack() as own:
                chunks = core.sb("prompt_chunks", [32, 16, 512], F32, own)

                def loads(sp):
                    write_rows(core, at, sp)
                    sp.wait_ge(core.prompt_rows_out, 16)
                    sp.dma_start(chunks[:, :, :], io["out_nsa_p"][0, 0].rearrange(
                        "(c j) s g d -> c j (s g d)", j=16)[:, :, 0:512]).then_inc(core.sig("prompt_chunks"), 16)
                compress(core, cmp, [(32, chunks[:, :, :], core.sig("prompt_chunks"), 16, DB, 1)], loads)
            with ExitStack() as own:
                kk = core.sb("keys_split", [P, 2, KVH, SEQ], F16, own)
                attention_inputs(core, at, kk)
                prompt_attention(core, at, cmp, kk)
            sample_attention(core, at, cmp)
        with ExitStack() as norm_ctx:
            core.norm_buffers(norm_ctx)
            features_to_y(core, 1, (core.hhi, core.hlo), 1)
            norms(core, 1, 2)
            ffn(core, 0, 2)
            norms(core, 3, 4)
        with ExitStack() as own:
            gla = Gla(core, own)
            gla_heads(core, gla, 4)
            token_major(core, 5, gla.vr)
            o = gla.vr[:, :, 0:GH * DV]
            gla_core(core, gla, o)
            gla_finish(core, gla, o)
        with ExitStack() as norm_ctx:
            core.norm_buffers(norm_ctx)
            features_to_y(core, 6, (core.hhi, core.hlo), 1)
            norms(core, 5, 6)
            ffn(core, 1, 7)
            norms(core, 7, None)
            write_y(core)


_INS = ["x_prompt", "x_sample", "cache_nsa_kv", "state_win_kv", "state_gla", "state_ffn_conv", "page_table",
        "norm_gain", "nsa_w_in", "nsa_cmp_pe", "nsa_cmp_w", "nsa_w_o", "gla_w_in", "gla_w_gate_up", "gla_b_gate",
        "gla_norm_gain", "gla_w_o", "ffn_w_up", "ffn_conv_w", "ffn_conv_b", "ffn_w_down"]
_OUTS = [("out_y_p", (1, SEQ, D)), ("out_y_s", (DB, DS, D)), ("out_nsa_p", (1, 1, SEQ, 4, KVH, DH)),
         ("out_nsa_s", (1, DB, DS, 4, KVH, DH)), ("out_win_p", (1, 1, SEQ, 2, KVH, DH)),
         ("out_win_s", (1, DB, PAST, 2, KVH, DH)), ("out_gla_p", (1, 1, GH, DK, DV)),
         ("out_gla_s", (1, DB, GH, DK, DV)), ("out_ffn_p", (2, 1, 2, F)), ("out_ffn_s", (2, DB, 2, F))]


def kernel(**inputs):
    import numpy as _np
    import concourse.bacc as _bacc
    from concourse import mybir as _mybir
    from concourse.bass_utils import run_bass_kernel_spmd as _run

    nc = _bacc.Bacc("TRN2", target_bir_lowering=False, num_devices=1)
    arrays, io = {}, {}
    for name in _INS + ["consts"]:
        a = constants() if name == "consts" else _np.ascontiguousarray(inputs[name])
        arrays[f"in_{name}"] = a
        io[name] = nc.dram_tensor(f"in_{name}", a.shape, _mybir.dt.from_np(a.dtype), kind="ExternalInput").ap()
    for name, shape in _OUTS:
        io[name] = nc.dram_tensor(name, shape, _mybir.dt.from_np(_np.dtype("float32")), kind="ExternalOutput").ap()
    program(nc, io)
    r = _run(nc, [arrays], core_ids=[0])
    return tuple(r.results[0][name] for name, _ in _OUTS)
```

```python
from contextlib import ExitStack, contextmanager

import numpy as np

import concourse.bass as bass
from concourse import mybir

F32 = mybir.dt.float32
F16 = mybir.dt.float16
BF16 = mybir.dt.bfloat16
I32 = mybir.dt.int32
ALU = mybir.AluOpType
ACT = mybir.ActivationFunctionType
AX = mybir.AxisListType

P = 128
D = 1024
KD = D // P
SEQ = 512
DB, DS = 8, 4
SAMP = DB * DS
T = SEQ + SAMP
HALF = T // 2
NT = 5
PAST = 512
PAGE = 128
NPAGE = PAST // PAGE
HEADS, KVH, GRP, DH = 16, 4, 4, 64
KVW = KVH * DH
NBLK = PAST // 16 - 1
PROJ = HEADS * DH + 6 * KVW + 3 * HEADS
QKV = HEADS * DH + 6 * KVW
GH, DK, DV = 4, 128, 256
GPROJ = 2 * GH * DK + 2 * GH * DV + 16
F = 2816
KF = F // P
SCALE = DH ** -0.5
NEG = -1e30
EPS = 1e-6
STAGE_SEMS = 180
SLOTS = 4
SLOTW = 11 * P

C_ID = 0
C_TRIN = C_ID + P
C_TRI1 = C_TRIN + P
C_CMPP = C_TRI1 + P
C_NEW = C_CMPP + 4 * 32
C_WIN = C_NEW + DB * 32
C_CMPS = C_WIN + 4
C_COS = C_CMPS + P
C_SIN = C_COS + NT * 64
C_SEG = C_SIN + NT * 64
C_ATT = C_SEG + T
C_ROW = C_ATT + SAMP
C_SEL = C_ROW + DB
C_COLM = C_SEL + DS * 64
NCONST = C_COLM + DB * SAMP


def constants():
    c = np.zeros((P, NCONST), np.float32)
    r = np.arange(P)
    c[:, C_ID:C_ID + P] = np.eye(P)
    c[:, C_TRIN:C_TRIN + P] = np.where(r[None] <= r[:, None], 0, NEG)
    c[:, C_TRI1:C_TRI1 + P] = r[:, None] <= r[None]
    n = np.arange(32)
    for i in range(4):
        t = i * P + r
        c[:, C_CMPP + i * 32:C_CMPP + i * 32 + 32] = np.where(
            (16 * n[None] + 31 <= t[:, None]) & (n[None] < NBLK), 0, NEG)
    tok, branch, grp = r % DS, r // 64, (r // 16) % KVH
    for b in range(DB):
        c[:, C_NEW + b * 32:C_NEW + b * 32 + 32] = np.where(
            (n[None] // DS == b) & (n[None] % DS <= tok[:, None]), 0, NEG)
    c[:, C_WIN:C_WIN + 4] = np.where((branch[:, None] == 1) & (np.arange(4)[None] < tok[:, None]), NEG, 0)
    c[:, C_CMPS:C_CMPS + P] = np.where((r[None] // 32 == grp[:, None]) & (r[None] % 32 < NBLK), 0, NEG)
    inv = (10000.0 ** (-np.arange(32, dtype=np.float32) / 32).astype(np.float64)).astype(np.float32)
    for i in range(NT):
        pos = (i * P + r if i < 4 else PAST + r % DS).astype(np.float32)
        ang = (pos[:, None] * inv[None]).astype(np.float32)
        co, si = np.cos(ang.astype(np.float64)), np.sin(ang.astype(np.float64))
        c[:, C_COS + i * 64:C_COS + i * 64 + 64] = np.concatenate([co, co], 1)
        c[:, C_SIN + i * 64:C_SIN + i * 64 + 64] = np.concatenate([-si, si], 1)
    seg = np.ones(T)
    seg[0:SEQ:P] = 0
    seg[SEQ::DS] = 0
    c[:, C_SEG:C_SEG + T] = seg
    s = np.arange(SAMP)
    c[:SAMP, C_ATT:C_ATT + SAMP] = (s[:, None] // DS == s[None] // DS) & (s[:, None] <= s[None])
    c[:, C_ROW:C_ROW + DB] = (r[:, None] // DS) == np.arange(DB)[None]
    c[:, C_COLM:] = (s[None] // DS == np.arange(DB)[:, None]).reshape(1, -1)
    row = np.arange(64)
    for t in range(DS):
        c[:HEADS, C_SEL + t * 64:C_SEL + t * 64 + 64] = (r[:HEADS, None] == row[None] // DS) & (row[None] % DS == t)
    return c


def since(count):
    return max(count, 0) if type(count) is int else count


def run(eng, n, body):
    body(0)
    if n > 3:
        with eng.Fori(1, n - 1) as i:
            body(i)
    else:
        for i in range(1, n - 1):
            body(i)
    if n > 1:
        body(n - 1)


class Core:

    def __init__(self, nc, io, ctx):
        self.nc, self.io, self.ctx = nc, io, ctx
        self.signals, self.names = {}, {}
        self.stage_ctx = ExitStack()
        self.pending = None
        sb = self.sb
        self.const = sb("const", [P, NCONST], F32)
        self.identb = sb("identb", [P, P], BF16)
        self.maskb = sb("maskb", [P, C_COS - C_TRIN], BF16)
        self.ones = sb("ones", [P, P], F32)
        self.gains = sb("gains", [P, KD, 8], F32)
        self.taps = sb("taps", [P, 2, KF, 20], F32)
        self.xT = sb("xT", [P, KD, T], F32)
        self.hhi = sb("hhi", [P, KD, T], F16)
        self.hlo = sb("hlo", [P, KD, T], BF16)
        self.wst = sb("wst", [P, SLOTS, SLOTW], F32)
        self.whi = sb("whi", [P, SLOTS, SLOTW], F16)
        self.wlo = sb("wlo", [P, SLOTS, SLOTW], BF16)
        self.ps = ctx.enter_context(nc.psum_tensor("ps", [P, 8, 512], F32))
        self.ident = self.const[:, C_ID:C_ID + P]
        self.stream = []
        self.w_landed = [self.lasting(f"w_landed{k}") for k in range(SLOTS)]
        self.w_hi = self.lasting("w_hi_ready")
        self.w_lo = self.lasting("w_lo_ready")
        self.w_used = self.lasting("w_used")

    def sb(self, name, shape, dt, ctx=None):
        n = self.names[name] = self.names.get(name, 0) + 1
        return (ctx or self.ctx).enter_context(self.nc.sbuf_tensor(f"{name}_{n}" if n > 1 else name, shape, dt))

    def norm_buffers(self, ctx):
        self.yT = self.sb("yT", [P, KD, T], F32, ctx)
        self.ssq = self.sb("ssq", [P, T], F32, ctx)
        self.rstd = self.sb("rstd", [P, 2, T], F32, ctx)
        self.h = self.sb("h_buffers", [P, 4, T], F32, ctx)
        self.sq = self.h[:, 0:2, :]

    def lasting(self, name):
        return self.ctx.enter_context(self.nc.semaphore(name))

    def sig(self, name):
        if name not in self.signals:
            self.signals[name] = self.stage_ctx.enter_context(
                self.nc.semaphore(name, num=STAGE_SEMS + len(self.signals)))
        return self.signals[name]

    @contextmanager
    def stage(self):
        with self.nc.Block() as block:
            yield block
        self.nc.all_engine_barrier(sems_to_clear=range(STAGE_SEMS, STAGE_SEMS + len(self.signals)))
        self.stage_ctx.close()
        self.signals.clear()
        self.pending = None



def load_block(core, sp, seg, i, k, first):
    _, width, source = core.stream[seg]
    n = i * 4 + k
    sp.wait_ge(core.w_hi, since(first + n - SLOTS + 1))
    sp.wait_ge(core.w_lo, since(first + n - SLOTS + 1))
    src = source(i, k)
    dst = core.wst[:, k, 0:width].rearrange("p (a c) -> p a c", a=src.shape[1])
    sp.dma_start(dst, src).then_inc(core.w_landed[k], 16)


def load_stage(core, sp, seg, first):
    n_blocks = core.stream[seg][0]
    if n_blocks // 4 > 3:
        with sp.Fori(2, n_blocks // 4) as i:
            for k in range(4):
                load_block(core, sp, seg, i, k, first)
    else:
        for i in range(2, n_blocks // 4):
            for k in range(4):
                load_block(core, sp, seg, i, k, first)
    if seg + 1 < len(core.stream):
        for i in range(2):
            for k in range(4):
                if not (i and k in LATE):
                    load_block(core, sp, seg + 1, i, k, first + n_blocks)


LATE = (2, 3)


def late_loads(core, sp):
    if core.pending is not None:
        for k in LATE:
            load_block(core, sp, core.pending, 1, k, core.starts[core.pending])


def late_heads(core, act):
    if core.pending is not None:
        for k in LATE:
            cast_hi(core, act, core.pending, -1, k, core.starts[core.pending])


def late_rests(core, pool):
    if core.pending is not None:
        for k in LATE:
            cast_lo(core, pool, core.pending, -1, k, core.starts[core.pending])


def late(core, seg, i, k):
    return k in LATE and type(i) is int and i == core.stream[seg][0] // 4 - 1


def cast_width(core, seg, i):
    n_blocks, width, _ = core.stream[seg]
    if type(i) is int and i == n_blocks // 4 - 1:
        return core.stream[seg + 1][1] if seg + 1 < len(core.stream) else 0
    return width


def cast_hi(core, act, seg, i, k, first):
    w = cast_width(core, seg, i)
    if not w or late(core, seg, i, k):
        return
    n = first + (i + 1) * 4 + k
    act.wait_ge(core.w_used, since(n - SLOTS + 1))
    act.wait_ge(core.w_landed[k], (n - k) * 4 + 16)
    act.copy(core.whi[:, k, 0:w], core.wst[:, k, 0:w]).then_inc(core.w_hi, 1)


def cast_lo(core, pool, seg, i, k, first):
    w = cast_width(core, seg, i)
    if not w or late(core, seg, i, k):
        return
    n = first + (i + 1) * 4 + k
    pool.wait_ge(core.w_used, since(n - SLOTS + 1))
    pool.wait_ge(core.w_hi, n + 1)
    pool.tensor_tensor(core.wlo[:, k, 0:w], core.wst[:, k, 0:w], core.whi[:, k, 0:w], ALU.subtract
        ).then_inc(core.w_lo, 1)


def weights_ready(core, pe, n):
    pe.wait_ge(core.w_hi, n + 1)
    pe.wait_ge(core.w_lo, n + 1)


def product(pe, out, parts, lhs, rhs, start, stop):
    n = len(parts)
    for j, (ka, kb) in enumerate(parts):
        a_hi, a_lo = lhs(ka)
        b_hi, b_lo = rhs(kb)
        pe.matmul(out, a_hi, b_hi, start=start and j == 0, stop=False)
        pe.matmul(out, a_hi, b_lo, start=False, stop=False)
        last = pe.matmul(out, a_lo, b_hi, start=False, stop=stop and j == n - 1)
    return last


def weight_streams(core):
    io = core.io

    def tokens_major(w, col0):
        def source(i, k):
            return w[(k % 2) * 512:(k % 2) * 512 + 512, bass.ds((i * 2 + k // 2) * 256 + col0, 256)].rearrange(
                "(a p) c -> p a c", p=P)
        return source

    def features(w, col0=0):
        def source(i, k):
            return w[:, bass.ds((i * 4 + k) * P + col0, P)].rearrange("(a p) c -> p a c", p=P)
        return source

    def up(w):
        def source(i, k):
            return w[:, bass.ds((i * 2 + k // 2) * P + (k % 2) * F, P)].rearrange("(a p) c -> p a c", p=P)
        return source

    def down(w):
        def source(i, k):
            r0 = (k % 2) * (F // 2)
            return w[r0:r0 + F // 2, bass.ds((i * 2 + k // 2) * P, P)].rearrange("(a p) c -> p a c", p=P)
        return source

    ffn = [[(2 * KF, 8 * P, up(io["ffn_w_up"][l])), (2 * KD, SLOTW, down(io["ffn_w_down"][l]))] for l in range(2)]
    core.stream = [
        (QKV // P, 8 * P, tokens_major(io["nsa_w_in"][0], 0)),
        (KD, 8 * P, features(io["nsa_w_o"][0])), *ffn[0],
        (2 * GH * DK // P, 8 * P, features(io["gla_w_in"][0])),
        (2 * GH * DV // P, 8 * P, tokens_major(io["gla_w_in"][0], 2 * GH * DK)),
        (KD, 8 * P, features(io["gla_w_o"][0])), *ffn[1]]
    core.starts = [sum(s[0] for s in core.stream[:n]) for n in range(len(core.stream))]



def setup(core, load):
    ps, io = core.ps, core.io
    with ExitStack() as own:
        xtok = core.sb("xtok", [P, NT, D], F32, own)
        rows = core.sb("rows", [20, 2, F], F32, own)
        grow = core.sb("grow", [8, D], F32, own)
        const_in, x_in, gains_in, rows_in = (core.sig(n) for n in ("const_in", "x_in", "gains_in", "rows_in"))
        turned, turned_small, taken, taken_small, filled = (
            core.sig(n) for n in ("x_turned", "small_turned", "x_taken", "small_taken", "constants_filled"))

        with core.stage() as block:
            @block.sync
            def _(sp):
                sp.dma_start(core.const[:, :], io["consts"]).then_inc(const_in, 16)
                for i in range(4):
                    sp.dma_start(xtok[:, i, :], io["x_prompt"][0, i * P:(i + 1) * P, :]).then_inc(x_in, 16)
                sp.dma_start(xtok[0:SAMP, 4, :], io["x_sample"].rearrange("b t d -> (b t) d")).then_inc(x_in, 16)
                sp.dma_start(grow[:, :], io["norm_gain"].rearrange("l n d -> (l n) d")).then_inc(gains_in, 16)
                for k in range(4):
                    load_block(core, sp, 0, 0, k, 0)
                for l in range(2):
                    sp.dma_start(rows[0:3, l, :], io["ffn_conv_w"][l]).then_inc(rows_in, 16)
                    sp.dma_start(rows[3:4, l, :], io["ffn_conv_b"][l:l + 1]).then_inc(rows_in, 16)
                    sp.dma_start(rows[4:20, l, :], io["state_ffn_conv"][l].rearrange("b j f -> (b j) f")
                                 ).then_inc(rows_in, 16)
                for k in range(4):
                    load_block(core, sp, 0, 1, k, 0)
                load(sp)

            @block.tensor
            def _(pe):
                pe.wait_ge(const_in, 16)
                pe.wait_ge(x_in, 80)
                for k in range(KD):
                    b = (k % 2) * 2
                    pe.wait_ge(taken, since(k - 1))
                    pe.wait_ge(taken_small, since(k - 1))
                    for i in range(4):
                        last = pe.transpose(ps[:, b, i * P:(i + 1) * P], xtok[:, i, k * P:(k + 1) * P], core.ident)
                    last.then_inc(turned, 1)
                    pe.transpose(ps[:, b + 1, 0:SAMP], xtok[0:SAMP, 4, k * P:(k + 1) * P],
                                 core.ident[0:SAMP, 0:SAMP]).then_inc(turned_small, 1)
                pe.wait_ge(gains_in, 16)
                for k in range(KD):
                    last = pe.transpose(ps[:, 4, k * 8:k * 8 + 8], grow[:, k * P:(k + 1) * P], core.ident[0:8, 0:8])
                last.then_inc(turned_small, 1)
                pe.wait_ge(rows_in, 96)
                for l in range(2):
                    for m in range(KF):
                        last = pe.transpose(ps[:, 5 + l, m * 20:m * 20 + 20], rows[:, l, m * P:(m + 1) * P],
                                            core.ident[0:20, 0:20])
                    last.then_inc(turned_small, 1)

            @block.scalar
            def _(act):
                for k in range(KD):
                    act.wait_ge(turned, k + 1)
                    act.copy(core.xT[:, k, 0:SEQ], ps[:, (k % 2) * 2, :]).then_inc(taken, 1)
                    if k % 2:
                        cast_hi(core, act, 0, -1, k // 2, 0)

            @block.vector
            def _(dve):
                dve.memset(core.ones[:, :], 1.0).then_inc(filled, 1)
                dve.wait_ge(const_in, 16)
                dve.tensor_copy(core.identb[:, :], core.ident).then_inc(filled, 1)
                dve.tensor_copy(core.maskb[:, :], core.const[:, C_TRIN:C_COS]).then_inc(filled, 1)
                for k in range(KD):
                    dve.wait_ge(turned_small, k + 1)
                    dve.tensor_copy(core.xT[:, k, SEQ:T], ps[:, (k % 2) * 2 + 1, 0:SAMP]).then_inc(taken_small, 1)
                dve.wait_ge(turned_small, KD + 1)
                dve.tensor_copy(core.gains[:, :, :], ps[:, 4, 0:KD * 8].rearrange("p (k g) -> p k g", g=8)
                    ).then_inc(taken_small, 1)
                for l in range(2):
                    dve.wait_ge(turned_small, KD + 2 + l)
                    dve.tensor_copy(core.taps[:, l, :, :], ps[:, 5 + l, 0:KF * 20].rearrange(
                    "p (m r) -> p m r", r=20)).then_inc(taken_small, 1)

            @block.gpsimd
            def _(pool):
                for k in range(4):
                    cast_lo(core, pool, 0, -1, k, 0)



POOL_TILES = (1, 3, 5)


def norms(core, post, pre, load=None):
    ps = core.ps
    xT, yT, sq, rstd, h = core.xT, core.yT, core.sq, core.rstd, core.h
    h_lo_dve = core.sig("h_lo_dve")
    summed, var, log, inverse = (core.sig(n) for n in ("squares_summed", "variance", "log_variance", "rstd_ready"))
    scaled, x_ready, sq_ready, sq_used, h32, h_hi, h_lo = (
        core.sig(n) for n in ("y_scaled", "x_ready", "square_ready", "square_used", "h_ready", "h_hi", "h_lo"))
    scaled_pool = core.sig("y_scaled_pool")
    n_post, n_pre = post is not None, pre is not None

    with core.stage() as block:
        @block.sync
        def _(sp):
            late_loads(core, sp)
            if load:
                load(sp)

        @block.tensor
        def _(pe):
            if n_post:
                for h in range(2):
                    last = pe.matmul(ps[:, h, 0:HALF], core.ones[:, :], core.ssq[:, h * HALF:(h + 1) * HALF],
                                     start=True, stop=True)
                last.then_inc(summed, 1)
            if n_pre:
                for k in range(KD):
                    pe.wait_ge(sq_ready, k + 1)
                    for h in range(2):
                        last = pe.matmul(ps[:, 2 + h, 0:HALF], core.ones[:, :],
                                         sq[:, k % 2, h * HALF:(h + 1) * HALF], start=(k == 0), stop=(k == KD - 1))
                    last.then_inc(sq_used, 1)

        @block.vector
        def _(dve):
            def variance(bank, slot, n):
                dve.tensor_scalar(rstd[:, slot, :].rearrange("p (h c) -> p h c", h=2),
                                  ps[:, bank:bank + 2, 0:HALF], 1.0 / D, EPS, ALU.mult, ALU.add).then_inc(var, 1)
                dve.wait_ge(inverse, n)
            if n_post:
                dve.wait_ge(summed, 1)
                variance(0, 0, 1)
                def add(k):
                    if k in POOL_TILES:
                        dve.wait_ge(scaled_pool, POOL_TILES.index(k) + 1)
                    else:
                        dve.wait_ge(scaled, k + 1 - sum(p < k for p in POOL_TILES))
                    dve.scalar_tensor_tensor(xT[:, k, :], yT[:, k, :], core.gains[:, k, post:post + 1], xT[:, k, :],
                                             ALU.mult, ALU.add).then_inc(x_ready, 1)
                for k in range(KD):
                    if k not in POOL_TILES:
                        dve.tensor_tensor(yT[:, k, :], yT[:, k, :], rstd[:, 0, :], ALU.mult).then_inc(scaled, 1)
                    if k:
                        add(k - 1)
                add(KD - 1)
            if n_pre:
                dve.wait_ge(sq_used, KD)
                variance(2, 1, n_post + 1)
                def rest(k):
                    dve.wait_ge(h_hi, k + 1)
                    dve.tensor_tensor(core.hlo[:, k, :], h[:, k % 4, :], core.hhi[:, k, :], ALU.subtract
                                      ).then_inc(h_lo_dve, 1)
                for k in range(KD):
                    if k >= 4:
                        dve.wait_ge(h_hi, k - 3)
                        dve.wait_ge(h_lo_dve, k // 2 - 1)
                        dve.wait_ge(h_lo, (k - 3) // 2 + (k - 3) % 2)
                    dve.scalar_tensor_tensor(h[:, k % 4, :], xT[:, k, :], core.gains[:, k, pre:pre + 1],
                                             rstd[:, 1, :], ALU.mult, ALU.mult).then_inc(h32, 1)
                    if k >= 3 and k % 2:
                        rest(k - 2)
                rest(KD - 1)

        @block.scalar
        def _(act):
            late_heads(core, act)

            def inverse_root(slot, n):
                act.activation(rstd[:, slot, :], rstd[:, slot, :], ACT.Ln).then_inc(log, 1)
                act.wait_ge(log, n)
                act.activation(rstd[:, slot, :], rstd[:, slot, :], ACT.Exp, scale=-0.5).then_inc(inverse, 1)

            if n_post:
                act.wait_ge(var, 1)
                inverse_root(0, 1)
            if n_pre:
                for k in range(KD):
                    if n_post:
                        act.wait_ge(x_ready, k + 1)
                    act.wait_ge(sq_used, since(k - 1))
                    act.activation(sq[:, k % 2, :], xT[:, k, :], ACT.Square).then_inc(sq_ready, 1)
                act.wait_ge(var, n_post + 1)
                inverse_root(1, n_post + 1)
                for k in range(KD):
                    act.wait_ge(h32, k + 1)
                    act.copy(core.hhi[:, k, :], h[:, k % 4, :]).then_inc(h_hi, 1)

        @block.gpsimd
        def _(pool):
            late_rests(core, pool)
            if n_post:
                pool.wait_ge(inverse, 1)
                for k in POOL_TILES:
                    pool.tensor_tensor(yT[:, k, :], yT[:, k, :], rstd[:, 0, :], ALU.mult).then_inc(scaled_pool, 1)
            if n_pre:
                for k in range(0, KD, 2):
                    pool.wait_ge(h_hi, k + 1)
                    pool.tensor_tensor(core.hlo[:, k, :], h[:, k % 4, :], core.hhi[:, k, :], ALU.subtract
                        ).then_inc(h_lo, 1)



def token_major(core, seg, dest, roped=None):
    ps = core.ps
    first = core.starts[seg]
    groups = core.stream[seg][0] // 2
    ready, taken, rot, t_ready = (core.sig(n) for n in ("rows_ready", "rows_taken", "rotated", "swapped"))
    cleared = core.sig("rows_cleared")
    h = lambda k, i: (core.hhi[:, k, i * P:min(i * P + P, T)], core.hlo[:, k, i * P:min(i * P + P, T)])

    with ExitStack() as own:
        swap = core.sb("swap", [P, NT, 256], F32, own) if roped else None
        with core.stage() as block:
            @block.sync
            def _(sp):
                late_loads(core, sp)
                load_stage(core, sp, seg, first)

            @block.tensor
            def _(pe):
                def body(i):
                    for g in range(2):
                        for k in (2 * g, 2 * g + 1):
                            weights_ready(core, pe, first + 4 * i + k)
                        pe.wait_ge(taken, since((2 * i + g) * 3 - 3))
                        for t in range(NT):
                            rows = P if t < 4 else SAMP
                            out = ps[0:rows, g * 3 + t // 2, (t % 2) * 256:(t % 2) * 256 + 256]
                            last = product(
                                pe, out, [(k, k) for k in range(KD)], lambda k: h(k, t),
                                lambda k: (block_hi(core, 2 * g + k // 4, 256)[:, k % 4, :],
                                           block_lo(core, 2 * g + k // 4, 256)[:, k % 4, :]), True, True)
                            if t in (1, 3):
                                last.then_inc(ready, 1)
                            if t == 4:
                                last.then_inc(core.w_used, 2)
                run(pe, groups // 2, body)

            @block.scalar
            def _(act):
                late_heads(core, act)

                def body(i):
                    for g in range(2):
                        n = 2 * i + g
                        col = n * 256
                        for t in range(3):
                            tiles = 2 if t < 2 else 1
                            rows = P if t < 2 else SAMP
                            if t < 2:
                                act.wait_ge(ready, n * 2 + t + 1)
                            else:
                                act.wait_ge(core.w_used, first + 2 * n + 2)
                            act.copy(dest[0:rows, 2 * t:2 * t + tiles, bass.ds(col, 256)],
                                     ps[0:rows, g * 3 + t, 0:256 * tiles].rearrange("p (a c) -> p a c", c=256)
                                         ).then_inc(taken, 1)
                        for k in (2 * g, 2 * g + 1):
                            cast_hi(core, act, seg, i, k, first)
                act.wait_ge(cleared, 1)
                run(act, groups // 2, body)

            @block.gpsimd
            def _(pool):
                late_rests(core, pool)

                def body(i):
                    for k in range(4):
                        cast_lo(core, pool, seg, i, k, first)
                run(pool, groups // 2, body)

            @block.vector
            def _(dve):
                if not roped:
                    dve.memset(dest[:, 4, :], 0.0).then_inc(cleared, 1)
                else:
                    cos = core.const[:, C_COS:C_SIN].rearrange("p (i d) -> p i d", i=NT)
                    sin = core.const[:, C_SIN:C_SEG].rearrange("p (i d) -> p i d", i=NT)
                    done = 0
                    dve.memset(dest[:, 4, :], 0.0).then_inc(cleared, 1)

                    def rotate(n, count):
                        dve.wait_ge(taken, n * 3 + 3)
                        x = dest[:, :, n * 256:n * 256 + 256]
                        x4 = x.rearrange("p i (h d) -> p i h d", d=DH)
                        s4 = swap[:, :, :].rearrange("p i (h d) -> p i h d", d=DH)
                        sn = sin.unsqueeze(2).broadcast_to([P, NT, 4, 64])
                        cs = cos.unsqueeze(2).broadcast_to([P, NT, 4, 64])
                        dve.wait_ge(rot, since(count))
                        dve.tensor_tensor(s4[:, :, :, 0:32], x4[:, :, :, 32:64], sn[:, :, :, 0:32], ALU.mult)
                        dve.tensor_tensor(s4[:, :, :, 32:64], x4[:, :, :, 0:32], sn[:, :, :, 32:64], ALU.mult
                            ).then_inc(t_ready, 1)
                        dve.wait_ge(t_ready, 2 * count + 1)
                        dve.tensor_tensor(x4, x4, cs, ALU.mult).then_inc(t_ready, 1)
                        dve.wait_ge(t_ready, 2 * count + 2)
                        dve.tensor_tensor(x, x, swap[:, :, :], ALU.add).then_inc(rot, 1)
                    for n in roped:
                        rotate(n, done)
                        done += 1
    core.pending = seg + 1


def block_hi(core, k, cols):
    return core.whi[:, k, 0:1024].rearrange("p (a c) -> p a c", c=cols)


def block_lo(core, k, cols):
    return core.wlo[:, k, 0:1024].rearrange("p (a c) -> p a c", c=cols)



class Compressed:

    def __init__(self, core, ctx):
        self.kcT = core.sb("kcT", [DH, DB + 1, P], F32, ctx)
        self.vcT = core.sb("vcT", [DH, DB + 1, P], F32, ctx)


class Taps:

    def __init__(self, core, ctx, group):
        self.core = core
        self.weight = core.sb("cmp_w", [P, 2, 8, 2, DH], F32, ctx)
        self.pe = core.sb("cmp_pe", [P, 2, 2, 8], F32, ctx)
        self.landed = core.lasting(f"cmp_w_in_{group}")

    def load(self, sp):
        w = self.core.io["nsa_cmp_w"][0]
        for kv in range(2):
            for h in range(2):
                sp.dma_start(self.weight[:, kv, :, h, :], w[kv, h * 16:h * 16 + 16].rearrange(
                    "(a j) d e -> (j d) a e", j=2)).then_inc(self.landed, 16)
            sp.dma_start(self.pe[:, kv, :, :], self.core.io["nsa_cmp_pe"][0, kv].rearrange(
                "(c a j) d -> (j d) c a", c=2, j=2), allow_slow_non_contiguous=True).then_inc(self.landed, 16)


def compress(core, cmp, taps, units, loads=None):
    ps = core.ps
    turned, moved, summed, shifted, combined, biased = (core.sig(n) for n in (
        "taps_turned", "taps_moved", "chunks_summed", "second_shifted", "blocks_combined", "pe_projected"))
    moved_act = core.sig("taps_moved_act")
    cleared = core.sig("cmp_cleared")
    n_q = len(units) * 16
    with ExitStack() as own:
        pairs = core.sb("tap_pairs", [P, 2, 4 * units[0][0]], F32, own)
        second = core.sb("second_half", [DH, 2, 4 * units[0][0]], F32, own)
        bias2 = core.sb("bias_second", [DH, 2], F32, own)
        weight, taps_pe = taps.weight, taps.pe
        bias = core.sb("cmp_bias", [DH, 2], F32, own)
        def move(eng, copy, q, j, signal):
            n = units[q // 16][0]
            eng.wait_ge(turned, q + 1)
            eng.wait_ge(summed, since(q - 1))
            for par in range(2):
                dst = pairs[j * DH:(j + 1) * DH, q % 2, 0:4 * n].rearrange("p (u a n) -> p u a n", u=2, a=2)[:, :, par]
                src = ps[par * DH:(par + 1) * DH, (q % 2) * 2 + j, 0:2 * n].rearrange("p (u n) -> p u n", u=2)
                copy(dst, src).then_inc(signal, 1)

        with core.stage() as block:
            @block.sync
            def _(sp):
                if loads:
                    loads(sp)

            @block.tensor
            def _(pe):
                pe.wait_ge(taps.landed, 96)
                for kv in range(2):
                    for a in range(8):
                        last = pe.matmul(ps[:, 6, kv * 2:kv * 2 + 2],
                                         weight[:, kv, a, :, :].rearrange("p h e -> p (h e)"),
                                         taps_pe[:, kv, :, a], start=(a == 0), stop=(a == 7))
                last.then_inc(biased, 1)

                def turn(q):
                    n, x, landed, value, _, _ = units[q // 16]
                    kv, a = q // 8 % 2, q % 8
                    if q % 16 == 0:
                        pe.wait_ge(landed, value)
                    pe.wait_ge(moved, since(2 * (q - 1)))
                    pe.wait_ge(moved_act, since(2 * (q - 1)))
                    tile, p0 = x(kv)
                    for j in range(2):
                        for u in range(2):
                            last = pe.transpose(ps[:, (q % 2) * 2 + j, u * n:(u + 1) * n],
                                                tile[:, 2 * a + j, u * P:(u + 1) * P],
                                                core.ident[p0:p0 + n, p0:p0 + n])
                    last.then_inc(turned, 1)
                turn(0)
                for q in range(n_q):
                    if q + 1 < n_q:
                        turn(q + 1)
                    n = units[q // 16][0]
                    kv, a, s = q // 8 % 2, q % 8, q // 8
                    if a == 0:
                        pe.wait_ge(combined, since(4 * (s - 1)))
                    pe.wait_ge(moved, 2 * q + 2)
                    pe.wait_ge(moved_act, 2 * q + 2)
                    pe.matmul(ps[:, 4 + s % 2, 0:4 * n], weight[:, kv, a, :, :].rearrange("p h e -> p (h e)"),
                              pairs[:, q % 2, 0:4 * n], start=(a == 0), stop=(a == 7)).then_inc(summed, 1)

            @block.scalar
            def _(act):
                act.wait_ge(biased, 1)
                act.copy(bias2[:, :], ps[DH:P, 6, 1:4:2]).then_inc(shifted, 1)

                def shift(s):
                    n = units[s // 2][0]
                    act.wait_ge(summed, 8 * s + 8)
                    act.wait_ge(combined, since(4 * (s - 1)))
                    act.copy(second[:, s % 2, 0:4 * n], ps[DH:P, 4 + s % 2, 0:4 * n]).then_inc(shifted, 1)
                for q in range(n_q):
                    move(act, act.copy, q, 0, moved_act)
                    if q % 8 == 7 and q > 8:
                        shift(q // 8 - 1)
                shift(n_q // 8 - 1)

            @block.vector
            def _(dve):
                b0 = units[0][4]
                for x in (cmp.kcT, cmp.vcT):
                    dve.memset(x[:, b0:b0 + sum(u[5] for u in units), :], 0.0).then_inc(cleared, 1)
                dve.wait_ge(shifted, 1)
                dve.tensor_tensor(bias[:, :], ps[0:DH, 6, 0:4:2], bias2[:, :], ALU.add).then_inc(cleared, 1)
                dve.wait_ge(cleared, 3)

                def combine(s):
                    n, _, _, _, b0, nb = units[s // 2]
                    kv = s % 2
                    dest = cmp.vcT if kv else cmp.kcT
                    dve.wait_ge(shifted, s + 2)
                    for g in range(KVH):
                        one = ps[0:DH, 4 + s % 2, g * n:(g + 1) * n].rearrange("p (b c) -> p b c", c=32)
                        two = second[:, s % 2, g * n:(g + 1) * n].rearrange("p (b c) -> p b c", c=32)
                        dve.scalar_tensor_tensor(
                        dest[:, b0:b0 + nb, g * 32:g * 32 + NBLK], one[:, :, 0:NBLK], bias[:, kv:kv + 1],
                        two[:, :, 1:NBLK + 1], ALU.add, ALU.add).then_inc(combined, 1)
                for q in range(n_q):
                    move(dve, dve.tensor_copy, q, 1, moved)
                    if q % 8 == 7 and q > 8:
                        combine(q // 8 - 1)
                combine(n_q // 8 - 1)



class Attention:
    def __init__(self, core, ctx):
        self.qkv = core.sb("qkv", [P, NT, QKV], F32, ctx)
        self.qd = self.qkv[:, 0:4, 1024:1024 + SEQ]
        self.gates = core.sb("gates", [P, NT, 48], F32, ctx)
        self.qs = core.sb("q_sample", [DH, DB, 64], F32, ctx)
        self.qblk = core.sb("q_blocks", [P, DB, 2, 64], F32, ctx)
        self.gate_rows = core.sb("gate_rows", [P, DB, 2], F32, ctx)
        self.kTn = core.sb("new_keys", [P, 2, 2, SAMP], F32, ctx)

KS, VS, KW, VW = 1536, 1792, 2048, 2304


def attention_inputs(core, at, kk, transfers):
    ps, io = core.ps, core.io
    gw_cast, gates_summed, gates_done = core.sig("gate_w_cast"), core.sig("gates_summed"), core.sig("gates_done")
    keys_turned, keys_hi, keys_lo = core.sig("keys_turned"), core.sig("keys_hi"), core.sig("keys_lo")
    q_turned, q_moved, zeroed, g_turned, g_moved = (
        core.sig(n) for n in ("qs_turned", "qs_moved", "qblk_zeroed", "gates_turned", "gates_moved"))
    with ExitStack() as own:
        gT = core.sb("gates_turned", [HEADS, 3, SAMP], F32, own)
        gs = core.sb("gates_contig", [SAMP, 3, HEADS], F32, own)
        gw = core.sb("gate_w", [P, KD, 48], F32, own)
        gwhi, gwlo = core.sb("gate_w_hi", [P, KD, 48], F16, own), core.sb("gate_w_lo", [P, KD, 48], BF16, own)
        with core.stage() as block:
            @block.sync
            def _(sp):
                sp.dma_start(gw[:, :, :], io["nsa_w_in"][0][:, QKV:PROJ].rearrange("(k p) c -> p k c", p=P)
                             ).then_inc(core.sig("gate_w_in"), 16)
                late_loads(core, sp)
                transfers(sp)

            @block.tensor
            def _(pe):
                for n in range(8):
                    y, g = n // 4, n % 4
                    col = (KS, KW)[y] + g * DH
                    pe.wait_ge(keys_lo, since(n - 3))
                    for i in range(4):
                        last = pe.transpose(ps[0:DH, n % 4, i * P:(i + 1) * P], at.qkv[:, i, col:col + DH], core.ident)
                    last.then_inc(keys_turned, 1)
                pe.wait_ge(gw_cast, 2)
                for t in range(NT):
                    rows = P if t < 4 else SAMP
                    last = product(pe, ps[0:rows, 4, t * 48:t * 48 + 48], [(k, k) for k in range(KD)],
                                   lambda k: (core.hhi[:, k, t * P:t * P + rows], core.hlo[:, k, t * P:t * P + rows]),
                                   lambda k: (gwhi[:, k, :], gwlo[:, k, :]), True, True)
                last.then_inc(gates_summed, 1)
                for h in range(HEADS):
                    last = pe.transpose(ps[0:DH, 5, h * SAMP:(h + 1) * SAMP],
                                        at.qkv[0:SAMP, 4, h * DH:(h + 1) * DH], core.ident[0:SAMP, 0:SAMP])
                last.then_inc(q_turned, 1)
                for y in range(2):
                    for u in range(2):
                        col = (KS, KW)[y] + u * P
                        last = pe.transpose(ps[:, 6, (y * 2 + u) * SAMP:(y * 2 + u + 1) * SAMP],
                                            at.qkv[0:SAMP, 4, col:col + P], core.ident[0:SAMP, 0:SAMP])
                last.then_inc(q_turned, 1)
                pe.wait_ge(gates_done, 4)
                for c in range(3):
                    last = pe.transpose(ps[0:HEADS, 7, c * SAMP:(c + 1) * SAMP], gs[:, c, :],
                                        core.ident[0:SAMP, 0:SAMP])
                last.then_inc(g_turned, 1)
                pe.wait_ge(g_moved, 1)
                for c in range(3):
                    for t in range(DS):
                        rows = slice(64, P) if c == 2 else slice(0, 64)
                        col = 128 + (8 if c == 0 else 0)
                        last = pe.matmul(ps[rows, 7, col:col + DB],
                                         core.const[0:HEADS, C_SEL + t * 64:C_SEL + t * 64 + 64],
                                         gT[:, c, :].rearrange("p (b t) -> p b t", t=DS)[:, :, t],
                                         start=(t == 0), stop=(t == DS - 1))
                last.then_inc(g_turned, 1)

            @block.scalar
            def _(act):
                late_heads(core, act)
                act.wait_ge(core.sig("gate_w_in"), 16)
                act.wait_ge(zeroed, 1)
                act.copy(gwhi[:, :, :], gw[:, :, :]).then_inc(gw_cast, 1)
                for n in range(8):
                    act.wait_ge(keys_turned, n + 1)
                    act.copy(kk[0:DH, n // 4, n % 4, :], ps[0:DH, n % 4, :]).then_inc(keys_hi, 1)
                act.wait_ge(gates_summed, 1)
                act.activation(at.gates[:, 0:4, :], ps[:, 4, 0:192].rearrange("p (t c) -> p t c", c=48),
                               ACT.Exp, scale=-1.0).then_inc(gates_done, 1)
                act.activation(at.gates[0:SAMP, 4, :], ps[0:SAMP, 4, 192:240], ACT.Exp, scale=-1.0
                    ).then_inc(gates_done, 1)

            @block.vector
            def _(dve):
                dve.memset(at.gates[:, 4, :], 0.0).then_inc(zeroed, 1)
                dve.memset(at.gate_rows[:, :, :], 0.0).then_inc(zeroed, 1)
                dve.memset(at.qblk[:, :, :, :], 0.0).then_inc(zeroed, 1)
                dve.wait_ge(gw_cast, 1)
                dve.tensor_tensor(gwlo[:, :, :], gw[:, :, :], gwhi[:, :, :], ALU.subtract).then_inc(gw_cast, 1)
                for n in range(8):
                    dve.wait_ge(keys_hi, n + 1)
                    dve.tensor_tensor(kk[DH:P, n // 4, n % 4, :], ps[0:DH, n % 4, :], kk[0:DH, n // 4, n % 4, :],
                                      ALU.subtract).then_inc(keys_lo, 1)
                dve.wait_ge(q_turned, 1)
                dve.tensor_copy(at.qs[:, :, :].rearrange("p b (h t) -> p h b t", t=DS),
                                ps[0:DH, 5, :].rearrange("p (h b t) -> p h b t", h=HEADS, b=DB)).then_inc(q_moved, 1)
                dve.wait_ge(q_turned, 2)
                dve.tensor_copy(at.kTn[:, :, :, :], ps[:, 6, 0:4 * SAMP].rearrange(
                "p (y u c) -> p y u c", y=2, u=2)).then_inc(q_moved, 1)
                dve.wait_ge(q_moved, 1)
                dve.wait_ge(zeroed, 3)
                for g in range(KVH):
                    p0 = (g % 2) * DH
                    dve.tensor_copy(at.qblk[p0:p0 + DH, :, g // 2, g * 16:g * 16 + 16],
                                    at.qs[:, :, g * 16:g * 16 + 16]).then_inc(q_moved, 1)
                dve.wait_ge(gates_done, 2)
                dve.tensor_scalar(at.gates[:, :, :], at.gates[:, :, :], 1.0, None, ALU.add).then_inc(gates_done, 1)
                dve.wait_ge(gates_done, 3)
                dve.reciprocal(at.gates[:, :, :], at.gates[:, :, :]).then_inc(q_moved, 1)
                dve.wait_ge(q_moved, 7)
                dve.tensor_copy(gs[:, :, :], at.gates[0:SAMP, 4, :].rearrange("p (h c) -> p c h", c=3)
                    ).then_inc(gates_done, 1)
                dve.wait_ge(g_turned, 1)
                dve.tensor_copy(gT[:, :, :], ps[0:HEADS, 7, 0:3 * SAMP].rearrange("p (c n) -> p c n", c=3)
                    ).then_inc(g_moved, 1)
                dve.wait_ge(g_turned, 2)
                dve.tensor_copy(at.gate_rows[:, :, 0], ps[:, 7, 128:128 + DB]).then_inc(g_moved, 1)
                dve.tensor_copy(at.gate_rows[0:64, :, 1], ps[0:64, 7, 136:136 + DB]).then_inc(g_moved, 1)

            @block.gpsimd
            def _(pool):
                late_rests(core, pool)
                pool.wait_ge(core.prompt_rows_out, 16)
                for u in range(2):
                    pool.tensor_copy(at.qd.rearrange("p i (h u d) -> p i h u d", u=2, d=DH)[:, :, :, u, :],
                                     at.qkv[:, 0:4, 0:256].rearrange("p i (h d) -> p i h d", d=DH)
                                     ).then_inc(core.sig("q_doubled"), 1)



def prompt_attention(core, at, cmp, kk):
    ps = core.ps
    names = ("q_staged", "v_staged", "kc_hi", "kc_lo", "vc_staged", "qT_turned", "q_hi", "q_lo", "vc_turned",
             "vc_by_tile", "cmp_scored", "cmp_step", "cmp_recip", "exp_cmp", "cmp_turned", "cmp_moved", "cmp_out",
             "out_set", "scored", "maxed", "shifts_ready", "keys_scored", "exp_done", "attended", "coef_step",
             "parts_taken", "parts_added", "out_turned", "out_hi", "out_lo", "tables_set")
    (q_staged, v_staged, kc_hi, kc_lo, vc_staged, qT_turned, q_hi, q_lo, vc_turned, vc_by_tile, cmp_scored, cmp_step,
     cmp_recip, exp_cmp, cmp_turned, cmp_moved, cmp_out, out_set, scored, maxed, shifts_ready, keys_scored, exp_done,
     attended, coef_step, parts_taken, parts_added, out_turned, out_hi, out_lo, tables_set) = (
        core.sig(n) for n in names)
    trin = core.maskb[:, 0:P]
    cmpp = core.maskb[:, C_CMPP - C_TRIN:C_NEW - C_TRIN]
    U = 16
    VD = DH + 1
    MAXB = (4, 7)
    OUTB = 5
    first = lambda g: type(g) is int and g == 0
    with ExitStack() as own:
        sb = lambda n, s, t=F32: core.sb(n, s, t, own)
        qd = at.qd
        vg = sb("v_group", [P, 4, 2, VD])
        qh, ql = sb("q_heads", [P, 4, SEQ], F16), sb("q_rests", [P, 4, SEQ], BF16)
        kcc, vcx, vcz = sb("kc_split", [P, 32], F16), sb("vc_repeated", [DH, 4, 32]), sb("vc_by_tile", [P, 4, DH])
        mc, sc = sb("max_cmp", [P, U]), sb("sum_cmp", [P, U])
        onesb, nident = sb("ones_bf16", [P, P], BF16), sb("neg_ident", [P, P], BF16)
        mx, shift = sb("row_max", [P, 2, 2, 4]), sb("shifts", [P, 2, 2, SEQ], BF16)
        pT = sb("prob_T", [P, 2, 4, SEQ])
        coef = sb("coef", [P, 2, 4])
        part = at.qkv[:, 0:4, KS:VS].rearrange("p i (u y d) -> p u y i d", u=2, y=2)
        shared = sb("cmp_then_out", [P, 4, 256])
        pc = shared[:, 0:2, :].rearrange("p a (u n) -> p (a u) n", n=32)
        pcT = shared[:, 2:4, :].rearrange("p a (h t) -> p (a h) t", t=P)
        og = shared[:, :, :]

        with core.stage() as block:
            @block.tensor
            def _(pe):
                def turn_out(g):
                    pe.wait_ge(parts_added, 8 * g)
                    for a in range(2):
                        for i in range(4):
                            last = pe.transpose(ps[:, MAXB[a], i * P:(i + 1) * P], og[:, i, a * P:(a + 1) * P],
                                                core.ident)
                        last.then_inc(out_turned, 1)

                def row_scores(g, hh, i):
                    n = 4 * g + hh
                    w = (i + 1) * P
                    for y in range(2):
                        pe.wait_ge(maxed, since(8 * n + 2 * i + y - 1))
                        out = ps[:, MAXB[y], :]
                        pe.matmul(out[:, i * P:w], core.identb[:, :], trin, start=True, stop=False)
                        last = pe.matmul(out[:, i * P:w], qh[0:DH, hh, i * P:w], kk[0:DH, y, g, i * P:w],
                                         start=False, stop=True)
                        if i:
                            last = pe.matmul(out[:, 0:i * P], qh[0:DH, hh, i * P:w], kk[0:DH, y, g, 0:i * P],
                                             start=True, stop=True)
                        last.then_inc(scored, 1)

                def key_scores(g, hh, j):
                    n = 4 * g + hh
                    if j == 0:
                        pe.wait_ge(shifts_ready, 8 * n + 8)
                    pe.wait_ge(exp_done, since(4 * n + j - 1))
                    for y in range(2):
                        out = ps[:, (j % 2) * 2 + y, j * P:SEQ]
                        keys = kk[:, y, g, j * P:(j + 1) * P]
                        pe.matmul(out, onesb[:, :], shift[:, hh % 2, y, j * P:SEQ], start=True, stop=False)
                        pe.matmul(out, keys, qh[:, hh, j * P:SEQ], start=False, stop=False)
                        pe.matmul(out, keys, ql[:, hh, j * P:SEQ], start=False, stop=False)
                        last = pe.matmul(ps[:, (j % 2) * 2 + y, j * P:(j + 1) * P], trin, core.identb[:, :],
                                         start=False, stop=True)
                    last.then_inc(keys_scored, 1)

                def body(g):
                    pe.wait_ge(q_staged, since(g))
                    pe.wait_ge(exp_done, since(16 * g))
                    for hh in range(4):
                        for i in range(4):
                            last = pe.transpose(ps[:, hh, i * P:(i + 1) * P], qd[:, i, hh * P:(hh + 1) * P],
                                                core.ident)
                        last.then_inc(qT_turned, 1)
                    if not first(g):
                        turn_out(g)
                    pe.wait_ge(parts_taken, since(4 * g))
                    pe.wait_ge(vc_staged, g + 1)
                    pe.matmul(ps[:, OUTB, :].rearrange("p (h c) -> p h c", h=4), core.identb[:, :],
                              cmpp.unsqueeze(1).broadcast_to([P, 4, P]), start=True, stop=False)
                    pe.transpose(ps[:, OUTB + 1, 0:DH], vcx[:, :, :].rearrange("p i n -> p (i n)"),
                                 core.ident[0:DH, 0:DH]).then_inc(vc_turned, 1)
                    pe.wait_ge(kc_lo, g + 1)
                    pe.wait_ge(q_hi, 4 * g + 4)
                    pe.wait_ge(q_lo, 4 * g + 4)
                    for u in range(U):
                        for q in (qh, ql):
                            last = pe.matmul(ps[:, OUTB, u * 32:u * 32 + 32], q[:, u // 4, (u % 4) * P:(u % 4 + 1) * P],
                                             kcc[:, :], start=False, stop=(u == U - 1 and q is ql))
                    last.then_inc(cmp_scored, 1)
                    pe.wait_ge(out_lo, since(2 * g))
                    for i in range(4):
                        row_scores(g, 0, i)
                    key_scores(g, 0, 0)
                    row_scores(g, 1, 0)
                    pe.wait_ge(vc_by_tile, 4 * g + 4)
                    pe.wait_ge(cmp_step, 5 * g + 5)
                    for hh in range(4):
                        last = pe.transpose(ps[:, OUTB + 1, hh * P:(hh + 1) * P],
                                            pc[:, hh * 4:hh * 4 + 4, :].rearrange("p u n -> p (u n)"), core.ident)
                    last.then_inc(cmp_turned, 1)
                    key_scores(g, 0, 1)
                    row_scores(g, 1, 1)
                    pe.wait_ge(cmp_moved, g + 1)
                    for hh in range(4):
                        last = pe.matmul(ps[:, OUTB + hh // 2, (hh % 2) * 256:(hh % 2) * 256 + 256], pcT[:, hh, :],
                                         vcz[:, :, :].rearrange("p i d -> p (i d)"), start=True, stop=True)
                    last.then_inc(cmp_out, 1)
                    pe.wait_ge(v_staged, 2 * g + 2)
                    for hh in range(4):
                        n = 4 * g + hh
                        for j in range(4):
                            if hh == 0 and j < 2:
                                continue
                            key_scores(g, hh, j)
                            if hh < 3:
                                row_scores(g, hh + 1, j)
                        if hh == 0:
                            pe.wait_ge(out_set, 2 * g + 2)
                        else:
                            pe.wait_ge(parts_taken, n)
                        for i in range(4):
                            pe.wait_ge(exp_done, 4 * n + i + 1)
                            for y in range(2):
                                for j in range(i + 1):
                                    last = pe.matmul(ps[:, OUTB + y, i * VD:(i + 1) * VD],
                                                     pT[:, y, j, i * P:(i + 1) * P], vg[:, j, y, :],
                                                     start=(j == 0), stop=(j == i))
                        last.then_inc(attended, 1)
                pe.wait_ge(tables_set, 3)
                run(pe, KVH, body)
                turn_out(KVH)

            @block.scalar
            def _(act):
                def heads_of_out(g):
                    for a in range(2):
                        act.wait_ge(out_turned, 2 * g + a - 1)
                        act.copy(core.hhi[:, 2 * g + a - 2, 0:SEQ], ps[:, MAXB[a], :]).then_inc(out_hi, 1)

                def body(g):
                    act.wait_ge(cmp_scored, since(g))
                    act.copy(kcc[0:DH, :], cmp.kcT[:, DB, bass.ds(g * 32, 32)]).then_inc(kc_hi, 1)
                    for hh in range(4):
                        act.wait_ge(qT_turned, 4 * g + hh + 1)
                        act.copy(qh[:, hh, :], ps[:, hh, :]).then_inc(q_hi, 1)
                    if not first(g):
                        heads_of_out(g)
                    act.wait_ge(cmp_step, 5 * g + 3)
                    act.activation(pc[:, :, :], pc[:, :, :], ACT.Exp, scale=SCALE).then_inc(exp_cmp, 1)

                    def expo(hh, j):
                        n = 4 * g + hh
                        act.wait_ge(keys_scored, 4 * n + j + 1)
                        act.wait_ge(attended, since(n))
                        b = (j % 2) * 2
                        act.activation(pT[:, :, j, j * P:SEQ], ps[:, b:b + 2, j * P:SEQ], ACT.Exp, scale=SCALE
                                       ).then_inc(exp_done, 1)
                    expo(0, 0)
                    expo(0, 1)
                    act.wait_ge(cmp_out, g + 1)
                    act.wait_ge(out_turned, since(2 * g))
                    for a in range(2):
                        act.copy(og[:, :, a * P:(a + 1) * P].rearrange("p i (h d) -> p h i d", d=DH),
                                 ps[:, OUTB + a, :].rearrange("p (h i d) -> p h i d", h=2, d=DH)
                                 ).then_inc(out_set, 1)
                    for hh in range(4):
                        for j in range(4):
                            if hh or j > 1:
                                expo(hh, j)
                run(act, KVH, body)
                heads_of_out(KVH)

            @block.vector
            def _(dve):
                dve.memset(onesb[:, :], 1.0).then_inc(tables_set, 1)
                dve.tensor_scalar(nident[:, :], core.identb[:, :], -1.0, None, ALU.mult).then_inc(tables_set, 1)
                dve.memset(vcz[:, :, :], 0.0).then_inc(tables_set, 1)
                dve.wait_ge(tables_set, 3)

                def rests_of_out(g):
                    for a in range(2):
                        dve.wait_ge(out_hi, 2 * g + a - 1)
                        dve.tensor_tensor(core.hlo[:, 2 * g + a - 2, 0:SEQ], ps[:, MAXB[a], :],
                                          core.hhi[:, 2 * g + a - 2, 0:SEQ], ALU.subtract).then_inc(out_lo, 1)

                def body(g):
                    dve.wait_ge(vc_turned, since(g))
                    dve.tensor_copy(vcx[:, :, :], cmp.vcT[:, DB, bass.ds(g * 32, 32)].unsqueeze(1)
                                    .broadcast_to([DH, 4, 32])).then_inc(vc_staged, 1)
                    dve.wait_ge(kc_hi, g + 1)
                    dve.tensor_tensor(kcc[DH:P, :], cmp.kcT[:, DB, bass.ds(g * 32, 32)], kcc[0:DH, :],
                                      ALU.subtract).then_inc(kc_lo, 1)
                    for hh in range(4):
                        dve.wait_ge(q_hi, 4 * g + hh + 1)
                        dve.tensor_tensor(ql[:, hh, :], ps[:, hh, :], qh[:, hh, :], ALU.subtract).then_inc(q_lo, 1)
                    dve.wait_ge(vc_turned, g + 1)
                    for i in range(4):
                        rows = slice(i * 32, i * 32 + 32)
                        dve.tensor_copy(vcz[rows, i, :], ps[rows, OUTB + 1, 0:DH]).then_inc(vc_by_tile, 1)
                    dve.wait_ge(cmp_scored, g + 1)
                    s3 = ps[:, OUTB, :].rearrange("p (u n) -> p u n", n=32)
                    dve.tensor_reduce(mc[:, :], s3, AX.X, ALU.max).then_inc(cmp_step, 1)
                    dve.wait_ge(cmp_step, 5 * g + 1)
                    dve.tensor_scalar(mc[:, :], mc[:, :], NEG / 10, None, ALU.max).then_inc(cmp_step, 1)
                    dve.wait_ge(cmp_step, 5 * g + 2)
                    dve.tensor_tensor(pc[:, :, :], s3, mc[:, :].unsqueeze(2).broadcast_to([P, U, 32]),
                                      ALU.subtract).then_inc(cmp_step, 1)
                    if not first(g):
                        rests_of_out(g)

                    def shifts(hh, i):
                        n, w = 4 * g + hh, (i + 1) * P
                        dve.wait_ge(attended, since(n - 1))
                        for y in range(2):
                            dve.wait_ge(scored, 8 * n + 2 * i + y + 1)
                            dve.tensor_reduce(mx[:, hh % 2, y, i:i + 1], ps[:, MAXB[y], 0:w], AX.X, ALU.max
                                              ).then_inc(maxed, 1)
                        for y in range(2):
                            dve.wait_ge(maxed, 8 * n + 2 * i + y + 1)
                            dve.tensor_scalar(shift[:, hh % 2, y, i * P:w], nident[:, :], mx[:, hh % 2, y, i:i + 1],
                                              None, ALU.mult).then_inc(shifts_ready, 1)

                    def combine(hh):
                        n = 4 * g + hh
                        dve.wait_ge(attended, n + 1)
                        dve.wait_ge(parts_taken, since(n))
                        dve.wait_ge(parts_added, since(2 * (n - 1)))
                        both = ps[:, OUTB:OUTB + 2, 0:4 * VD].rearrange("p y (i c) -> p y i c", c=VD)
                        dve.tensor_scalar(coef[:, :, :], both[:, :, :, DH], 1e-30, None, ALU.max
                            ).then_inc(coef_step, 1)
                        dve.wait_ge(coef_step, 3 * n + 1)
                        dve.reciprocal(coef[:, :, :], coef[:, :, :]).then_inc(coef_step, 1)
                        dve.wait_ge(coef_step, 3 * n + 2)
                        dve.tensor_tensor(coef[:, :, :], coef[:, :, :],
                                          at.gates[:, 0:4, bass.ds(g * 12 + hh * 3 + 1, 2)].rearrange("p i y -> p y i"),
                                          ALU.mult).then_inc(coef_step, 1)
                        dve.wait_ge(coef_step, 3 * n + 3)
                        dve.tensor_tensor(part[:, hh % 2, :, :, :], both[:, :, :, 0:DH],
                                          coef[:, :, :].unsqueeze(3).broadcast_to([P, 2, 4, DH]), ALU.mult
                                          ).then_inc(parts_taken, 1)
                    for i in range(4):
                        shifts(0, i)
                    dve.wait_ge(exp_cmp, g + 1)
                    dve.tensor_reduce(sc[:, :], pc[:, :, :], AX.X, ALU.add).then_inc(cmp_step, 1)
                    dve.wait_ge(cmp_step, 5 * g + 4)
                    dve.tensor_scalar(sc[:, :], sc[:, :], 1e-30, None, ALU.max).then_inc(cmp_recip, 1)
                    dve.wait_ge(cmp_recip, 3 * g + 1)
                    dve.reciprocal(sc[:, :], sc[:, :]).then_inc(cmp_recip, 1)
                    dve.wait_ge(cmp_recip, 3 * g + 2)
                    dve.tensor_tensor(
                        sc[:, :].rearrange("p (h i) -> p h i", i=4), sc[:, :].rearrange("p (h i) -> p h i", i=4),
                        at.gates[:, 0:4, bass.ds(g * 12, 12)].rearrange("p i (h c) -> p h i c", c=3)[:, :, :, 0],
                        ALU.mult).then_inc(cmp_recip, 1)
                    dve.wait_ge(cmp_recip, 3 * g + 3)
                    dve.tensor_tensor(pc[:, :, :], pc[:, :, :], sc[:, :].unsqueeze(2).broadcast_to([P, U, 32]),
                                      ALU.mult).then_inc(cmp_step, 1)
                    shifts(1, 0)
                    dve.wait_ge(cmp_turned, g + 1)
                    dve.tensor_copy(pcT[:, :, :], ps[:, OUTB + 1, :].rearrange("p (h t) -> p h t", h=4)
                                    ).then_inc(cmp_moved, 1)
                    for hh in range(4):
                        if hh < 3:
                            for i in range(1 if hh == 0 else 0, 4):
                                shifts(hh + 1, i)
                        combine(hh)
                run(dve, KVH, body)
                rests_of_out(KVH)

            @block.gpsimd
            def _(pool):
                q4 = lambda g: at.qkv[:, 0:4, bass.ds(g * 256, 256)].rearrange("p i (h d) -> p i h d", d=DH)
                qd4 = qd.rearrange("p i (h u d) -> p i h u d", u=2, d=DH)

                def stage_q(g):
                    pool.wait_ge(qT_turned, since(4 * g))
                    pool.tensor_copy(qd4[:, :, :, 0, :], q4(g)).then_inc(q_doubled, 1)
                    pool.tensor_copy(qd4[:, :, :, 1, :], q4(g)).then_inc(q_staged, 1)
                q_doubled = core.sig("q_doubled")
                pool.memset(vg[:, :, :, DH:VD], 1.0).then_inc(core.sig("ones_set"), 1)
                def body(g):
                    pool.wait_ge(attended, since(4 * g))
                    for y in range(2):
                        v = at.qkv[:, 0:4, bass.ds(g * DH + (VS, VW)[y], DH)]
                        pool.tensor_copy(vg[:, :, y, 0:DH], v).then_inc(v_staged, 1)
                    for hh in range(4):
                        n = 4 * g + hh
                        pool.wait_ge(out_set, 2 * g + 2)
                        pool.wait_ge(parts_taken, n + 1)
                        for y in range(2):
                            o = og[:, :, hh * DH:(hh + 1) * DH]
                            pool.wait_ge(parts_added, since(2 * n + y))
                            pool.tensor_tensor(o, o, part[:, hh % 2, y, :, :], ALU.add).then_inc(parts_added, 1)
                        if hh == 0 and not (type(g) is int and g == KVH - 1):
                            stage_q(g + 1)
                run(pool, KVH, body)



def sample_attention(core, at, cmp):
    ps, io = core.ps, core.io
    names = ("page_in", "vc_turned", "vc_moved", "keys_filled", "k_landed", "v_landed0", "v_landed1", "k_turned",
             "kT_moved_dve", "kT_moved_act", "rows_staged", "v_staged", "s_scored", "s_max", "s_exp", "s_sum",
             "s_scaled", "s_turned", "s_moved", "s_attended", "s_out", "s_spread", "s_hi", "s_lo")
    (page_in, vc_turned, vc_moved, keys_filled, k_landed, v_landed0, v_landed1, k_turned, kT_dve, kT_act, staged,
     v_staged, scored, maxed, exped, summed, scaled, turned, moved, attended, out_taken, spread, s_hi, s_lo) = (
        core.sig(n) for n in names)
    v_landed = (v_landed0, v_landed1)
    moved_act = core.sig("s_moved_act")
    trin0 = C_TRIN
    before_end = lambda b, n: not (type(b) is int and b + n >= DB)
    with ExitStack() as own:
        sb = lambda n, s: core.sb(n, s, F32, own)
        pages = core.sb("pages", [1, DB * NPAGE], I32, own)
        kn, vn = sb("k_rows", [P, 2, NPAGE, 256]), sb("v_rows", [P, 2, 2, NPAGE, 256])
        kTb = sb("kT_batch", [P, 2, 2, T])
        qst, qcs, vcs = sb("q_stage", [P, 2, 64]), sb("qc_stage", [DH, P]), sb("vc_stage", [P, 2, DH])
        prob, pcs = sb("s_prob", [P, T]), sb("s_pcmp", [64, P])
        pT, pcT = sb("s_probT", [P, 5, P]), sb("s_pcmpT", [P, 64])
        mx2, mx = sb("s_max2", [P, 2]), sb("s_mx", [P, 2])
        sums, coef = sb("s_sums", [P, 2]), sb("s_coef", [P, 2])
        vc = sb("vc", [P, DB, DH])
        outs, oT = sb("s_outs", [P, DB, 64]), sb("s_oT", [P, KD, SAMP])

        with core.stage() as block:
            @block.sync
            def _(sp):
                sp.dma_start(pages[:, :], io["page_table"].rearrange("(o b) n -> o (b n)", o=1)).then_inc(
                    page_in, 16)
                sp.wait_ge(page_in, 16)

                def body(i):
                    for par in range(2):
                        b = 2 * i + par
                        ids = [sp.value_load(pages[0:1, bass.ds(b * NPAGE + n, 1)], min_val=0,
                                             max_val=io["cache_nsa_kv"].shape[1] - 1) for n in range(NPAGE)]
                        sp.wait_ge(k_turned, since(4 * b))
                        pool_kv = io["cache_nsa_kv"][0]
                        win = io["state_win_kv"][0, b] if type(b) is int else \
                            io["state_win_kv"][0, bass.ds(b, 1)].rearrange("o t s g d -> (o t) s g d")
                        rows = [pool_kv[bass.ds(p, 1)].rearrange("o t s g d -> (o t) s (g d)") for p in ids]
                        for n in range(NPAGE):
                            sp.dma_start(kn[:, 0, n, :], rows[n][:, 2, :]).then_inc(k_landed, 16)
                        sp.dma_start(kn[:, 1, :, :], win[:, 0].rearrange("(n p) g d -> p n (g d)", p=P)
                                     ).then_inc(k_landed, 16)
                        sp.wait_ge(attended, since(b - 1))
                        for n in range(NPAGE):
                            sp.dma_start(vn[:, par, 0, n, :], rows[n][:, 3, :]).then_inc(v_landed[par], 16)
                        sp.dma_start(vn[:, par, 1, :, :], win[:, 1].rearrange("(n p) g d -> p n (g d)", p=P)
                                     ).then_inc(v_landed[par], 16)
                run(sp, DB // 2, body)

            @block.tensor
            def _(pe):
                for b in range(DB):
                    last = pe.transpose(ps[:, 7, b * DH:(b + 1) * DH], cmp.vcT[:, b, :], core.ident[0:DH, 0:DH])
                last.then_inc(vc_turned, 1)

                def turn_keys(b):
                    pe.wait_ge(k_landed, 16 * 5 * (b + 1))
                    pe.wait_ge(kT_dve, since(2 * b))
                    pe.wait_ge(kT_act, since(2 * b))
                    for y in range(2):
                        for u in range(2):
                            for n in range(NPAGE):
                                last = pe.transpose(ps[:, y * 2 + u, n * P:(n + 1) * P],
                                                    kn[:, y, n, u * P:(u + 1) * P], core.ident)
                            last.then_inc(k_turned, 1)

                def score(b):
                    pe.wait_ge(staged, 2 * b + 2)
                    pe.wait_ge(kT_dve, 2 * b + 2)
                    pe.wait_ge(kT_act, 2 * b + 2)
                    pe.wait_ge(exped, since(2 * b))
                    for y in range(2):
                        rows = slice(y * 64, y * 64 + 64)
                        for h in range(2):
                            for u in range(2):
                                pe.matmul(ps[rows, 4 + h, 0:HALF], qst[:, u, :],
                                          kTb[:, y, u, h * HALF:(h + 1) * HALF], start=(u == 0), stop=False)
                    pe.matmul(ps[:, 4, 0:DS], core.identb[:, :],
                              core.maskb[:, C_WIN - trin0:C_WIN - trin0 + DS], start=False, stop=True)
                    pe.matmul(ps[:, 5, HALF - 32:HALF], core.identb[:, :],
                              core.maskb[:, bass.ds(b * 32 + C_NEW - trin0, 32)], start=False, stop=True)
                    pe.matmul(ps[:, 4, HALF:HALF + P], core.identb[:, :],
                              core.maskb[:, C_CMPS - trin0:C_CMPS - trin0 + P], start=True, stop=False)
                    pe.matmul(ps[:, 4, HALF:HALF + P], qcs[:, :], cmp.kcT[:, b, :], start=False, stop=True
                              ).then_inc(scored, 1)

                def body(i):
                    for par in range(2):
                        b = 2 * i + par
                        pe.wait_ge(scaled, 2 * b + 2)
                        for n in range(4):
                            last = pe.transpose(ps[:, 7, n * P:(n + 1) * P], prob[:, n * P:(n + 1) * P], core.ident)
                        last.then_inc(turned, 1)
                        pe.transpose(ps[0:32, 6, P:2 * P], prob[:, SEQ:T], core.ident)
                        pe.transpose(ps[:, 6, 2 * P:2 * P + 64], pcs[:, :], core.ident[0:64, 0:64]
                            ).then_inc(turned, 1)
                        if before_end(b, 1):
                            score(b + 1)
                        pe.wait_ge(moved, 2 * b + 2)
                        pe.wait_ge(moved_act, b + 1)
                        pe.wait_ge(v_staged, b + 1)
                        pe.wait_ge(out_taken, since(b))
                        pe.wait_ge(v_landed[par], 16 * 5 * (i + 1))
                        for u in range(2):
                            out = ps[:, 6, 384 + u * 32:416 + u * 32]
                            for y in range(2):
                                c = y * 64 + u * 32
                                for n in range(4):
                                    pe.matmul(out, vn[:, par, y, n, u * P:(u + 1) * P], pT[:, n, c:c + 32],
                                              start=(y == 0 and n == 0), stop=False)
                                v = (VS, VW)[y] + u * P
                                pe.matmul(out, at.qkv[0:SAMP, 4, v:v + P], pT[0:SAMP, 4, c:c + 32],
                                          start=False, stop=False)
                            last = pe.matmul(out, vcs[:, :, :].rearrange("p a d -> p (a d)"),
                                             pcT[:, u * 32:u * 32 + 32], start=False, stop=True)
                        last.then_inc(attended, 1)
                        if before_end(b, 2):
                            turn_keys(b + 2)
                pe.wait_ge(vc_moved, 1)
                turn_keys(0)
                score(0)
                turn_keys(1)
                run(pe, DB // 2, body)

            @block.scalar
            def _(act):
                def move_keys(b):
                    for u in range(2):
                        act.wait_ge(k_turned, 4 * b + 3 + u)
                        act.wait_ge(scored, since(b))
                        act.copy(kTb[:, 1, u, 0:PAST], ps[:, 2 + u, :]).then_inc(kT_act, 1)

                def body(i):
                    for par in range(2):
                        b = 2 * i + par
                        act.wait_ge(maxed, 5 * b + 5)
                        act.wait_ge(turned, since(2 * b))
                        act.activation(prob[:, :].rearrange("p (h c) -> p h c", h=2), ps[:, 4:6, 0:HALF], ACT.Exp,
                                       bias=mx[:, 0:1], scale=SCALE, accum_out=sums[:, 0:1]).then_inc(exped, 1)
                        act.activation(pcs[:, :], ps[0:64, 4, HALF:HALF + P], ACT.Exp, bias=mx[0:64, 1:2], scale=SCALE,
                                       accum_out=sums[0:64, 1:2]).then_inc(exped, 1)
                        if before_end(b, 1):
                            move_keys(b + 1)
                        act.wait_ge(turned, 2 * b + 2)
                        act.wait_ge(attended, since(b))
                        act.copy(pT[:, 0:4, :], ps[:, 7, :].rearrange("p (n r) -> p n r", n=4)).then_inc(moved_act, 1)
                move_keys(0)
                run(act, DB // 2, body)
                act.wait_ge(spread, 8)
                act.copy(core.hhi[:, :, SEQ:T], oT[:, :, :]).then_inc(s_hi, 1)

            @block.vector
            def _(dve):
                dve.memset(sums[:, :], 1.0).then_inc(keys_filled, 1)
                dve.memset(mx[:, :], 0.0).then_inc(keys_filled, 1)
                dve.memset(qcs[:, :], 0.0).then_inc(keys_filled, 1)
                dve.tensor_copy(kTb[:, :, :, PAST:T], at.kTn[:, :, :, :]).then_inc(keys_filled, 1)
                dve.wait_ge(vc_turned, 1)
                dve.tensor_copy(vc[:, :, :], ps[:, 7, :].rearrange("p (b d) -> p b d", d=DH)).then_inc(vc_moved, 1)
                dve.wait_ge(vc_moved, 1)
                dve.wait_ge(keys_filled, 4)

                def stage(b):
                    dve.wait_ge(scored, since(b))
                    dve.tensor_copy(qst[:, :, :], at.qblk[:, b, :, :]).then_inc(staged, 1)
                    dve.tensor_copy(qcs[:, 0:64], at.qs[:, b, :]).then_inc(staged, 1)

                def take_out(b):
                    dve.wait_ge(attended, b + 1)
                    dve.tensor_copy(outs[:, b, :], ps[:, 6, 384:448]).then_inc(out_taken, 1)

                def move_keys(b):
                    for u in range(2):
                        dve.wait_ge(k_turned, 4 * b + 1 + u)
                        dve.wait_ge(scored, since(b))
                        dve.tensor_copy(kTb[:, 0, u, 0:PAST], ps[:, u, :]).then_inc(kT_dve, 1)

                def body(i):
                    for par in range(2):
                        b = 2 * i + par
                        dve.wait_ge(scored, b + 1)
                        dve.tensor_reduce(mx2[:, :], ps[:, 4:6, 0:HALF], AX.X, ALU.max).then_inc(maxed, 1)
                        dve.tensor_reduce(mx[0:64, 1:2], ps[0:64, 4, HALF:HALF + P], AX.X, ALU.max).then_inc(maxed, 1)
                        dve.wait_ge(maxed, 5 * b + 2)
                        dve.tensor_reduce(mx[:, 0:1], mx2[:, :], AX.X, ALU.max).then_inc(maxed, 1)
                        dve.tensor_scalar(mx[0:64, 1:2], mx[0:64, 1:2], NEG / 10, -SCALE, ALU.max, ALU.mult
                                          ).then_inc(maxed, 1)
                        dve.wait_ge(maxed, 5 * b + 3)
                        dve.tensor_scalar(mx[:, 0:1], mx[:, 0:1], -SCALE, None, ALU.mult).then_inc(maxed, 1)
                        if before_end(b, 1):
                            stage(b + 1)
                        if not (type(b) is int and b == 0):
                            take_out(b - 1)
                        dve.wait_ge(attended, since(b))
                        dve.tensor_copy(vcs[:, :, :], vc[:, b, :].unsqueeze(1).broadcast_to([P, 2, DH])
                                        ).then_inc(v_staged, 1)
                        dve.wait_ge(exped, 2 * b + 2)
                        dve.tensor_scalar(coef[:, :], sums[:, :], 1e-30, None, ALU.max).then_inc(summed, 1)
                        dve.wait_ge(summed, 3 * b + 1)
                        dve.reciprocal(coef[:, :], coef[:, :]).then_inc(summed, 1)
                        dve.wait_ge(summed, 3 * b + 2)
                        dve.tensor_tensor(coef[:, :], coef[:, :], at.gate_rows[:, b, :], ALU.mult).then_inc(summed, 1)
                        dve.wait_ge(summed, 3 * b + 3)
                        dve.tensor_scalar(prob[:, :], prob[:, :], coef[:, 0:1], None, ALU.mult).then_inc(scaled, 1)
                        dve.tensor_scalar(pcs[:, :], pcs[:, :], coef[0:64, 1:2], None, ALU.mult).then_inc(scaled, 1)
                        if before_end(b, 1):
                            move_keys(b + 1)
                        dve.wait_ge(turned, 2 * b + 2)
                        dve.tensor_copy(pT[0:32, 4, :], ps[0:32, 6, P:2 * P]).then_inc(moved, 1)
                        dve.tensor_copy(pcT[:, :], ps[:, 6, 2 * P:2 * P + 64]).then_inc(moved, 1)
                stage(0)
                move_keys(0)
                run(dve, DB // 2, body)
                take_out(DB - 1)
                dve.wait_ge(out_taken, DB)
                for g in range(KVH):
                    for c in range(2):
                        src = outs[(g % 2) * DH:(g % 2) * DH + DH, :, g * 16:g * 16 + 16].rearrange(
                            "p b (a c t) -> p c a b t", a=2, c=2)[:, c]
                        dst = oT[c * DH:c * DH + DH, 2 * g:2 * g + 2, :].rearrange("p a (b t) -> p a b t", t=DS)
                        dve.tensor_copy(dst, src).then_inc(spread, 1)
                dve.wait_ge(s_hi, 1)
                dve.tensor_tensor(core.hlo[:, :, SEQ:T], oT[:, :, :], core.hhi[:, :, SEQ:T], ALU.subtract
                    ).then_inc(s_lo, 1)



def features_to_y(core, seg, moving, parts, epilogue=None):
    ps = core.ps
    first = core.starts[seg]
    n_tiles = core.stream[seg][0] // parts
    kt = core.stream[seg][1] // P
    per = 4 // parts
    y_taken, y_sq, y_added, cleared = (
        core.sig(n) for n in ("y_taken", "y_squared", "ssq_added", "ssq_cleared"))
    hi, lo = moving
    extra = epilogue or {}
    with core.stage() as block:
        @block.sync
        def _(sp):
            late_loads(core, sp)
            load_stage(core, sp, seg, first)
            if "sync" in extra:
                extra["sync"](sp)

        @block.tensor
        def _(pe):
            if "tensor" in extra:
                extra["tensor"](pe)

            def body(i):
                for k in range(4):
                    m, part = i * per + k // parts, k % parts
                    bank = (k // parts) % 2 * 2
                    weights_ready(core, pe, first + 4 * i + k)
                    if part == 0:
                        pe.wait_ge(y_taken, since(m - 1))
                    w_hi, w_lo = (w[:, k, 0:kt * P].rearrange("p (a c) -> p a c", c=P) for w in (core.whi, core.wlo))
                    for h in range(2):
                        cols = slice(h * HALF, (h + 1) * HALF)
                        last = product(pe, ps[:, bank + h, 0:HALF], [(a, part * kt + a) for a in range(kt)],
                                       lambda a: (w_hi[:, a, :], w_lo[:, a, :]),
                                       lambda a: (hi[:, a, cols], lo[:, a, cols]), part == 0, part == parts - 1)
                    last.then_inc(core.w_used, 1)
            run(pe, n_tiles // per, body)

        @block.scalar
        def _(act):
            late_heads(core, act)
            if "scalar" in extra:
                extra["scalar"](act)

            def body(i):
                for k in range(4):
                    m = i * per + k // parts
                    cast_hi(core, act, seg, i, k, first)
                    if k % parts == parts - 1:
                        act.wait_ge(y_taken, m + 1)
                        act.wait_ge(y_added, since(m - 1))
                        act.activation(core.sq[:, (k // parts) % 2, :], core.yT[:, m, :], ACT.Square
                            ).then_inc(y_sq, 1)
            run(act, n_tiles // per, body)

        @block.vector
        def _(dve):
            dve.memset(core.ssq[:, :], 0.0).then_inc(cleared, 1)
            dve.wait_ge(cleared, 1)
            if "vector" in extra:
                extra["vector"](dve)

            def body(i):
                for j in range(per):
                    m = i * per + j
                    dve.wait_ge(core.w_used, first + (m + 1) * parts)
                    dve.tensor_copy(core.yT[:, m, :].rearrange("p (h c) -> p h c", h=2),
                                    ps[:, (j % 2) * 2:(j % 2) * 2 + 2, 0:HALF]).then_inc(y_taken, 1)
                    dve.wait_ge(y_sq, m + 1)
                    dve.wait_ge(y_added, since(m))
                    dve.tensor_tensor(core.ssq[:, :], core.ssq[:, :], core.sq[:, j % 2, :], ALU.add
                        ).then_inc(y_added, 1)
            run(dve, n_tiles // per, body)

        @block.gpsimd
        def _(pool):
            late_rests(core, pool)

            def body(i):
                for k in range(4):
                    cast_lo(core, pool, seg, i, k, first)
            run(pool, n_tiles // per, body)
    core.pending = seg + 1 if seg + 1 < len(core.stream) else None



GW = 2 + SEQ + DB * (DS + 2)


def ffn_up(core, l, seg, ghi, glo, kept):
    ps = core.ps
    first = core.starts[seg]
    gate_in, conv, gelu, prod, g_hi, g_lo, keep, cleared = (core.sig(n) for n in (
        "gate_in", "conv_step", "gelu_done", "product_done", "g_hi", "g_lo", "rows_kept", "gate_cleared"))
    with ExitStack() as own:
        gate = core.sb("gate", [P, 2, GW], F32, own)
        cv = core.sb("conv", [P, 2, GW - 2], F32, own)
        ge = core.sb("gelu", [P, 2, GW - 2], F32, own)
        gp = core.sb("gated", [P, 2, T], F32, own)
        later = lambda x: x.rearrange("p (b j) -> p b j", j=DS + 2)
        with core.stage() as block:
            @block.sync
            def _(sp):
                late_loads(core, sp)
                load_stage(core, sp, seg, first)

            @block.tensor
            def _(pe):
                def body(i):
                    for k in range(4):
                        m, q, val = 2 * i + k // 2, k // 2, k % 2
                        weights_ready(core, pe, first + 4 * i + k)
                        if val:
                            pe.wait_ge(prod, since(3 * (m - 1)))
                        else:
                            pe.wait_ge(gate_in, since(4 * (m - 1)))
                        w_hi, w_lo = block_hi(core, k, P), block_lo(core, k, P)
                        for h in range(2):
                            cols = slice(h * HALF, (h + 1) * HALF)
                            last = product(pe, ps[:, 4 * q + 2 * val + h, 0:HALF], [(a, a) for a in range(KD)],
                                           lambda a: (w_hi[:, a, :], w_lo[:, a, :]),
                                           lambda a: (core.hhi[:, a, cols], core.hlo[:, a, cols]), True, True)
                        last.then_inc(core.w_used, 1)
                run(pe, KF // 2, body)

            @block.scalar
            def _(act):
                late_heads(core, act)
                act.wait_ge(cleared, 1)

                def body(i):
                    for q in range(2):
                        m = 2 * i + q
                        act.wait_ge(core.w_used, first + 2 * m + 1)
                        act.wait_ge(conv, since(3 * (m - 1)))
                        act.wait_ge(keep, since(2 * (m - 1)))
                        act.copy(gate[:, q, 2:2 + HALF], ps[:, 4 * q, 0:HALF]).then_inc(gate_in, 1)
                        act.copy(gate[:, q, 2 + HALF:2 + SEQ], ps[:, 4 * q + 1, 0:SEQ - HALF]).then_inc(gate_in, 1)
                        act.copy(later(gate[:, q, 2 + SEQ:GW])[:, :, 2:],
                                 ps[:, 4 * q + 1, SEQ - HALF:HALF].rearrange("p (b t) -> p b t", t=DS)
                                     ).then_inc(gate_in, 1)
                        act.copy(later(gate[:, q, 2 + SEQ:GW])[:, :, 0:2],
                                 core.taps[:, l, m, 4:20].rearrange("p (b j) -> p b j", j=2)).then_inc(gate_in, 1)
                        cast_hi(core, act, seg, i, 2 * q, first)
                        act.wait_ge(conv, 3 * m + 3)
                        act.wait_ge(prod, since(3 * (m - 1)))
                        act.activation(ge[:, q, :], cv[:, q, :], ACT.Gelu_apprx_tanh).then_inc(gelu, 1)
                        cast_hi(core, act, seg, i, 2 * q + 1, first)
                        act.wait_ge(prod, 3 * m + 3)
                        act.copy(ghi[:, m, :], gp[:, q, :]).then_inc(g_hi, 1)
                run(act, KF // 2, body)

            @block.vector
            def _(dve):
                dve.memset(gate[:, :, 0:2], 0.0).then_inc(cleared, 1)

                def body(i):
                    for q in range(2):
                        m = 2 * i + q
                        tap = lambda j: core.taps[:, l, m, j:j + 1]
                        dve.wait_ge(gate_in, 4 * m + 4)
                        dve.wait_ge(gelu, since(m - 1))
                        dve.tensor_scalar(cv[:, q, :], gate[:, q, 0:GW - 2], tap(0), tap(3), ALU.mult, ALU.add
                            ).then_inc(conv, 1)
                        for j in (1, 2):
                            dve.wait_ge(conv, 3 * m + j)
                            dve.scalar_tensor_tensor(cv[:, q, :], gate[:, q, j:GW - 2 + j], tap(j), cv[:, q, :],
                                                     ALU.mult, ALU.add).then_inc(conv, 1)
                        dve.wait_ge(gelu, m + 1)
                        dve.wait_ge(core.w_used, first + 2 * m + 2)
                        dve.wait_ge(g_lo, since(m - 1))
                        for out, a, v in (
                                (gp[:, q, 0:HALF], ge[:, q, 0:HALF], ps[:, 4 * q + 2, 0:HALF]),
                                (gp[:, q, HALF:SEQ], ge[:, q, HALF:SEQ], ps[:, 4 * q + 3, 0:SEQ - HALF]),
                                (gp[:, q, SEQ:T].rearrange("p (b t) -> p b t", t=DS), later(ge[:, q, SEQ:])[:, :, 2:],
                                 ps[:, 4 * q + 3, SEQ - HALF:HALF].rearrange("p (b t) -> p b t", t=DS))):
                            dve.tensor_tensor(out, a, v, ALU.mult).then_inc(prod, 1)
                run(dve, KF // 2, body)

            @block.gpsimd
            def _(pool):
                late_rests(core, pool)

                def body(i):
                    for q in range(2):
                        m = 2 * i + q
                        pool.wait_ge(gate_in, 4 * m + 4)
                        pool.tensor_copy(kept[:, m, 0:2], gate[:, q, SEQ:SEQ + 2]).then_inc(keep, 1)
                        pool.tensor_copy(kept[:, m, 2:18].rearrange("p (b j) -> p b j", j=2),
                                         later(gate[:, q, 2 + SEQ:GW])[:, :, DS:]).then_inc(keep, 1)
                        cast_lo(core, pool, seg, i, 2 * q, first)
                        pool.wait_ge(g_hi, m + 1)
                        pool.tensor_tensor(glo[:, m, :], gp[:, q, :], ghi[:, m, :], ALU.subtract).then_inc(g_lo, 1)
                        cast_lo(core, pool, seg, i, 2 * q + 1, first)
                run(pool, KF // 2, body)
    core.pending = seg + 1


def ffn(core, l, seg):
    io, ps = core.io, core.ps
    with ExitStack() as own:
        ghi = core.sb("g_hi", [P, KF, T], F16, own)
        glo = core.sb("g_lo", [P, KF, T], BF16, own)
        kept = core.sb("kept", [P, KF, 18], F32, own)
        rows = core.sb("kept_rows", [18, F], F32, own)
        ffn_up(core, l, seg, ghi, glo, kept)
        k_turned, k_moved = core.sig("kept_turned"), core.sig("kept_moved")
        core.conv_out = core.sig("conv_rows_out")
        n = -(-KF // 4)

        def turn(pe):
            for j in range(n):
                pe.wait_ge(k_moved, since(j - 3))
                for m in range(4 * j, min(4 * j + 4, KF)):
                    last = pe.transpose(ps[0:18, 4 + j % 4, (m % 4) * P:(m % 4 + 1) * P], kept[:, m, :], core.ident)
                last.then_inc(k_turned, 1)

        def move(dve):
            for j in range(n):
                dve.wait_ge(k_turned, j + 1)
                w = min(512, F - 512 * j)
                dve.tensor_copy(rows[:, 512 * j:512 * j + w], ps[0:18, 4 + j % 4, 0:w]).then_inc(k_moved, 1)

        def out(sp):
            sp.wait_ge(k_moved, n)
            sp.dma_start(io["out_ffn_p"][l, 0], rows[0:2, :]).then_inc(core.conv_out, 16)
            sp.dma_start(io["out_ffn_s"][l].rearrange("b j f -> (b j) f"), rows[2:18, :]).then_inc(core.conv_out, 16)
            sp.wait_ge(core.conv_out, 32)
        features_to_y(core, seg + 1, (ghi, glo), 2, dict(sync=out, tensor=turn, vector=move))



class Gla:
    def __init__(self, core, ctx):
        self.qk = core.sb("gla_qk", [P, 2 * GH, T], F32, ctx)
        self.cum = core.sb("gla_cum", [P, GH, T], F32, ctx)
        self.vr = core.sb("gla_vr", [P, NT, 2 * GH * DV], F32, ctx)
        self.sumsq = core.sb("gla_sumsq", [P, NT, GH], F32, ctx)
        self.ng = core.sb("gla_norm", [P, DV], F32, ctx)


def gla_heads(core, gla, seg):
    ps, io = core.ps, core.io
    first = core.starts[seg]
    n_tiles = core.stream[seg][0]
    taken, small_in, low, low_taken, z_ready, z_taken, steps, cast = (core.sig(n) for n in (
        "qk_taken", "gla_small_in", "low_rank_ready", "low_rank_taken", "gates_raw", "gates_biased", "decay_step",
        "low_w_cast"))
    with ExitStack() as own:
        gw = core.sb("low_w", [P, KD, 16], F32, own)
        gwhi, gwlo = core.sb("low_w_hi", [P, KD, 16], F16, own), core.sb("low_w_lo", [P, KD, 16], BF16, own)
        up = core.sb("gate_up", [16, GH * DK], F32, own)
        bias = core.sb("gate_bias", [P, GH], F32, own)
        ngrow = core.sb("norm_row", [1, DV], F32, own)
        lowT = core.sb("low_T", [16, T], F32, own)
        z = core.sb("z", [P, GH, T], F32, own)
        with core.stage() as block:
            @block.sync
            def _(sp):
                sp.dma_start(gw[:, :, :], io["gla_w_in"][0][:, GPROJ - 16:GPROJ].rearrange("(k p) c -> p k c", p=P)
                             ).then_inc(small_in, 16)
                sp.dma_start(up[:, :], io["gla_w_gate_up"][0]).then_inc(small_in, 16)
                sp.dma_start(bias[:, :], io["gla_b_gate"].rearrange("o (h p) -> p (o h)", p=P),
                             allow_slow_non_contiguous=True).then_inc(
                    small_in, 16)
                sp.dma_start(ngrow[:, :], io["gla_norm_gain"]).then_inc(small_in, 16)
                late_loads(core, sp)
                load_stage(core, sp, seg, first)

            @block.tensor
            def _(pe):
                pe.wait_ge(small_in, 64)
                pe.matmul(ps[:, 6, 0:DV], core.ones[0:1, :], ngrow[:, :], start=True, stop=True).then_inc(low, 1)
                pe.wait_ge(cast, 2)
                for h in range(2):
                    cols = slice(h * HALF, (h + 1) * HALF)
                    last = product(pe, ps[0:16, 4 + h, 0:HALF], [(a, a) for a in range(KD)],
                                   lambda a: (gwhi[:, a, :], gwlo[:, a, :]),
                                   lambda a: (core.hhi[:, a, cols], core.hlo[:, a, cols]), True, True)
                last.then_inc(low, 1)
                pe.wait_ge(low_taken, 2)
                for t in range(GH):
                    pe.wait_ge(z_taken, since(t))
                    for h in range(2):
                        last = pe.matmul(ps[:, 4 + h, 0:HALF], up[:, t * DK:(t + 1) * DK],
                                         lowT[:, h * HALF:(h + 1) * HALF], start=True, stop=True)
                    last.then_inc(z_ready, 1)

                def body(i):
                    for k in range(4):
                        n = 4 * i + k
                        weights_ready(core, pe, first + n)
                        pe.wait_ge(taken, since(n - 1))
                        w_hi, w_lo = block_hi(core, k, P), block_lo(core, k, P)
                        for h in range(2):
                            cols = slice(h * HALF, (h + 1) * HALF)
                            last = product(pe, ps[:, (k % 2) * 2 + h, 0:HALF], [(a, a) for a in range(KD)],
                                           lambda a: (w_hi[:, a, :], w_lo[:, a, :]),
                                           lambda a: (core.hhi[:, a, cols], core.hlo[:, a, cols]), True, True)
                        last.then_inc(core.w_used, 1)
                run(pe, n_tiles // 4, body)

            @block.scalar
            def _(act):
                late_heads(core, act)
                act.wait_ge(small_in, 64)
                act.copy(gwhi[:, :, :], gw[:, :, :]).then_inc(cast, 1)
                act.wait_ge(low, 1)
                act.copy(gla.ng[:, :], ps[:, 6, 0:DV]).then_inc(low_taken, 1)
                act.wait_ge(low, 2)
                act.copy(lowT[:, :].rearrange("p (h c) -> p h c", h=2), ps[0:16, 4:6, 0:HALF]).then_inc(low_taken, 1)
                for t in range(GH):
                    act.wait_ge(z_ready, t + 1)
                    act.activation(z[:, t, :].rearrange("p (h c) -> p h c", h=2), ps[:, 4:6, 0:HALF],
                                   ACT.Identity, bias=bias[:, t:t + 1]).then_inc(z_taken, 1)
                act.wait_ge(steps, 1)
                act.activation(gla.cum[:, :, :], gla.cum[:, :, :], ACT.Exp).then_inc(steps, 1)
                act.wait_ge(steps, 2)
                act.activation(gla.cum[:, :, :], gla.cum[:, :, :], ACT.Ln, bias=1.0).then_inc(steps, 1)

                def body(i):
                    for k in range(4):
                        act.wait_ge(core.w_used, first + 4 * i + k + 1)
                        act.copy(gla.qk[:, 4 * i + k, :].rearrange("p (h c) -> p h c", h=2),
                                 ps[:, (k % 2) * 2:(k % 2) * 2 + 2, 0:HALF]).then_inc(taken, 1)
                        cast_hi(core, act, seg, i, k, first)
                run(act, n_tiles // 4, body)

            @block.vector
            def _(dve):
                dve.wait_ge(small_in, 64)
                dve.wait_ge(cast, 1)
                dve.tensor_tensor(gwlo[:, :, :], gw[:, :, :], gwhi[:, :, :], ALU.subtract).then_inc(cast, 1)
                dve.wait_ge(z_taken, GH)
                dve.scalar_tensor_tensor(gla.cum[:, :, :], z[:, :, :], -1.0, z[:, :, :], ALU.mult, ALU.min
                    ).then_inc(steps, 1)
                dve.wait_ge(steps, 3)
                dve.scalar_tensor_tensor(z[:, :, :], z[:, :, :], 0.0, gla.cum[:, :, :], ALU.min, ALU.subtract
                    ).then_inc(steps, 1)
                dve.wait_ge(steps, 4)
                for h in range(GH):
                    dve.tensor_tensor_scan(gla.cum[:, h, :], core.const[:, C_SEG:C_SEG + T], z[:, h, :], 0.0,
                                           ALU.mult, ALU.add).then_inc(steps, 1)

            @block.gpsimd
            def _(pool):
                late_rests(core, pool)

                def body(i):
                    for k in range(4):
                        cast_lo(core, pool, seg, i, k, first)
                run(pool, n_tiles // 4, body)
    core.pending = seg + 1



LIMIT = 40 * 16.0


def gla_core(core, gla, o):
    ps, io = core.ps, core.io
    C = SEQ // P
    names = ("g_diff", "g_exp", "g_prod", "g_turned", "g_kend", "g_att", "g_att_masked", "g_kv", "g_state", "g_out",
             "g_out_taken", "s0_in", "s_rows", "s_kv", "s_new", "states_out", "decays")
    (diff, exped, prod, turned, kend_ready, att, att_masked, kv, state, out, out_taken, s0_in, s_rows, s_kv, s_new,
     states_out, decays) = (core.sig(n) for n in names)
    with ExitStack() as own:
        sb = lambda n, s: core.sb(n, s, F32, own)
        d = sb("g_d", [P, 2, T])
        e = sb("g_e", [P, 2, 4, T])
        kend = sb("g_kend", [P, NT, P])
        am = sb("g_am", [P, SEQ + 32])
        S = sb("g_S", [P, C, DV])
        el = sb("g_el", [P, 2, C + DB])
        qb, kb = sb("g_qb", [P, 2, DB, SAMP]), sb("g_kb", [SAMP, DB, P])
        s0, s1 = (x[:, :, :].rearrange("p k t -> p (k t)").bitcast(F32)[:, 0:DB * DV].rearrange(
            "p (b v) -> p b v", b=DB) for x in (core.hhi, core.hlo))
        sqs = sb("g_sqs", [P, DV])
        chunks = lambda x: x[:, 0:SEQ].rearrange("p (c t) -> p c t", t=P)
        seqs = lambda x: x[:, SEQ:T].rearrange("p (b t) -> p b t", t=DS)

        with core.stage() as block:
            @block.sync
            def _(sp):
                late_loads(core, sp)

                def body(h):
                    sp.wait_ge(s_new, since(8 * h))
                    g_read = core.sig("s0_read")
                    sp.wait_ge(g_read, since(h))
                    src = io["state_gla"][0].rearrange("b h k v -> h k b v")
                    sp.dma_start(s0[:, :, :], src[h] if type(h) is int else
                                 src[bass.ds(h, 1)].rearrange("o k b v -> (o k) b v")).then_inc(s0_in, 16)
                    sp.wait_ge(s_new, 8 * h + 8)
                    dst = io["out_gla_s"][0].rearrange("b h k v -> h k b v")
                    sp.dma_start(dst[h] if type(h) is int else dst[bass.ds(h, 1)].rearrange("o k b v -> (o k) b v"),
                                 s1[:, :, :]).then_inc(states_out, 16)
                    sp.wait_ge(state, C * h + C)
                    dst = io["out_gla_p"][0, 0]
                    sp.dma_start(dst[h] if type(h) is int else dst[bass.ds(h, 1)].rearrange("o k v -> (o k) v"),
                                 S[:, C - 1, :]).then_inc(core.sig("state_p_out"), 16)
                run(sp, GH, body)
                sp.wait_ge(states_out, 16 * GH)
                sp.wait_ge(core.sig("state_p_out"), 16 * GH)

            @block.tensor
            def _(pe):
                def body(h):
                    qd, kd, qi, ke = (e[:, h % 2, n, :] for n in range(4))
                    v = lambda i, rows: gla.vr[0:rows, i, bass.ds(h * DV, DV)]
                    pe.wait_ge(prod, 5 * h + 1)
                    pe.wait_ge(kend_ready, since(h))
                    for c in range(C):
                        last = pe.transpose(ps[:, 0, c * P:(c + 1) * P], ke[:, c * P:(c + 1) * P], core.ident)
                    last.then_inc(turned, 1)
                    pe.wait_ge(out_taken, since(3 * h - 2))
                    pe.transpose(ps[0:SAMP, 6, 0:P], ke[:, SEQ:T], core.ident).then_inc(turned, 1)
                    pe.wait_ge(prod, 5 * h + 5)
                    for c in range(C):
                        last = pe.matmul(ps[:, 1, c * P:(c + 1) * P], kd[:, c * P:(c + 1) * P],
                                         qd[:, c * P:(c + 1) * P], start=True, stop=True)
                    last.then_inc(att, 1)
                    pe.matmul(ps[0:SAMP, 7, 0:SAMP], kd[:, SEQ:T], qi[:, SEQ:T], start=True, stop=True
                        ).then_inc(att, 1)
                    pe.wait_ge(s_rows, 2 * h + 2)
                    pe.wait_ge(out_taken, since(3 * h))
                    for b in range(DB):
                        last = pe.matmul(ps[:, 2 + b // 2, (b % 2) * DV:(b % 2 + 1) * DV], kb[:, b, :],
                                         v(4, SAMP), start=True, stop=True)
                        if b % 2:
                            last.then_inc(s_kv, 1)
                    pe.wait_ge(core.sig("set"), 2)
                    pe.wait_ge(att_masked, 2 * h + 2)
                    pe.wait_ge(s0_in, 16 * h + 16)
                    o_s = ps[0:SAMP, 6, 256:512]
                    for b in range(DB):
                        pe.matmul(o_s, qb[:, h % 2, b, :], s0[:, b, :], start=(b == 0), stop=False)
                    pe.matmul(o_s, am[:, SEQ:SEQ + SAMP], v(4, P), start=False, stop=True
                        ).then_inc(core.sig("s0_read"), 1)
                    pe.wait_ge(s_new, 8 * h + 8)
                    pe.wait_ge(kend_ready, h + 1)
                    for c in range(C):
                        last = pe.matmul(ps[:, 2 + c // 2, (c % 2) * DV:(c % 2 + 1) * DV], kend[:, c, :], v(c, P),
                                         start=True, stop=True)
                    last.then_inc(kv, 1)
                    for c in range(C):
                        o_c = ps[:, 4 + c // 2, (c % 2) * DV:(c % 2 + 1) * DV]
                        last = pe.matmul(o_c, am[:, c * P:(c + 1) * P], v(c, P), start=True, stop=(c == 0))
                        if c:
                            pe.wait_ge(state, C * h + c)
                            last = pe.matmul(o_c, qi[:, c * P:(c + 1) * P], S[:, c - 1, :], start=False, stop=True)
                        if c % 2:
                            last.then_inc(out, 1)
                for h in range(GH):
                    body(h)

            @block.scalar
            def _(act):
                late_heads(core, act)

                def decay(h):
                    act.wait_ge(prod, since(5 * (h - 1)))
                    act.activation(e[:, h % 2, 2, :], gla.cum[:, h, :], ACT.Exp, scale=1 / 16).then_inc(exped, 1)
                    act.wait_ge(diff, 5 * h + 5)
                    act.activation(e[:, h % 2, 3, :], d[:, 1, :], ACT.Exp, scale=1 / 16).then_inc(exped, 1)
                    act.activation(e[:, h % 2, 0, :], d[:, 0, :], ACT.Exp, scale=1 / 16).then_inc(exped, 1)
                    act.activation(e[:, h % 2, 1, :], d[:, 0, :], ACT.Exp, scale=-1 / 16).then_inc(exped, 1)

                def body(h):
                    act.wait_ge(turned, 2 * h + 1)
                    act.wait_ge(kv, since(h))
                    act.copy(kend[:, 0:C, :], ps[:, 0, :].rearrange("p (c k) -> p c k", k=P)).then_inc(kend_ready, 1)
                    if h + 1 < GH:
                        decay(h + 1)
                    for n in range(3):
                        if n == 0:
                            act.wait_ge(core.sig("s0_read"), h + 1)
                            src, rows, t0, nt = ps[0:SAMP, 6, 256:512], SAMP, 4, 1
                        else:
                            act.wait_ge(out, 2 * h + n)
                            src, rows, t0, nt = ps[:, 3 + n, :], P, 2 * n - 2, 2
                        dst = o[0:rows, t0:t0 + nt, bass.ds(h * DV, DV)]
                        act.copy(dst, src.rearrange("p (a c) -> p a c", c=DV)).then_inc(out_taken, 1)
                        act.wait_ge(out_taken, 3 * h + n + 1)
                        for t in range(t0, t0 + nt):
                            act.activation(sqs[0:rows, :], o[0:rows, t, bass.ds(h * DV, DV)], ACT.Square,
                                           accum_out=gla.sumsq[0:rows, t, bass.ds(h, 1)]
                                               ).then_inc(core.sig("squared"), 1)
                            act.wait_ge(core.sig("squared"), 5 * h + {4: 0, 0: 1, 1: 2, 2: 3, 3: 4}[t] + 1)
                decay(0)
                for h in range(GH):
                    body(h)

            @block.vector
            def _(dve):
                dve.memset(gla.sumsq[:, 4, :], 1.0).then_inc(core.sig("set"), 1)
                dve.memset(am[:, SEQ:SEQ + SAMP], 0.0).then_inc(core.sig("set"), 1)

                def exponents(h):
                    cum = gla.cum[:, h, :]
                    c3, s3 = chunks(cum), seqs(cum)
                    dve.wait_ge(exped, since(4 * h))
                    dve.tensor_tensor(chunks(d[:, 1, :]), c3[:, :, P - 1:P].broadcast_to([P, C, P]), c3,
                                      ALU.subtract).then_inc(diff, 1)
                    dve.tensor_tensor(seqs(d[:, 1, :]), s3[:, :, DS - 1:DS].broadcast_to([P, DB, DS]), s3,
                                      ALU.subtract).then_inc(diff, 1)
                    dve.tensor_tensor(chunks(d[:, 0, :]), c3, c3[:, :, P // 2 - 1:P // 2].broadcast_to([P, C, P]),
                                      ALU.subtract).then_inc(diff, 1)
                    dve.tensor_copy(d[:, 0, SEQ:T], cum[:, SEQ:T]).then_inc(diff, 1)
                    dve.wait_ge(diff, 5 * h + 4)
                    dve.tensor_scalar(d[:, 0, :], d[:, 0, :], LIMIT, -LIMIT, ALU.min, ALU.max).then_inc(diff, 1)

                def operands(h):
                    q, k = gla.qk[:, h, :], gla.qk[:, h + GH, :]
                    qd, kd, qi, ke = (e[:, h % 2, n, :] for n in range(4))
                    dve.wait_ge(exped, 4 * h + 1)
                    dve.wait_ge(state, since(C * (h - 1)))
                    dve.wait_ge(out, since(2 * (h - 1)))
                    dve.tensor_copy(el[:, h % 2, 0:C].unsqueeze(2), chunks(qi)[:, :, P - 1:P]).then_inc(decays, 1)
                    dve.tensor_copy(el[:, h % 2, C:C + DB].unsqueeze(2), seqs(qi)[:, :, DS - 1:DS]
                        ).then_inc(decays, 1)
                    dve.wait_ge(exped, 4 * h + 2)
                    dve.tensor_tensor(ke, k, ke, ALU.mult).then_inc(prod, 1)
                    dve.wait_ge(decays, 2 * h + 2)
                    dve.scalar_tensor_tensor(qi, q, DK ** -0.5, qi, ALU.mult, ALU.mult).then_inc(prod, 1)
                    dve.wait_ge(prod, 5 * h + 2)
                    dve.tensor_tensor(qb[:, h % 2, :, :], qi[:, SEQ:T].unsqueeze(1).broadcast_to([P, DB, SAMP]),
                                      core.const[:, C_COLM:C_COLM + DB * SAMP].rearrange(
                                          "p (b c) -> p b c", b=DB), ALU.mult).then_inc(prod, 1)
                    dve.wait_ge(exped, 4 * h + 4)
                    dve.scalar_tensor_tensor(qd, q, DK ** -0.5, qd, ALU.mult, ALU.mult).then_inc(prod, 1)
                    dve.tensor_tensor(kd, k, kd, ALU.mult).then_inc(prod, 1)

                def body(h):
                    dve.wait_ge(turned, 2 * h + 2)
                    dve.wait_ge(s_kv, since(4 * h))
                    dve.tensor_copy(kend[0:SAMP, C, :], ps[0:SAMP, 6, 0:P]).then_inc(s_rows, 1)
                    dve.wait_ge(s_rows, 2 * h + 1)
                    dve.tensor_tensor(kb[:, :, :], kend[0:SAMP, C:C + 1, :].broadcast_to([SAMP, DB, P]),
                                      core.const[0:SAMP, C_ROW:C_ROW + DB].unsqueeze(2).broadcast_to(
                                          [SAMP, DB, P]), ALU.mult).then_inc(s_rows, 1)
                    dve.wait_ge(att, 2 * h + 1)
                    dve.scalar_tensor_tensor(
                    chunks(am), ps[:, 1, :].rearrange("p (c t) -> p c t", t=P), 3e38,
                    core.const[:, C_TRI1:C_TRI1 + P].unsqueeze(1).broadcast_to([P, C, P]), ALU.min, ALU.mult
                        ).then_inc(att_masked, 1)
                    dve.wait_ge(core.sig("set"), 2)
                    dve.wait_ge(att, 2 * h + 2)
                    dve.scalar_tensor_tensor(am[0:SAMP, SEQ:SEQ + SAMP], ps[0:SAMP, 7, 0:SAMP], 3e38,
                                             core.const[0:SAMP, C_ATT:C_ATT + SAMP], ALU.min, ALU.mult
                                                 ).then_inc(att_masked, 1)
                    if h + 1 < GH:
                        exponents(h + 1)
                    dve.wait_ge(decays, 2 * h + 2)
                    dve.wait_ge(s0_in, 16 * h + 16)
                    dve.wait_ge(states_out, since(16 * h))
                    for b in range(DB):
                        dve.wait_ge(s_kv, 4 * h + b // 2 + 1)
                        dve.scalar_tensor_tensor(s1[:, b, :], s0[:, b, :], el[:, h % 2, C + b:C + b + 1],
                                                 ps[:, 2 + b // 2, (b % 2) * DV:(b % 2 + 1) * DV],
                                                 ALU.mult, ALU.add).then_inc(s_new, 1)
                    if h + 1 < GH:
                        operands(h + 1)
                    dve.wait_ge(kv, h + 1)
                    dve.wait_ge(core.sig("state_p_out"), since(16 * h))
                    dve.tensor_copy(S[:, 0, :], ps[:, 2, 0:DV]).then_inc(state, 1)
                    for c in range(1, C):
                        dve.wait_ge(state, C * h + c)
                        dve.scalar_tensor_tensor(S[:, c, :], S[:, c - 1, :], el[:, h % 2, c:c + 1],
                                                 ps[:, 2 + c // 2, (c % 2) * DV:(c % 2 + 1) * DV],
                                                 ALU.mult, ALU.add).then_inc(state, 1)
                exponents(0)
                operands(0)
                for h in range(GH):
                    body(h)

            @block.gpsimd
            def _(pool):
                late_rests(core, pool)


def gla_finish(core, gla, o):
    ps = core.ps
    names = ("f_var", "f_silu", "f_normed", "f_gated", "f_turned", "f_hi", "f_lo")
    var, silu, normed, gated, turned, f_hi, f_lo = (core.sig(n) for n in names)
    NV = GH * DV
    rows = lambda i: P if i < 4 else SAMP
    bank = lambda i: ps[:, 2 * (i % 2):2 * (i % 2) + 2, :].rearrange("p b (k t) -> p b k t", t=P)[:, :, :, 0:rows(i)]
    halves = lambda x, i: x[:, :, i * P:i * P + rows(i)].rearrange("p (b k) t -> p b k t", b=2)
    with core.stage() as block:
        @block.tensor
        def _(pe):
            for i in range(NT):
                pe.wait_ge(gated, i + 1)
                pe.wait_ge(f_lo, since(i - 1))
                for k in range(KD):
                    last = pe.transpose(ps[:, 2 * (i % 2) + k // 4, (k % 4) * P:(k % 4) * P + rows(i)],
                                        o[0:rows(i), i, k * P:(k + 1) * P], core.ident[0:rows(i), 0:rows(i)])
                last.then_inc(turned, 1)

        @block.scalar
        def _(act):
            act.wait_ge(var, 1)
            act.activation(gla.sumsq[:, :, :], gla.sumsq[:, :, :], ACT.Sqrt).then_inc(var, 1)
            for i in range(NT):
                act.activation(gla.vr[:, i, NV:2 * NV], gla.vr[:, i, NV:2 * NV], ACT.Silu).then_inc(silu, 1)
            for i in range(NT):
                act.wait_ge(turned, i + 1)
                act.copy(halves(core.hhi, i), bank(i)).then_inc(f_hi, 1)

        @block.vector
        def _(dve):
            dve.tensor_scalar(gla.sumsq[:, :, :], gla.sumsq[:, :, :], 1.0 / DV, EPS, ALU.mult, ALU.add
                ).then_inc(var, 1)
            dve.wait_ge(var, 2)
            dve.reciprocal(gla.sumsq[:, :, :], gla.sumsq[:, :, :]).then_inc(var, 1)
            dve.wait_ge(var, 3)

            def rest(i):
                dve.wait_ge(f_hi, i + 1)
                dve.tensor_tensor(halves(core.hlo, i), bank(i), halves(core.hhi, i), ALU.subtract).then_inc(f_lo, 1)
            for i in range(NT):
                for h in range(GH):
                    x = o[0:rows(i), i, h * DV:(h + 1) * DV]
                    dve.scalar_tensor_tensor(x, x, gla.sumsq[0:rows(i), i, h:h + 1], gla.ng[0:rows(i), :], ALU.mult,
                                             ALU.mult).then_inc(normed, 1)
                if i > 1:
                    rest(i - 2)
            rest(NT - 2)
            rest(NT - 1)

        @block.gpsimd
        def _(pool):
            for i in range(NT):
                pool.wait_ge(silu, i + 1)
                pool.wait_ge(normed, GH * (i + 1))
                pool.tensor_tensor(o[0:rows(i), i, :], o[0:rows(i), i, :], gla.vr[0:rows(i), i, NV:2 * NV], ALU.mult
                                   ).then_inc(gated, 1)



def write_y(core):
    ps, io = core.ps, core.io
    turned, moved_a, moved_d = core.sig("y_turned"), core.sig("y_moved_act"), core.sig("y_moved_dve")
    y_out = [core.sig("y_out0"), core.sig("y_out1")]
    with ExitStack() as own:
        yt = core.sb("y_rows", [P, 2, D], F32, own)
        with core.stage() as block:
            @block.tensor
            def _(pe):
                for i in range(NT):
                    rows = P if i < 4 else SAMP
                    pe.wait_ge(moved_a, since(i - 1))
                    pe.wait_ge(moved_d, since(i - 1))
                    for k in range(KD):
                        last = pe.transpose(ps[0:rows, (i % 2) * 2 + k // 4, (k % 4) * P:(k % 4 + 1) * P],
                                            core.xT[:, k, i * P:i * P + rows], core.ident)
                    last.then_inc(turned, 1)

            def mover(eng, copy, half, moved):
                for i in range(NT):
                    rows = P if i < 4 else SAMP
                    eng.wait_ge(turned, i + 1)
                    eng.wait_ge(y_out[i % 2], since(16 * (i // 2)))
                    copy(yt[0:rows, i % 2, half * 512:half * 512 + 512], ps[0:rows, (i % 2) * 2 + half, :]
                        ).then_inc(moved, 1)

            @block.scalar
            def _(act):
                mover(act, act.copy, 0, moved_a)

            @block.vector
            def _(dve):
                mover(dve, dve.tensor_copy, 1, moved_d)

            @block.sync
            def _(sp):
                for i in range(NT):
                    rows = P if i < 4 else SAMP
                    sp.wait_ge(moved_a, i + 1)
                    sp.wait_ge(moved_d, i + 1)
                    dst = io["out_y_p"][0, i * P:(i + 1) * P, :] if i < 4 else \
                        io["out_y_s"].rearrange("b t d -> (b t) d")
                    sp.dma_start(dst, yt[0:rows, i % 2, :]).then_inc(y_out[i % 2], 16)
                sp.wait_ge(y_out[0], 48)
                sp.wait_ge(y_out[1], 32)
                sp.wait_ge(core.rows_out, 16 * (2 + DB))
                sp.wait_ge(core.prompt_rows_out, 16)
                sp.wait_ge(core.window_out, 16 * DB)


def write_rows(core, at, sp):
    io = core.io
    sp.dma_start(io["out_nsa_p"][0, 0].rearrange("(i p) s g d -> p i (s g d)", p=P),
                 at.qkv[:, 0:4, 1024:2048]).then_inc(core.prompt_rows_out, 16)
    sp.dma_start(io["out_nsa_s"][0].rearrange("b t s g d -> (b t) (s g d)"),
                 at.qkv[0:SAMP, 4, 1024:2048]).then_inc(core.rows_out, 16)
    sp.dma_start(io["out_win_p"][0, 0].rearrange("(i p) s g d -> p i (s g d)", p=P),
                 at.qkv[:, 0:4, KW:QKV]).then_inc(core.rows_out, 16)
    for b in range(DB):
        sp.dma_start(io["out_win_s"][0, b, PAST - DS:PAST].rearrange("t s g d -> t (s g d)"),
                     at.qkv[b * DS:b * DS + DS, 4, KW:QKV]).then_inc(core.rows_out, 16)


def program(nc, io):
    with ExitStack() as ctx:
        core = Core(nc, io, ctx)
        weight_streams(core)
        with ExitStack() as nsa:
            cmp = Compressed(core, nsa)
            with ExitStack() as own:
                taps = Taps(core, own, "sample")
                pages = core.sb("chunk_pages", [1, DB * NPAGE], I32, own)
                pages_in = core.lasting("chunk_pages_in")
                landed = [core.lasting("chunks_in0"), core.lasting("chunks_in1")]
                core.window_out = core.lasting("window_out")

                def load_first(sp):
                    sp.dma_start(pages[:, :], io["page_table"].rearrange("(o b) n -> o (b n)", o=1)).then_inc(
                        pages_in, 16)
                    taps.load(sp)
                setup(core, load_first)
                chunks = core.sb("chunks", [P, 2, 16, 512], F32, own)

                def load(sp, half):
                    sp.wait_ge(pages_in, 16)
                    for b in range(4 * half, 4 * half + 4):
                        for n in range(NPAGE):
                            page = sp.value_load(pages[0:1, b * NPAGE + n:b * NPAGE + n + 1], min_val=0,
                                                 max_val=io["cache_nsa_kv"].shape[1] - 1)
                            p0 = (b % 4) * 32 + n * 8
                            sp.dma_start(chunks[p0:p0 + 8, b // 4, :, :],
                                         io["cache_nsa_kv"][0][bass.ds(page, 1)].rearrange(
                                             "o (c j) s g d -> (o c) j (s g d)", j=16)[:, :, 0:512]).then_inc(
                                landed[b // 4], 16)

                def load_rest(sp):
                    load(sp, 1)
                    for b in range(DB):
                        sp.dma_start(io["out_win_s"][0, b, 0:PAST - DS].rearrange("t s g d -> t (s g d)"),
                                     io["state_win_kv"][0, b, DS:PAST].rearrange("t s g d -> t (s g d)")).then_inc(
                            core.window_out, 16)
                with ExitStack() as norm_ctx:
                    core.norm_buffers(norm_ctx)
                    norms(core, None, 0, lambda sp: load(sp, 0))
                compress(core, cmp, taps, [
                    (P, lambda kv, h=h: (chunks[:, h, :, kv * KVW:(kv + 1) * KVW], 0), landed[h], 256, 4 * h, 4)
                    for h in range(2)], load_rest)
            at = Attention(core, nsa)
            token_major(core, 0, at.qkv, roped=(0, 1, 2, 3, 4, 6, 8))
            core.rows_out, core.prompt_rows_out = core.lasting("cache_rows_out"), core.lasting("prompt_rows_out")
            chunks_in = core.lasting("prompt_chunks_in")
            with ExitStack() as own:
                kk = core.sb("keys_split", [P, 2, KVH, SEQ], F16, own)
                with ExitStack() as first:
                    chunks = core.sb("prompt_chunks", [64, 16, KVW], F32, first)

                    taps = Taps(core, first, "prompt")

                    def write_and_read(sp):
                        taps.load(sp)
                        write_rows(core, at, sp)
                        sp.wait_ge(core.prompt_rows_out, 16)
                        for kv in range(2):
                            sp.dma_start(chunks[kv * 32:kv * 32 + 32, :, :], io["out_nsa_p"][0, 0].rearrange(
                                "(c j) s g d -> c j (s g d)", j=16)[:, :, kv * KVW:(kv + 1) * KVW]
                                         ).then_inc(chunks_in, 16)
                    attention_inputs(core, at, kk, write_and_read)
                    compress(core, cmp, taps, [(32, lambda kv: (chunks[kv * 32:kv * 32 + 32, :, :], kv * 32), chunks_in, 32,
                                          DB, 1)])
                prompt_attention(core, at, cmp, kk)
            sample_attention(core, at, cmp)
        with ExitStack() as norm_ctx:
            core.norm_buffers(norm_ctx)
            features_to_y(core, 1, (core.hhi, core.hlo), 1)
            norms(core, 1, 2)
            ffn(core, 0, 2)
            norms(core, 3, 4)
        with ExitStack() as own:
            gla = Gla(core, own)
            gla_heads(core, gla, 4)
            token_major(core, 5, gla.vr)
            o = gla.vr[:, :, 0:GH * DV]
            gla_core(core, gla, o)
            gla_finish(core, gla, o)
        with ExitStack() as norm_ctx:
            core.norm_buffers(norm_ctx)
            features_to_y(core, 6, (core.hhi, core.hlo), 1)
            norms(core, 5, 6)
            ffn(core, 1, 7)
            norms(core, 7, None)
            write_y(core)


_INS = ["x_prompt", "x_sample", "cache_nsa_kv", "state_win_kv", "state_gla", "state_ffn_conv", "page_table",
        "norm_gain", "nsa_w_in", "nsa_cmp_pe", "nsa_cmp_w", "nsa_w_o", "gla_w_in", "gla_w_gate_up", "gla_b_gate",
        "gla_norm_gain", "gla_w_o", "ffn_w_up", "ffn_conv_w", "ffn_conv_b", "ffn_w_down"]
_OUTS = [("out_y_p", (1, SEQ, D)), ("out_y_s", (DB, DS, D)), ("out_nsa_p", (1, 1, SEQ, 4, KVH, DH)),
         ("out_nsa_s", (1, DB, DS, 4, KVH, DH)), ("out_win_p", (1, 1, SEQ, 2, KVH, DH)),
         ("out_win_s", (1, DB, PAST, 2, KVH, DH)), ("out_gla_p", (1, 1, GH, DK, DV)),
         ("out_gla_s", (1, DB, GH, DK, DV)), ("out_ffn_p", (2, 1, 2, F)), ("out_ffn_s", (2, DB, 2, F))]


def kernel(**inputs):
    import numpy as _np
    import concourse.bacc as _bacc
    from concourse import mybir as _mybir
    from concourse.bass_utils import run_bass_kernel_spmd as _run

    nc = _bacc.Bacc("TRN2", target_bir_lowering=False, num_devices=1)
    arrays, io = {}, {}
    for name in _INS + ["consts"]:
        a = constants() if name == "consts" else _np.ascontiguousarray(inputs[name])
        arrays[f"in_{name}"] = a
        io[name] = nc.dram_tensor(f"in_{name}", a.shape, _mybir.dt.from_np(a.dtype), kind="ExternalInput").ap()
    for name, shape in _OUTS:
        io[name] = nc.dram_tensor(name, shape, _mybir.dt.from_np(_np.dtype("float32")), kind="ExternalOutput").ap()
    program(nc, io)
    r = _run(nc, [arrays], core_ids=[0])
    return tuple(r.results[0][name] for name, _ in _OUTS)
```
